# Optimizing a Trainium2 kernel written in Bass

```python
import jax
import jax.numpy as jnp
from jax import lax
import numpy as np

D_MODEL = 1024
BATCH = 1
SEQ = 256
DEPTH = 1

MEM_LEN = 256
MIX_W = D_MODEL
LRU_W = MIX_W // 2
RWKV_W = MIX_W - LRU_W
LRU_BLOCKS = 8
LRU_BLOCK = LRU_W // LRU_BLOCKS
CONV_W = 4
LRU_C = 8.0
RWKV_HEAD = 64
RWKV_HEADS = RWKV_W // RWKV_HEAD
DECAY_LORA = 64
AAA_LORA = 64
GATE_LORA = 128
RWKV_IN = 3 * RWKV_W + DECAY_LORA + AAA_LORA + GATE_LORA
IN_W = 2 * LRU_W + RWKV_IN
XA_HEADS = 4
XA_HEAD = D_MODEL // XA_HEADS
N_EXPERTS = 32
TOP_K = 4
D_FF = D_MODEL
SWIGLU_LIMIT = 7.0
SWIGLU_ALPHA = 1.702
MOE_BLOCK = 256
EPS = 1e-6
GN_EPS = 64e-5

kernel_name = 'hymba_rglru_rwkv7_xattn_moe'

def rmsnorm(x, g):
    xf = x.astype(jnp.float32)
    y = xf * lax.rsqrt(jnp.mean(xf * xf, axis=-1, keepdims=True) + EPS)
    return (y * g.astype(jnp.float32)).astype(x.dtype)

def token_shift(u):
    return jnp.pad(u, ((0, 0), (1, 0), (0, 0)))[:, :-1]

def causal_dwconv(x, w, b):
    c = x.shape[-1]
    y = lax.conv_general_dilated(x, w[:, None, :].astype(x.dtype), window_strides=(1,),
                                 padding=[(CONV_W - 1, 0)],
                                 dimension_numbers=('NWC', 'WIO', 'NWC'),
                                 feature_group_count=c)
    return y + b

def rg_lru(xc, wx, bx, wa, ba, lam):
    bsz, s, _ = xc.shape
    xb = xc.reshape(bsz, s, LRU_BLOCKS, LRU_BLOCK)
    gx = jax.nn.sigmoid(jnp.einsum('bsni,nij->bsnj', xb, wx).reshape(bsz, s, LRU_W) + bx)
    ga = jax.nn.sigmoid(jnp.einsum('bsni,nij->bsnj', xb, wa).reshape(bsz, s, LRU_W) + ba)
    log_a = -LRU_C * ga.astype(jnp.float32) * jax.nn.softplus(-lam.astype(jnp.float32))
    a = jnp.exp(log_a)
    bt = jnp.sqrt(-jnp.expm1(2.0 * log_a)) * gx.astype(jnp.float32) * xc.astype(jnp.float32)

    def combine(left, right):
        a1, b1 = left
        a2, b2 = right
        return a1 * a2, a2 * b1 + b2

    _, h = lax.associative_scan(combine, (a, bt), axis=1)
    return h.astype(xc.dtype)

def rwkv7_mix(u, mu, w0, w_up, a0, a_up, g_up, k_k, k_a, r_k, lnx_g, lnx_b):
    bsz, s, _ = u.shape
    u = u + (token_shift(u) - u) * mu
    c1 = RWKV_W
    c2 = 2 * RWKV_W
    c3 = 3 * RWKV_W
    c4 = c3 + DECAY_LORA
    c5 = c4 + AAA_LORA
    r, k, v, dw, da, dg = jnp.split(u, [c1, c2, c3, c4, c5], axis=-1)
    w = -jax.nn.softplus(-(w0 + jnp.tanh(dw) @ w_up)) - 0.5
    decay = jnp.exp(-jnp.exp(w.astype(jnp.float32)))
    a = jax.nn.sigmoid(a0 + da @ a_up)
    g = jax.nn.sigmoid(dg) @ g_up

    def hs(t):
        return t.reshape(bsz, s, RWKV_HEADS, RWKV_HEAD).astype(jnp.float32)

    kk = hs(k * k_k)
    kk = kk / jnp.maximum(jnp.sqrt(jnp.sum(kk * kk, axis=-1, keepdims=True)), 1e-12)
    k = k * (1.0 + (a - 1.0) * k_a)
    rh, kh, vh, ah, wh = hs(r), hs(k), hs(v), hs(a), hs(decay)

    def step(state, inp):
        r_t, w_t, k_t, v_t, kk_t, a_t = inp
        sa = jnp.einsum('bhvk,bhk->bhv', state, -kk_t)
        state = (state * w_t[:, :, None, :]
                 + sa[..., None] * (kk_t * a_t)[:, :, None, :]
                 + v_t[..., None] * k_t[:, :, None, :])
        y_t = jnp.einsum('bhvk,bhk->bhv', state, r_t)
        return state, y_t

    def tm(t):
        return jnp.swapaxes(t, 0, 1)

    s0 = jnp.zeros((bsz, RWKV_HEADS, RWKV_HEAD, RWKV_HEAD), jnp.float32)
    _, y = lax.scan(step, s0, (tm(rh), tm(wh), tm(kh), tm(vh), tm(kk), tm(ah)))
    y = tm(y)
    mean = jnp.mean(y, axis=-1, keepdims=True)
    var = jnp.mean(jnp.square(y - mean), axis=-1, keepdims=True)
    y = ((y - mean) * lax.rsqrt(var + GN_EPS) * lnx_g.reshape(RWKV_HEADS, RWKV_HEAD).astype(jnp.float32)
         + lnx_b.reshape(RWKV_HEADS, RWKV_HEAD).astype(jnp.float32))
    y = y + jnp.sum(rh * kh * r_k.astype(jnp.float32), axis=-1, keepdims=True) * vh
    return (y.reshape(bsz, s, RWKV_W) * g.astype(jnp.float32)).astype(u.dtype)

def cross_attn(h, mem_h, wq, wk, wv, wo):
    bsz, s, d = h.shape
    m = mem_h.shape[1]
    q = (h @ wq).reshape(bsz, s, XA_HEADS, XA_HEAD)
    k = (mem_h @ wk).reshape(bsz, m, XA_HEADS, XA_HEAD)
    v = (mem_h @ wv).reshape(bsz, m, XA_HEADS, XA_HEAD)
    sc = jnp.einsum('bshd,bmhd->bhsm', q, k).astype(jnp.float32) * (XA_HEAD ** -0.5)
    p = jax.nn.softmax(sc, axis=-1).astype(h.dtype)
    o = jnp.einsum('bhsm,bmhd->bshd', p, v).reshape(bsz, s, d)
    return o @ wo

def clamped_swiglu(gu):
    gate, up = jnp.split(gu, 2, axis=-1)
    gate = jnp.minimum(gate, SWIGLU_LIMIT)
    up = jnp.clip(up, -SWIGLU_LIMIT, SWIGLU_LIMIT)
    return (up + 1.0) * (gate * jax.nn.sigmoid(SWIGLU_ALPHA * gate))

def moe(h, w_router, b_router, w_gu, b_gu, w_dn, b_dn):
    bsz, s, d = h.shape
    t = bsz * s
    xt = h.reshape(t, d)
    logits = (xt @ w_router + b_router).astype(jnp.float32)
    top_val, top_idx = lax.top_k(logits, TOP_K)
    gates = jax.nn.softmax(top_val, axis=-1)
    n_assign = t * TOP_K
    e_flat = top_idx.reshape(n_assign)
    tok_flat = jnp.repeat(jnp.arange(t, dtype=jnp.int32), TOP_K)
    g_flat = gates.reshape(n_assign)
    order = jnp.argsort(e_flat)
    e_s = e_flat[order]
    tok_s = tok_flat[order]
    g_s = g_flat[order]
    counts = jnp.bincount(e_flat, length=N_EXPERTS)
    starts = jnp.cumsum(counts) - counts
    padded = (counts + MOE_BLOCK - 1) // MOE_BLOCK * MOE_BLOCK
    pends = jnp.cumsum(padded)
    pstarts = pends - padded
    dest = pstarts[e_s] + (jnp.arange(n_assign) - starts[e_s])
    n_blocks = (n_assign + N_EXPERTS * (MOE_BLOCK - 1) + MOE_BLOCK - 1) // MOE_BLOCK
    rows = n_blocks * MOE_BLOCK
    buf_tok = jnp.full((rows,), t, jnp.int32).at[dest].set(tok_s)
    buf_g = jnp.zeros((rows,), jnp.float32).at[dest].set(g_s)
    block_e = jnp.minimum(jnp.searchsorted(pends, jnp.arange(n_blocks) * MOE_BLOCK, side='right'),
                          N_EXPERTS - 1).astype(jnp.int32)
    x_pad = jnp.concatenate([xt, jnp.zeros((1, d), xt.dtype)], axis=0)

    def block_fn(args):
        tok_b, g_b, e = args
        xb = x_pad[tok_b]
        act = clamped_swiglu(xb @ w_gu[e] + b_gu[e])
        y = act @ w_dn[e] + b_dn[e]
        return y * g_b[:, None].astype(y.dtype)

    ys = lax.map(block_fn, (buf_tok.reshape(n_blocks, MOE_BLOCK),
                            buf_g.reshape(n_blocks, MOE_BLOCK), block_e))
    out = jnp.zeros((t + 1, d), ys.dtype).at[buf_tok].add(ys.reshape(rows, d))[:t]
    return out.reshape(bsz, s, d).astype(h.dtype)

def setup_inputs(seed: int = 0) -> dict:
    key = jax.random.key(seed)
    ks = iter(jax.random.split(key, 48))
    f32 = jnp.float32

    def nrm(shape, scale):
        return jax.random.normal(next(ks), shape, f32) * scale

    def gain(shape):
        return 1.0 + 0.05 * jax.random.normal(next(ks), shape, f32)

    L = DEPTH
    u_lam = jax.random.uniform(next(ks), (L, LRU_W), f32, 0.9, 0.999)
    a_base = u_lam ** (1.0 / LRU_C)
    lru_lambda = jnp.log(a_base) - jnp.log1p(-a_base)
    return {
        'x': nrm((BATCH, SEQ, D_MODEL), 1.0),
        'mem': nrm((BATCH, MEM_LEN, D_MODEL), 1.0),
        'norm_mix_g': gain((L, D_MODEL)),
        'w_in': nrm((L, D_MODEL, IN_W), D_MODEL ** -0.5),
        'conv_w': nrm((L, CONV_W, LRU_W), CONV_W ** -0.5),
        'conv_b': nrm((L, LRU_W), 0.02),
        'lru_wx': nrm((L, LRU_BLOCKS, LRU_BLOCK, LRU_BLOCK), LRU_BLOCK ** -0.5),
        'lru_bx': nrm((L, LRU_W), 0.02),
        'lru_wa': nrm((L, LRU_BLOCKS, LRU_BLOCK, LRU_BLOCK), LRU_BLOCK ** -0.5),
        'lru_ba': nrm((L, LRU_W), 0.02),
        'lru_lambda': lru_lambda,
        'rwkv_mu': jax.random.uniform(next(ks), (L, RWKV_IN), f32, 0.0, 1.0),
        'rwkv_w0': jax.random.uniform(next(ks), (L, RWKV_W), f32, -4.0, 1.0),
        'rwkv_w_up': nrm((L, DECAY_LORA, RWKV_W), 0.1 * DECAY_LORA ** -0.5),
        'rwkv_a0': nrm((L, RWKV_W), 0.5),
        'rwkv_a_up': nrm((L, AAA_LORA, RWKV_W), 0.1 * AAA_LORA ** -0.5),
        'rwkv_g_up': nrm((L, GATE_LORA, RWKV_W), GATE_LORA ** -0.5),
        'rwkv_k_k': 0.85 + 0.05 * jax.random.normal(next(ks), (L, RWKV_W), f32),
        'rwkv_k_a': gain((L, RWKV_W)),
        'rwkv_r_k': nrm((L, RWKV_HEADS, RWKV_HEAD), 0.1),
        'rwkv_lnx_g': gain((L, RWKV_W)),
        'rwkv_lnx_b': nrm((L, RWKV_W), 0.02),
        'w_out': nrm((L, MIX_W, D_MODEL), MIX_W ** -0.5),
        'norm_xa_g': gain((L, D_MODEL)),
        'norm_mem_g': gain((L, D_MODEL)),
        'xa_wq': nrm((L, D_MODEL, D_MODEL), D_MODEL ** -0.5),
        'xa_wk': nrm((L, D_MODEL, D_MODEL), D_MODEL ** -0.5),
        'xa_wv': nrm((L, D_MODEL, D_MODEL), D_MODEL ** -0.5),
        'xa_wo': nrm((L, D_MODEL, D_MODEL), D_MODEL ** -0.5),
        'norm_ffn_g': gain((L, D_MODEL)),
        'w_router': nrm((L, D_MODEL, N_EXPERTS), D_MODEL ** -0.5),
        'b_router': nrm((L, N_EXPERTS), 0.01),
        'w_gu': nrm((L, N_EXPERTS, D_MODEL, 2 * D_FF), D_MODEL ** -0.5),
        'b_gu': nrm((L, N_EXPERTS, 2 * D_FF), 0.02),
        'w_dn': nrm((L, N_EXPERTS, D_FF, D_MODEL), D_FF ** -0.5),
        'b_dn': nrm((L, N_EXPERTS, D_MODEL), 0.02),
        'final_norm_g': gain((D_MODEL,)),
    }

def reference(x, mem, norm_mix_g, w_in, conv_w, conv_b, lru_wx, lru_bx, lru_wa, lru_ba,
              lru_lambda, rwkv_mu, rwkv_w0, rwkv_w_up, rwkv_a0, rwkv_a_up, rwkv_g_up,
              rwkv_k_k, rwkv_k_a, rwkv_r_k, rwkv_lnx_g, rwkv_lnx_b, w_out, norm_xa_g,
              norm_mem_g, xa_wq, xa_wk, xa_wv, xa_wo, norm_ffn_g, w_router, b_router,
              w_gu, b_gu, w_dn, b_dn, final_norm_g):
    for l in range(DEPTH):
        h = rmsnorm(x, norm_mix_g[l])
        u = h @ w_in[l]
        x_lru, g_lru, u_rwkv = jnp.split(u, [LRU_W, 2 * LRU_W], axis=-1)
        xc = causal_dwconv(x_lru, conv_w[l], conv_b[l])
        y_lru = rg_lru(xc, lru_wx[l], lru_bx[l], lru_wa[l], lru_ba[l], lru_lambda[l]) * jax.nn.gelu(g_lru)
        y_rwkv = rwkv7_mix(u_rwkv, rwkv_mu[l], rwkv_w0[l], rwkv_w_up[l], rwkv_a0[l], rwkv_a_up[l],
                           rwkv_g_up[l], rwkv_k_k[l], rwkv_k_a[l], rwkv_r_k[l],
                           rwkv_lnx_g[l], rwkv_lnx_b[l])
        x = x + jnp.concatenate([y_lru, y_rwkv], axis=-1) @ w_out[l]
        x = x + cross_attn(rmsnorm(x, norm_xa_g[l]), rmsnorm(mem, norm_mem_g[l]),
                           xa_wq[l], xa_wk[l], xa_wv[l], xa_wo[l])
        x = x + moe(rmsnorm(x, norm_ffn_g[l]), w_router[l], b_router[l],
                    w_gu[l], b_gu[l], w_dn[l], b_dn[l])
    return rmsnorm(x, final_norm_g)


_drawn_inputs = setup_inputs


def setup_inputs(seed=0):
    import zlib

    import numpy as np

    out = dict(_drawn_inputs(seed))
    spreads = {}
    factors = {'lru_bx': 5.231, 'lru_ba': 5.093, 'rwkv_w_up': 3.354, 'b_gu': 5.525, 'b_dn': 6.411}
    for name, (base, spread) in spreads.items():
        noise = np.random.default_rng([zlib.crc32(name.encode()), seed]).standard_normal(out[name].shape)
        drawn = base * np.exp(spread * noise) if base else spread * noise
        out[name] = jnp.asarray(drawn.astype(out[name].dtype))
    for name, factor in factors.items():
        out[name] = (out[name] * factor).astype(out[name].dtype)
    return out
```

```python
from contextlib import ExitStack

import numpy as np

import concourse.bass as bass
from concourse import mybir

ALU = mybir.AluOpType
ACT = mybir.ActivationFunctionType
F32 = mybir.dt.float32
I32 = mybir.dt.int32
AX_X = mybir.AxisListType.X

P = 128
T, D = 256, 1024
TT = T // P
KT = D // P
LRU_W = RW = 512
CT = RW // P
IN_W = 2816
HEAD = 64
NH = RW // HEAD
CH = 64
NCH = T // CH
XH, XD = 4, 256
NE = 32
SLOTS = 64
ROUNDS = T // SLOTS
EPS, GN_EPS = 1e-6, 64e-5
ROOT_D, ROOT_HEAD = float(np.sqrt(D)), float(np.sqrt(HEAD))
DECAY = float(np.exp(-0.5))
LIMIT, ALPHA = 7.0, 1.702
UNIT = 1024

PARAM_ROWS = [("norm_mix_g", KT), ("norm_mem_g", KT), ("norm_xa_g", KT), ("norm_ffn_g", KT),
              ("conv_w", 4 * CT), ("conv_b", CT), ("lru_bx", CT), ("lru_ba", CT), ("lru_lambda", CT),
              ("rwkv_mu", 14), ("rwkv_w0", CT), ("rwkv_a0", CT), ("rwkv_k_k", CT), ("rwkv_k_a", CT),
              ("rwkv_r_k", CT)]
COL, NPAR = {}, 0
for _name, _rows in PARAM_ROWS:
    COL[_name] = NPAR
    NPAR += _rows


SHARED = {}
for _sem, _steps in (
    ("early_pe", [("par_ps", 1), ("t_x", 4), ("t_mem", 4), ("u_xl", 4), ("u_gl", 4), ("u_r", 4), ("u_k", 4),
                  ("lru_gates", 4), ("u_lora", 2), ("u_v", 4), ("z_a", 1), ("g_ps", 2)]),
    ("early_dve", [("xl_pads", 1), ("xn", 2), ("par", 1), ("omu", 1), ("lam_abs", 1), ("lam_w", 1),
                   ("memn", 2), ("hT_v", 4), ("mT_v", 4), ("lam_rate", 2), ("conv", 16)]),
    ("early_act", [("ss_x", 2), ("ss_mem", 2), ("lam_e", 1), ("lam_ln", 1), ("hT_a", 4), ("mT_a", 4), ("xl", 4),
                   ("gelu", 4), ("sa_r", 4), ("sa_k", 4)]),
    ("router_pe", [("rl_ps", 2), ("rank_ps", 3), ("gt_ps", 2)]),
    ("router_dve", [("gate", 2), ("key", 1), ("steps_v", 1), ("gate_t", 1)]),
    ("rwkv_pe", [("kk_ss", 2), ("tok_ps", 8), ("bonus_ps", 1), ("st_ps", 8), ("n_ps", 4), ("G_ps", 1), ("N2_ps", 1),
                 ("N2t_ps", 1), ("P2_ps", 1), ("N4_ps", 1), ("N4t_ps", 1), ("P4_ps", 1), ("N8_ps", 1), ("T16_ps", 1),
                 ("E_ps", 1), ("Et_ps", 1), ("YW_ps", 1), ("YG_ps", 1), ("E2t_ps", 1), ("Y2w_ps", 1), ("Y2g_ps", 1),
                 ("XW_ps", 1), ("XU_ps", 1), ("NS_ps", 1), ("M_ps", 1), ("Yuv_ps", 1), ("Q_ps", 1), ("S_ps", 2),
                 ("Ys_ps", 2), ("yT_ps", 2)]),
    ("rwkv_dve", [("al_c", 1), ("bt_c", 1), ("kt_c", 1), ("r_til", 1), ("bh_c", 1), ("kh_c", 1), ("rkk", 4),
                  ("tok_v", 4), ("bonus", 1), ("st", 8)]),
    ("solve_dve", [("P1", 4), ("N2t", 2), ("P2", 2), ("N4t", 2), ("P4", 2), ("T16", 2), ("Et", 2), ("Y1g", 2),
                   ("DI", 2), ("Y2", 4), ("XW", 2), ("XU", 2), ("NS", 2), ("Mt", 2), ("Q", 3), ("St_v", 2), ("Y", 4)]),
    ("solve_act", [("G", 2), ("N2", 2), ("N4", 2), ("N8", 2), ("E", 2), ("Y1", 2), ("E2t", 2), ("Yuv", 4), ("St_a", 2)]),
):
    _at = 0
    for _name, _n in _steps:
        SHARED[_name] = (_sem, _at)
        _at += _n


def build(nc, a, out):
    with ExitStack() as ctx:
        def sb(name, shape, dt=F32):
            return ctx.enter_context(nc.sbuf_tensor(name, shape, dt))

        sems = {}

        def S(name):
            name = SHARED.get(name, (name, 0))[0]
            if name not in sems:
                sems[name] = ctx.enter_context(nc.semaphore(name))
            return sems[name]

        def at(name, n):
            return S(name), SHARED[name][1] + n if name in SHARED else n

        A = sb("A", [P, 24576])
        B = sb("B", [P, 8192])
        X = sb("X", [P, TT, D])
        HT = sb("HT", [P, KT, T])
        MT = sb("MT", [P, KT, T])
        VX = sb("VX", [P, 2048])
        YT = sb("YT", [P, KT, T])
        R = sb("R", [P, 2, UNIT])
        par_rows = sb("par_rows", [P, P])
        par = sb("par", [P, P])
        omu = sb("omu", [P, 14])
        ident = sb("ident", [P, P])
        ones = sb("ones", [P, P])
        neg_half = sb("neg_half", [P, TT * NH])
        before = sb("before", [P, P])
        head_ones = sb("head_ones", [P, P])
        M = sb("M", [P, 2560])
        m8 = [M[:, i * 512:(i + 1) * 512].rearrange("p (e k) -> p e k", e=8) for i in range(5)]
        eye8, mask_n, mask_o, mask_nt = m8[:4]
        mask_ar = M[:, 2048:2560].rearrange("p (c w k) -> p c w k", c=4, w=2)
        restart = sb("restart", [P, T])
        slot_no = sb("slot_no", [P, 2, SLOTS])
        w_bd = sb("w_bd", [P, 2 * CT * P])
        wx_bd, wa_bd = (w_bd[:, i * 512:(i + 1) * 512].rearrange("p (c j) -> p c j", c=CT) for i in range(2))
        wa_up = sb("wa_up", [P, RW])
        g_up = sb("g_up", [P, RW])
        lnx = sb("lnx", [P, 2, RW])
        w_rt = sb("w_rt", [P, KT, NE])
        b_rt = sb("b_rt", [P, NE])
        st = sb("st", [P, 32])
        lam = sb("lam", [P, 8, CT])
        dc = sb("dc", [P, CT, NCH])
        gst = sb("gst", [P, 8, TT, NH])
        ast = sb("ast", [P, 4, 2 * XH])
        rt = M[:, 1024:1664].rearrange("p (w i e) -> p w i e", w=10, i=TT)
        top = sb("top", [P, TT, 8])
        key, gate = (M[:, 1664 + i * 64:1728 + i * 64].rearrange("p (i e) -> p i e", i=TT) for i in range(2))
        gate_t = M[0:NE, 1792:2048]
        cnt = sb("cnt", [P, 8])
        steps_i = sb("steps_i", [P, 1], I32)
        PS = [ctx.enter_context(nc.psum_tensor(f"PS{i}", [P, 512], F32)) for i in range(8)]

        def U(i, n=1):
            return A[:, i * UNIT:(i + n) * UNIT]

        def chan(ap):
            return ap.rearrange("p (c t) -> p c t", c=CT)

        def heads(ap):
            return ap.rearrange("p (j h k) -> p j h k", j=2, h=NH)

        def col(name, c=0):
            return par[:, COL[name] + c:COL[name] + c + 1]

        w_in_q = [A[:, q * 4096:(q + 1) * 4096].rearrange("p (c n) -> p c n", c=KT) for q in range(5)]
        w_lora = A[:, 5 * 4096:5 * 4096 + 2048].rearrange("p (c n) -> p c n", c=KT)
        W2 = A[:, 16384:24576].rearrange("p (c n) -> p c n", c=KT)
        W1 = A[:, 8192:16384].rearrange("p (c n) -> p c n", c=KT)
        WB = B[:, :].rearrange("p (c n) -> p c n", c=KT)
        WV = {"xl": (w_in_q[0], 0), "gl": (w_in_q[1], 512), "r": (w_in_q[2], 1024),
              "k": (w_in_q[3], 1536), "v": (w_in_q[4], 2048), "lora": (w_lora, 2560)}
        xl_pad = VX[:, 0:CT * 260].rearrange("p (c t) -> p c t", c=CT)
        mem = R
        lora = R[:, 0, 0:512].rearrange("p (c t) -> p c t", c=2)
        V = VX[:, :].rearrange("p (m d) -> p m d", m=2)

        xc, gx, ga, th = chan(U(0)), chan(U(1)), chan(U(2)), chan(U(3))
        dec = chan(U(4))
        r_c, k_c, v_c = chan(U(5)), chan(U(6)), chan(U(7))
        sig, a_c, Z = chan(U(8)), chan(U(9)), chan(U(10))
        Dt, inv_d, d_prev, kk, zp = chan(U(11)), chan(U(12)), chan(U(13)), chan(U(14)), chan(U(15))
        sq, beta = chan(U(1)), chan(U(2))
        AR = U(3, 2).rearrange("p (w c t) -> p w c t", w=2, c=CT)
        bt_c, kt_c = chan(U(8)), chan(U(15))
        bh_c, kh_c = chan(U(0)), chan(U(1))
        rkk = chan(U(2))
        al_t, v_t, bh_t, kh_t = heads(U(9)), heads(U(10)), heads(U(13)), heads(U(14))
        STb = U(5, 2).rearrange("p (j h w k) -> p j h w k", j=2, h=NH, w=2)
        STk = U(11, 2).rearrange("p (j h w k) -> p j h w k", j=2, h=NH, w=2)
        Nm, Om, Ntm = heads(U(7)), heads(U(2)), heads(R[:, 0, :])
        P1, N2, N2t, P2 = heads(U(0)), heads(U(1)), heads(U(8)), heads(U(15))
        N4, N4t, N8, P4, T16 = heads(U(7)), heads(R[:, 0, :]), heads(U(1)), heads(U(0)), heads(U(15))
        G = heads(R[:, 1, :])
        E, Et, E2t = heads(U(7)), heads(U(8)), heads(U(2))
        Y1 = [heads(U(0)), heads(U(1))]
        Y2 = [heads(U(15)), heads(R[:, 0, :])]
        XW, XU = heads(U(7)), heads(U(2))
        DI = U(9)[:, 0:512].rearrange("p (n c k) -> p n c k", n=2, c=CT)
        Mt = U(9)[:, 512:1024].rearrange("p (n c k) -> p n c k", n=2, c=CT)
        NS = U(0)[:, 0:768].rearrange("p (n c k) -> p n c k", n=3, c=CT)
        Q = U(1).rearrange("p (n c k) -> p n c k", n=NCH, c=CT)
        St = U(15)[:, 0:512].rearrange("p (n c k) -> p n c k", n=2, c=CT)
        Yuv = heads(U(8))
        Y, Yt1 = heads(R[:, 0, :]), heads(R[:, 1, :])
        g_t = heads(w_bd[:, :])
        A_prob = R[:, :, :].rearrange("p a (b t) -> p (a b) t", b=4)
        A_probt = M[:, 0:1024].rearrange("p (h m t) -> p h m t", h=2, m=2)
        xn = B[:, 0:2048].rearrange("p (i d) -> p i d", i=TT)
        xm = R

        def prob(u):
            return A_prob[:, u, :]

        def prob_t(h):
            return A_probt[:, h % 2]

        gu = [A[:, q * 4096:(q + 1) * 4096].rearrange("p (c w g n) -> p c w g n", c=2, w=2, g=2) for q in range(4)]
        dn = [A[:, (4 + q) * 4096:(5 + q) * 4096].rearrange("p (c g n) -> p c g n", c=4, g=2) for q in range(2)]
        bgu = B[0:1, 0:2048].rearrange("p (w g n) -> p w g n", w=2, g=2)
        bdn = B[0:NE, 2048:3072]
        fin_g = B[:, 3072:4096]
        x3n = HT[:, :, :].rearrange("p c t -> p (c t)").rearrange("p (i d) -> p i d", i=TT)
        x3t = MT
        yt_f = YT[:, :, :].rearrange("p c t -> p (c t)")
        sel = yt_f[:, 0:256].rearrange("p (i w s) -> p i w s", i=TT, w=2)
        self_ = yt_f[:, 256:384].rearrange("p (i s) -> p i s", i=TT)
        sel_t = yt_f[:, 512:768].rearrange("p (i t) -> p i t", i=TT)
        xg = yt_f[:, 1024:1536].rearrange("p (c s) -> p c s", c=KT)
        act_t = yt_f[:, 1536:2048].rearrange("p (f m) -> p f m", f=4)
        vx_f = VX[:, :]
        m_g, m_s, m_u, m_a = (vx_f[:, i * 512:(i + 1) * 512] for i in range(4))
        y_e = R[:, 0, 0:512]
        fin = R[:, :, :]

        dram = {k: (v[0] if k not in ("x", "mem", "final_norm_g") else v) for k, v in a.items()}
        krows = lambda w: w.rearrange("(c p) n -> p c n", p=P)

        block = ctx.enter_context(nc.Block())

        @block.sync
        def _(sp):
            sp.dma_start(X[:], dram["x"][0].rearrange("(i p) d -> p i d", p=P)).then_inc(S("ld_x"), 16)

            def load_in(name):
                w, at = WV[name]
                n = w.shape[2]
                sp.dma_start(w, krows(dram["w_in"][:, at:at + n])).then_inc(S("ld_" + name), 16)

            load_in("xl")
            sp.dma_start(mem[:], dram["mem"][0].rearrange("(i p) d -> p i d", p=P)).then_inc(S("ld_mem"), 16)
            for name in ("gl", "r", "k", "lora", "v"):
                load_in(name)
            sp.wait_ge(*at("t_x", 4))
            sp.dma_start(WB, krows(dram["xa_wk"])).then_inc(S("ld_wk"), 16)
            sp.wait_ge(*at("u_v", CT))
            sp.dma_start(W2, krows(dram["w_out"])).then_inc(S("ld_wo1"), 16)
            sp.wait_ge(*at("pe_k", KT))
            sp.dma_start(WB, krows(dram["xa_wv"])).then_inc(S("ld_wv"), 16)
            sp.wait_ge(*at("yT_ps", 2))
            sp.dma_start(W1, krows(dram["xa_wq"])).then_inc(S("ld_wq"), 16)
            sp.wait_ge(*at("pe_v", 4))
            sp.dma_start(WB, krows(dram["xa_wo"])).then_inc(S("ld_wo2"), 16)

            def load_gu(e, q):
                src = dram["w_gu"][e, q * 256:(q + 1) * 256, :].rearrange("(c p) n -> p c n", p=P)
                dst = A[:, q * 4096:(q + 1) * 4096].rearrange("p (c n) -> p c n", c=2)
                sp.dma_start(dst, src).then_inc(S(f"ld_gu{q}"), 16)

            def load_dn(e, q):
                src = dram["w_dn"][e, q * 512:(q + 1) * 512, :].rearrange("(c p) n -> p c n", p=P)
                dst = A[:, (4 + q) * 4096:(5 + q) * 4096].rearrange("p (c n) -> p c n", c=4)
                sp.dma_start(dst, src).then_inc(S(f"ld_dn{q}"), 16)

            for q in range(2):
                load_gu(0, q)
            sp.wait_ge(*at("pe_wout", 4))
            for q in range(2):
                load_dn(0, q)
            sp.wait_ge(*at("pe_q", KT))
            for q in range(2, 4):
                load_gu(0, q)
            sp.wait_ge(*at("pe_wo", 4))
            sp.dma_start(bgu, dram["b_gu"][0:1, :].rearrange("p (w g n) -> p w g n", w=2, g=2)).then_inc(S("ld_bgu"), 16)
            sp.dma_start(bdn, dram["b_dn"]).then_inc(S("ld_bdn"), 16)
            sp.dma_start(fin_g, a["final_norm_g"].partition_broadcast(P)).then_inc(S("ld_fing"), 16)

            def load_expert(e, i):
                sp.wait_ge(*at("used_b", i))
                sp.dma_start(bgu, dram["b_gu"][bass.ds(e, 1), :].rearrange("p (w g n) -> p w g n", w=2, g=2)).then_inc(S("ld_bgu"), 16)
                for q in range(4):
                    sp.wait_ge(*at(f"used_gu{q}", i))
                    load_gu(e, q)
                for q in range(2):
                    sp.wait_ge(*at(f"used_dn{q}", i))
                    load_dn(e, q)

            with sp.Fori(1, NE) as i:
                load_expert(i, i)
            sp.wait_ge(*at("steps", 1))
            total = sp.value_load(steps_i[0:1, 0:1], min_val=NE, max_val=NE * ROUNDS)
            with sp.If(total > NE):
                with sp.Fori(NE, total) as i:
                    load_expert(i % NE, i)
            sp.wait_ge(*at("y_out", TT))
            sp.dma_start(out[0].rearrange("(i p) d -> p i d", p=P), fin).then_inc(S("stored"), 16)
            sp.wait_ge(*at("stored", 16))

        @block.gpsimd
        def _(pool):
            pg = nc.gpsimd
            n = [0]

            def c(ins):
                n[0] += 1
                ins.then_inc(S("consts"), 1)
                pool.wait_ge(*at("consts", n[0]))

            c(pg.memset(neg_half[:], -0.5))
            c(pg.memset(ident[:], 0.0))
            c(pg.affine_select(out=ident[:], in_=ident[:], compare_op=ALU.not_equal, fill=1.0, base=0,
                               pattern=[[-1, P]], channel_multiplier=1))
            pool.sem_inc(S("ident"), 1)
            for w in (wx_bd, wa_bd):
                pg.memset(w, 0.0).then_inc(S("bd_zero"), 1)
            pool.wait_ge(*at("bd_zero", 2))
            for name, w in (("lru_wx", wx_bd), ("lru_wa", wa_bd)):
                for half in range(2):
                    src = dram[name].rearrange("(c w) i j -> w i c j", w=2)[half]
                    pool.dma_start(w[64 * half:64 * half + 64, :, 64 * half:64 * half + 64], src).then_inc(S("ld_lruw"), 16)
            c(pg.memset(ones[:], 1.0))
            c(pg.memset(before[:], 1.0))
            c(pg.affine_select(out=before[:], in_=before[:], compare_op=ALU.is_gt, fill=0.0, base=0,
                               pattern=[[1, P]], channel_multiplier=-1))
            c(pg.memset(head_ones[:], 0.0))
            for h in range(2):
                c(pg.memset(head_ones[64 * h:64 * h + 64, 64 * h:64 * h + 64], 1.0))
            c(pg.memset(restart[:], 1.0))
            c(pg.memset(restart[:].rearrange("p (n t) -> p n t", t=CH)[:, :, 0:1], 0.0))
            c(pg.memset(eye8, 0.0))
            for h in range(2):
                s = slice(64 * h, 64 * h + 64)
                c(pg.affine_select(out=eye8[s], in_=eye8[s], compare_op=ALU.not_equal, fill=1.0, base=0,
                                   pattern=[[0, 8], [-1, 64]], channel_multiplier=1))
            for m in (mask_ar, mask_n, mask_o, mask_nt):
                c(pg.memset(m, 1.0))
            for h in range(2):
                s = slice(64 * h, 64 * h + 64)
                for w, op in ((0, ALU.is_gt), (1, ALU.is_ge)):
                    v = mask_ar[s, :, w, :]
                    c(pg.affine_select(out=v, in_=v, compare_op=op, fill=0.0, base=0,
                                       pattern=[[0, 4], [1, 64]], channel_multiplier=-1))
                v = mask_o[s].rearrange("p e (b j) -> p e b j", j=16)
                c(pg.affine_select(out=v, in_=v, compare_op=ALU.is_ge, fill=0.0, base=-16,
                                   pattern=[[0, 8], [-16, 4], [0, 16]], channel_multiplier=1))
                v = mask_n[s].rearrange("p e (b j) -> p e b j", j=16)
                c(pg.affine_select(out=v, in_=v, compare_op=ALU.is_gt, fill=0.0, base=16,
                                   pattern=[[0, 8], [16, 4], [0, 16]], channel_multiplier=-1))
                c(pg.affine_select(out=mask_n[s], in_=mask_n[s], compare_op=ALU.is_gt, fill=0.0, base=0,
                                   pattern=[[0, 8], [-1, 64]], channel_multiplier=1))
                v = mask_nt[s].rearrange("p e (b j) -> p e b j", j=16)
                c(pg.affine_select(out=v, in_=v, compare_op=ALU.is_ge, fill=0.0, base=0,
                                   pattern=[[0, 8], [-16, 4], [0, 16]], channel_multiplier=1))
                c(pg.affine_select(out=mask_nt[s], in_=mask_nt[s], compare_op=ALU.is_gt, fill=0.0, base=0,
                                   pattern=[[0, 8], [1, 64]], channel_multiplier=-1))
            c(pg.iota(slot_no[:], pattern=[[0, 2], [1, SLOTS]], base=0, channel_multiplier=0,
                      allow_small_or_imprecise_dtypes=True))
            pool.sem_inc(S("consts_all"), 1)

            def inv_root(dst, ss, shift, name, half):
                c(pg.tensor_scalar(dst, ss, shift, None, ALU.add))
                pg.tensor_tensor(dst, dst, half, ALU.pow).then_inc(S(name), 1)

            pool.wait_ge(*at("ss_x", 2))
            inv_root(st[:, 2:4], st[:, 0:2], D * EPS, "rs_x", neg_half[:, 0:2])
            pool.wait_ge(*at("ss_mem", 2))
            inv_root(st[:, 6:8], st[:, 4:6], D * EPS, "rs_mem", neg_half[:, 0:2])
            pool.wait_ge(*at("gn_ss", 1))
            inv_root(gst[:, 4], gst[:, 2], HEAD * GN_EPS, "gn_rs", neg_half[:, :].rearrange("p (i h) -> p i h", i=TT))
            for r in range(3):
                for i in range(TT):
                    pool.wait_ge(S(f"ss_x{r + 1}"), i + 1)
                    inv_root(st[:, 10 + 4 * r + i:11 + 4 * r + i], st[:, 8 + 4 * r + i:9 + 4 * r + i], D * EPS, f"rs_x{r + 1}", neg_half[:, 0:1])

        @block.scalar
        def _(act):
            ac = nc.scalar
            made = {}

            def done(ins, name):
                sem = S(name)
                made[sem.name] = made.get(sem.name, 0) + 1
                ins.then_inc(sem, 1)
                act.wait_ge(sem, made[sem.name])

            r0 = 0
            for name, rows in PARAM_ROWS:
                src = dram[name]
                if len(src.shape) == 2:
                    src = src.rearrange("a b -> (a b)")
                act.dma_start(par_rows[r0:r0 + rows, :], src.rearrange("(r p) -> r p", p=P)).then_inc(S("ld_par"), 16)
                r0 += rows
            act.dma_start(wa_up[0:64, :], dram["rwkv_w_up"]).then_inc(S("ld_lora_up"), 16)
            act.dma_start(wa_up[64:128, :], dram["rwkv_a_up"]).then_inc(S("ld_lora_up"), 16)
            act.dma_start(g_up[:], dram["rwkv_g_up"]).then_inc(S("ld_lora_up"), 16)
            act.dma_start(lnx[:, 0, :], dram["rwkv_lnx_g"].partition_broadcast(P)).then_inc(S("ld_late"), 16)
            act.dma_start(lnx[:, 1, :], dram["rwkv_lnx_b"].partition_broadcast(P)).then_inc(S("ld_late"), 16)
            act.dma_start(b_rt[:], dram["b_router"].partition_broadcast(P)).then_inc(S("ld_late"), 16)
            act.dma_start(w_rt[:], krows(dram["w_router"])).then_inc(S("ld_late"), 16)

            act.wait_ge(*at("ld_x", 16))
            for i in range(TT):
                done(ac.activation(YT[:, 4 * i:4 * i + 4, :], X[:, i, :].rearrange("p (c t) -> p c t", c=4), ACT.Square,
                                   accum_out=st[:, i:i + 1]), "ss_x")
            act.wait_ge(*at("ld_mem", 16))
            for i in range(TT):
                done(ac.activation(YT[:, 4 * i:4 * i + 4, :], mem[:, i, :].rearrange("p (c t) -> p c t", c=4), ACT.Square,
                                   accum_out=st[:, 4 + i:5 + i]), "ss_mem")
            act.wait_ge(*at("par", 1))
            act.wait_ge(*at("lam_abs", 1))
            done(ac.activation(lam[:, 1, :], lam[:, 0, :], ACT.Exp, scale=-1.0), "lam_e")
            act.wait_ge(*at("lam_w", 1))
            done(ac.activation(lam[:, 3, :], lam[:, 2, :], ACT.Ln), "lam_ln")
            act.wait_ge(*at("t_x", 4))
            for c in (4, 5, 6, 7):
                done(ac.activation(HT[:, c, :], PS[c // 2][:, (c % 2) * 256:(c % 2) * 256 + 256], ACT.Identity,
                                   scale=col("norm_mix_g", c)), "hT_a")
            act.wait_ge(*at("t_mem", 4))
            for c in (4, 5, 6, 7):
                done(ac.activation(MT[:, c, :], PS[c // 2][:, (c % 2) * 256:(c % 2) * 256 + 256], ACT.Identity,
                                   scale=col("norm_mem_g", c)), "mT_a")
            act.wait_ge(*at("xl_pads", 1))
            for c in range(CT):
                act.wait_ge(*at("u_xl", c + 1))
                done(ac.copy(xl_pad[:, c, 3:3 + T], PS[4 + c][:, 0:T]), "xl")
            for c in range(CT):
                act.wait_ge(*at("u_gl", c + 1))
                done(ac.activation(YT[:, c, :], PS[4 + c][:, 0:T], ACT.Gelu_apprx_tanh), "gelu")

            def shift_a(name, dst, mu0):
                n = 2 if name == "lora" else CT
                for c in range(n):
                    act.wait_ge(*at("u_" + name, c + 1))
                    b = PS[4 + c]
                    done(ac.activation(dst[:, c, :], b[:, 0:T], ACT.Identity, scale=omu[:, mu0 + c:mu0 + c + 1]),
                         "sa_" + name)

            act.wait_ge(*at("omu", 1))
            shift_a("r", r_c, 0)
            shift_a("k", k_c, 4)
            for c in range(CT):
                act.wait_ge(*at("lru_gates", c + 1))
                done(ac.activation(gx[:, c, :], PS[c][:, 0:T], ACT.Sigmoid, bias=col("lru_bx", c)), "gx")
                done(ac.activation(ga[:, c, :], PS[c][:, T:2 * T], ACT.Sigmoid, bias=col("lru_ba", c)), "ga")
            shift_a("lora", lora, 12)
            act.wait_ge(*at("sv_lora", 2))
            done(ac.activation(lora[0:64, 0, :], lora[0:64, 0, :], ACT.Tanh), "lora_f")
            done(ac.activation(lora[:, 1, :], lora[:, 1, :], ACT.Sigmoid), "lora_f")
            act.wait_ge(*at("lam_rate", 2))
            for c in range(CT):
                done(ac.activation(th[:, c, :], ga[:, c, :], ACT.Tanh, scale=lam[:, 6, c:c + 1]), "lru_th")
            for c in range(CT):
                done(ac.activation(dec[:, c, :], ga[:, c, :], ACT.Exp, scale=lam[:, 7, c:c + 1]), "lru_dec")
            shift_a("v", v_c, 8)
            act.wait_ge(*at("lru_b2", 1))
            done(ac.activation(th, th, ACT.Sqrt), "lru_root")
            for c in range(CT):
                act.wait_ge(*at("z_a", 1))
                done(ac.activation(sig[:, c, :], PS[c // 2][:, (c % 2) * T:(c % 2) * T + T], ACT.Sigmoid,
                                   bias=col("rwkv_w0", c)), "sig")
            for c in range(CT):
                done(ac.activation(a_c[:, c, :], PS[2 + c // 2][:, (c % 2) * T:(c % 2) * T + T], ACT.Sigmoid,
                                   bias=col("rwkv_a0", c)), "a_c")
            act.wait_ge(*at("g_ps", 2))
            for i in range(TT):
                done(ac.copy(g_t[:, i], PS[4 + i][:, :].rearrange("p (h k) -> p h k", h=NH)), "g_t")
            act.wait_ge(*at("kk", 1))
            act.wait_ge(*at("lru_in", 1))
            done(ac.activation(sq, kk, ACT.Square), "kk_sq")
            for c in range(2):
                act.wait_ge(*at("kk_ss", c + 1))
                done(ac.activation(U(1)[:, c * 512:(c + 1) * 512], PS[c][:, :], ACT.Sqrt), "kk_rn")
            act.wait_ge(*at("Z", CT))
            done(ac.activation(Dt, Z, ACT.Exp, scale=-DECAY), "exps")
            done(ac.activation(inv_d, Z, ACT.Exp, scale=DECAY), "exps")
            act.wait_ge(*at("zp", 1))
            done(ac.activation(d_prev, zp, ACT.Exp, scale=-DECAY), "exps")

            def k_copy(lo, hi):
                for c in range(lo, hi):
                    act.wait_ge(*at("pe_k", c + 1))
                    done(ac.copy(HT[:, c, :], PS[6 + c % 2][:, 0:T]), "K")

            def v_copy(lo, hi):
                for q in range(lo, hi):
                    act.wait_ge(*at("pe_v", q + 1))
                    done(ac.copy(V[:, q // 2, (q % 2) * 512:(q % 2) * 512 + 512], PS[6 + q % 2][:, :]), "V")

            k_copy(0, 8)
            for q, (dst, b) in enumerate(((v_t, 0), (al_t, 2))):
                act.wait_ge(*at("tok_ps", 2 * q + 2))
                for i in range(TT):
                    done(ac.copy(dst[:, i], PS[b + i][:, :].rearrange("p (h k) -> p h k", h=NH)), "tok")
            v_copy(0, 1)

            def out_of(name, banks, dst, made_name):
                act.wait_ge(*at(name, 1))
                for j in range(2):
                    done(ac.copy(dst[:, j], PS[banks + j][:, :].rearrange("p (h k) -> p h k", h=NH)), made_name)

            out_of("G_ps", 4, G, "G")
            out_of("N2_ps", 0, N2, "N2")
            out_of("N4_ps", 0, N4, "N4")
            v_copy(1, 2)
            out_of("N8_ps", 2, N8, "N8")
            v_copy(2, 4)
            out_of("E_ps", 0, E, "E")
            out_of("YW_ps", 4, Y1[0], "Y1")
            out_of("E2t_ps", 4, E2t, "E2t")
            act.wait_ge(*at("Yuv_ps", 1))
            for j in range(2):
                for np_ in range(2):
                    s = slice(64 * np_, 64 * np_ + 64)
                    done(ac.copy(Yuv[s, j ^ np_], PS[2 + j][s, :].rearrange("p (h k) -> p h k", h=NH)), "Yuv")
            for n in (1, 2):
                act.wait_ge(*at("S_ps", n))
                done(ac.copy(St[64:128, n - 1], PS[1][64:128, 0:256].rearrange("p (c k) -> p c k", c=CT)), "St_a")
            act.wait_ge(*at("yT_ps", 2))
            done(ac.copy(YT[:, 6:8, :], PS[1][:, :].rearrange("p (c t) -> p c t", c=2)), "yT_a")

            def square(name, r):
                for i in range(TT):
                    act.wait_ge(*at(name, i * 2 + 2))
                    done(ac.activation(YT[:, 4 * i:4 * i + 4, :], X[:, i, :].rearrange("p (c t) -> p c t", c=4),
                                       ACT.Square, accum_out=st[:, 4 + 4 * r + i:5 + 4 * r + i]), f"ss_x{r}")

            act.wait_ge(*at("pe_wout", 4))
            square("x1", 1)

            def turned(ps_name, gain, made_name):
                act.wait_ge(*at(ps_name, 4))
                for c in (4, 5, 6, 7):
                    done(ac.activation(MT[:, c, :], PS[c // 2][:, (c % 2) * 256:(c % 2) * 256 + 256], ACT.Identity,
                                       scale=col(gain, c)), made_name)

            turned("t_x1", "norm_xa_g", "x1T_a")
            for c in range(1, KT, 2):
                act.wait_ge(*at("pe_q", c + 1))
                done(ac.activation(YT[:, c, :], PS[4 + c % 4][:, 0:T], ACT.Identity, scale=float(XD) ** -0.5), "q_a")
            for u in range(2 * XH):
                act.wait_ge(*at("nmax", u + 1))
                done(ac.activation(prob(u), PS[u % 4][:, 0:T], ACT.Exp, bias=ast[:, 1, u:u + 1],
                                   accum_out=ast[:, 2, u:u + 1]), "expd")
            for u in range(XH):
                act.wait_ge(*at("pT_ps", u + 1))
                done(ac.copy(prob_t(u)[:, 1], PS[4 + 2 * (u % 2) + 1][:, 0:T]), "pT_a")
            for u in range(XH):
                act.wait_ge(*at("o_ps", 2 * u + 2))
                done(ac.copy(YT[:, 2 * u + 1, :], PS[2 * (u % 2) + 1][:, 0:T]), "oT_a")
            act.wait_ge(*at("pe_wo", 4))
            square("x2", 2)
            turned("t_x2", "norm_ffn_g", "x2T_a")
            for i in range(TT):
                act.wait_ge(*at("nl", i + 1))
                done(ac.activation(rt[:, 1, i, :], rt[:, 0, i, :], ACT.Exp, bias=top[:, i, 7:8]), "r_exp")

            act.wait_ge(*at("steps", 1))
            total = act.value_load(steps_i[0:1, 0:1], min_val=NE, max_val=NE * ROUNDS)
            with act.Fori(0, total) as i:
                act.wait_ge(S("gate_in"), i + 1)
                ac.activation(m_s, m_g, ACT.Sigmoid, scale=ALPHA).then_inc(S("gate_sig"), 1)
                act.wait_ge(S("turned"), i + 2)
                ac.copy(sel_t, PS[6][:, 0:256].rearrange("p (i t) -> p i t", i=TT)).then_inc(S("sel_t"), 1)
                act.wait_ge(S("used_dn1"), i + 1)
                ac.copy(y_e, PS[6][:, :]).then_inc(S("y_sb"), 1)
            for i in range(TT):
                act.wait_ge(*at("x3", 2 * i + 2))
                done(ac.activation(yt_f[:, 0:1024], X[:, i, :], ACT.Square, accum_out=st[:, 16 + i:17 + i]), "ss_x3")

        @block.vector
        def _(dve):
            v = nc.vector
            made = {}

            def done(ins, name="dve_step"):
                sem = S(name)
                made[sem.name] = made.get(sem.name, 0) + 1
                ins.then_inc(sem, 1)
                dve.wait_ge(sem, made[sem.name])

            done(v.memset(VX[:], 0.0), "xl_pads")
            dve.wait_ge(*at("rs_x", 1))
            for i in range(TT):
                done(v.tensor_scalar(xn[:, i, :], X[:, i, :],
                                     st[:, 2 + i:3 + i], ROOT_D, ALU.mult, ALU.mult), "xn")
            dve.wait_ge(*at("par_ps", 1))
            done(v.tensor_copy(par[:, 0:NPAR], PS[7][:, 0:NPAR]), "par")
            done(v.tensor_scalar(omu[:], par[:, COL["rwkv_mu"]:COL["rwkv_mu"] + 14], -1.0, 1.0, ALU.mult, ALU.add), "omu")
            lm = par[:, COL["lru_lambda"]:COL["lru_lambda"] + CT]
            done(v.tensor_scalar(lam[:, 4, :], lm, -1.0, None, ALU.mult))
            done(v.tensor_tensor(lam[:, 0, :], lam[:, 4, :], lm, ALU.max), "lam_abs")
            dve.wait_ge(*at("lam_e", 1))
            done(v.tensor_scalar(lam[:, 2, :], lam[:, 1, :], 1.0, None, ALU.add), "lam_w")
            done(v.tensor_scalar(lam[:, 5, :], lam[:, 2, :], -1.0, None, ALU.add))
            dve.wait_ge(*at("rs_mem", 1))
            for i in range(TT):
                done(v.tensor_scalar(mem[:, i, :], mem[:, i, :], st[:, 6 + i:7 + i], ROOT_D, ALU.mult, ALU.mult), "memn")
            dve.wait_ge(*at("t_x", 2))
            for c in range(4):
                done(v.tensor_scalar(HT[:, c, :], PS[c // 2][:, (c % 2) * 256:(c % 2) * 256 + 256],
                                     col("norm_mix_g", c), None, ALU.mult), "hT_v")
            dve.wait_ge(*at("t_mem", 2))
            for c in range(4):
                done(v.tensor_scalar(MT[:, c, :], PS[c // 2][:, (c % 2) * 256:(c % 2) * 256 + 256],
                                     col("norm_mem_g", c), None, ALU.mult), "mT_v")
            dve.wait_ge(*at("lam_ln", 1))
            done(v.tensor_scalar(lam[:, 0, :], lam[:, 5, :], 0.0, None, ALU.is_equal))
            done(v.tensor_tensor(lam[:, 5, :], lam[:, 5, :], lam[:, 0, :], ALU.add))
            done(v.reciprocal(lam[:, 5, :], lam[:, 5, :]))
            done(v.tensor_tensor(lam[:, 3, :], lam[:, 3, :], lam[:, 5, :], ALU.mult))
            done(v.tensor_tensor(lam[:, 3, :], lam[:, 3, :], lam[:, 0, :], ALU.add))
            done(v.tensor_tensor(lam[:, 3, :], lam[:, 3, :], lam[:, 1, :], ALU.mult))
            done(v.scalar_tensor_tensor(out=lam[:, 3, :], in0=lam[:, 4, :], scalar=0.0, in1=lam[:, 3, :],
                                        op0=ALU.max, op1=ALU.add))
            done(v.tensor_scalar(lam[:, 6, :], lam[:, 3, :], 8.0, None, ALU.mult), "lam_rate")
            done(v.tensor_scalar(lam[:, 7, :], lam[:, 3, :], -8.0, None, ALU.mult), "lam_rate")
            dve.wait_ge(*at("u_gl", CT))
            for c in range(CT):
                dve.wait_ge(*at("xl", c + 1))
                done(v.tensor_scalar(xc[:, c, :], xl_pad[:, c, 0:T], col("conv_w", c), col("conv_b", c),
                                     ALU.mult, ALU.add), "conv")
                for j in range(1, 4):
                    done(v.scalar_tensor_tensor(out=xc[:, c, :], in0=xl_pad[:, c, j:j + T],
                                                scalar=col("conv_w", 4 * j + c), in1=xc[:, c, :],
                                                op0=ALU.mult, op1=ALU.add), "conv")

            def shift_v(name, dst, mu0):
                n = 2 if name == "lora" else CT
                for c in range(n):
                    dve.wait_ge(*at("sa_" + name, c + 1))
                    done(v.scalar_tensor_tensor(out=dst[:, c, 1:T], in0=PS[4 + c][:, 0:T - 1],
                                                scalar=col("rwkv_mu", mu0 + c), in1=dst[:, c, 1:T],
                                                op0=ALU.mult, op1=ALU.add), "sv_" + name)

            shift_v("r", r_c, 0)
            shift_v("k", k_c, 4)
            dve.wait_ge(*at("u_k", CT))
            for c in range(CT):
                done(v.tensor_scalar(kk[:, c, :], k_c[:, c, :], col("rwkv_k_k", c), None, ALU.mult),
                     "kk" if c == CT - 1 else "dve_step")
            shift_v("lora", lora, 12)
            dve.wait_ge(*at("lru_dec", CT))
            done(v.tensor_scalar(ga, th, 1.0, None, ALU.add))
            done(v.reciprocal(ga, ga))
            done(v.scalar_tensor_tensor(out=U(3), in0=U(3), scalar=2.0, in1=U(2), op0=ALU.mult, op1=ALU.mult))
            done(v.tensor_tensor(gx, gx, xc, ALU.mult), "lru_b2")
            shift_v("v", v_c, 8)
            dve.wait_ge(*at("lru_root", 1))
            done(v.tensor_tensor(th, th, gx, ALU.mult), "lru_in")
            for c in range(CT):
                done(v.tensor_tensor_scan(ga[:, c, :], dec[:, c, :], th[:, c, :], 0.0, ALU.mult, ALU.add))
            done(v.tensor_tensor(YT[:, 0:CT, :], YT[:, 0:CT, :], ga, ALU.mult), "y_lru")
            dve.wait_ge(*at("sig", CT))
            for c in range(CT):
                done(v.tensor_tensor_scan(Z[:, c, :], restart[:], sig[:, c, :], 0.0, ALU.mult, ALU.add), "Z")
            done(v.tensor_tensor(zp, Z, sig, ALU.subtract), "zp")
            dve.wait_ge(*at("kk_rn", 2))
            done(v.tensor_scalar(sq, sq, 1e-12, None, ALU.max))
            done(v.reciprocal(sq, sq))
            done(v.tensor_tensor(kk, kk, sq, ALU.mult))
            dve.wait_ge(*at("a_c", CT))
            done(v.tensor_tensor(beta, kk, a_c, ALU.mult))
            for c in range(CT):
                done(v.tensor_scalar(a_c[:, c, :], a_c[:, c, :], 1.0, col("rwkv_k_a", c), ALU.subtract, ALU.mult))
            done(v.scalar_tensor_tensor(out=U(6), in0=U(9), scalar=1.0, in1=U(6), op0=ALU.add, op1=ALU.mult))
            dve.wait_ge(*at("exps", 3))
            done(v.scalar_tensor_tensor(out=U(3), in0=U(14), scalar=-1.0, in1=U(13), op0=ALU.mult, op1=ALU.mult), "al_c")
            done(v.tensor_tensor(bt_c, beta, inv_d, ALU.mult), "bt_c")
            done(v.tensor_tensor(kt_c, k_c, inv_d, ALU.mult), "kt_c")
            done(v.tensor_tensor(AR[:, 1], r_c, Dt, ALU.mult), "r_til")
            last_d = Dt.rearrange("p c (n s) -> p c n s", s=CH)[:, :, :, CH - 1:CH]
            done(v.tensor_copy(dc[:].unsqueeze(3), last_d))
            dcb = dc[:].unsqueeze(3).broadcast_to([P, CT, NCH, CH])
            done(v.tensor_tensor(bh_c.rearrange("p c (n s) -> p c n s", s=CH),
                                 bt_c.rearrange("p c (n s) -> p c n s", s=CH), dcb, ALU.mult), "bh_c")
            done(v.tensor_tensor(kh_c.rearrange("p c (n s) -> p c n s", s=CH),
                                 kt_c.rearrange("p c (n s) -> p c n s", s=CH), dcb, ALU.mult), "kh_c")
            for c in range(CT):
                done(v.scalar_tensor_tensor(out=rkk[:, c, :], in0=r_c[:, c, :], scalar=col("rwkv_r_k", c),
                                            in1=k_c[:, c, :], op0=ALU.mult, op1=ALU.mult), "rkk")
            for q, (dst, b) in enumerate(((bh_t, 4), (kh_t, 0))):
                dve.wait_ge(*at("tok_ps", 2 * q + 6))
                for i in range(TT):
                    done(v.tensor_copy(dst[:, i], PS[b + i][:, :].rearrange("p (h k) -> p h k", h=NH)), "tok_v")
            dve.wait_ge(*at("bonus_ps", 1))
            done(v.tensor_copy(gst[:, 7], PS[2][:, 0:TT * NH].rearrange("p (i h) -> p i h", i=TT)), "bonus")
            for u in range(8):
                kind, i, hp = u // 4, (u // 2) % 2, u % 2
                dst = (STb, STk)[kind]
                dve.wait_ge(*at("st_ps", 2 * (u // 2) + 2))
                done(v.tensor_tensor(dst[:, i].rearrange("p (c e) w k -> p c e w k", e=2)[:, :, hp],
                                     PS[2 + u % 4][:, :].rearrange("p (c w k) -> p c w k", c=CT, w=2),
                                     mask_ar, ALU.mult), "st")
            for i in range(TT):
                dve.wait_ge(*at("n_ps", 2 * i + 2))
                for hp in range(2):
                    src = PS[2 * i + hp][:, 0:256].rearrange("p (c k) -> p c k", c=CT)
                    for dst, mask, nm in ((Nm, mask_n, "dve_step"), (Om, mask_o, "n_sb")):
                        done(v.tensor_tensor(dst[:, i].rearrange("p (c e) k -> p c e k", e=2)[:, :, hp], src,
                                             mask[:, 0:4, :], ALU.mult), nm)
                done(v.tensor_tensor(Ntm[:, i], STb[:, i, :, 0, :], mask_nt, ALU.mult), "nt_sb")
            for j in range(2):
                for np_ in range(2):
                    s = slice(64 * np_, 64 * np_ + 64)
                    done(v.tensor_tensor(P1[s, j], Ntm[s, j ^ np_], eye8[s], ALU.add), "P1")

            def out_of(name, banks, dst, made_name, add=None):
                dve.wait_ge(*at(name, 1))
                for j in range(2):
                    src = PS[banks + j][:, :].rearrange("p (h k) -> p h k", h=NH)
                    if add is None:
                        done(v.tensor_copy(dst[:, j], src), made_name)
                    else:
                        done(v.tensor_tensor(dst[:, j], src, add[:, j], ALU.add), made_name)

            out_of("N2t_ps", 2, N2t, "N2t")
            out_of("P2_ps", 4, P2, "P2", P1)
            out_of("N4t_ps", 2, N4t, "N4t")
            out_of("P4_ps", 4, P4, "P4", P2)
            out_of("T16_ps", 0, T16, "T16", P4)
            out_of("Et_ps", 2, Et, "Et")
            out_of("YG_ps", 0, Y1[1], "Y1g")
            for n in (1, 2):
                done(v.tensor_tensor(DI[:, n - 1], eye8[:, 0:CT, :],
                                     dc[:, :, n:n + 1].broadcast_to([P, CT, CH]), ALU.mult), "DI")
            out_of("Y2w_ps", 0, Y2[0], "Y2", Y1[0])
            out_of("Y2g_ps", 2, Y2[1], "Y2", Y1[1])
            out_of("XW_ps", 4, XW, "XW", Y2[0])
            out_of("XU_ps", 0, XU, "XU", Y2[1])
            dve.wait_ge(*at("NS_ps", 1))
            done(v.tensor_copy(NS[:, 0:3:2], PS[4][:, :].rearrange("p (i c k) -> p i c k", i=2, c=CT)), "NS")
            done(v.tensor_copy(NS[:, 1], PS[5][:, 0:256].rearrange("p (c k) -> p c k", c=CT)), "NS")
            dve.wait_ge(*at("M_ps", 1))
            done(v.tensor_tensor(Mt[:, 0], PS[1][:, 0:256].rearrange("p (c k) -> p c k", c=CT), DI[:, 0], ALU.add), "Mt")
            done(v.tensor_tensor(Mt[:, 1], PS[0][:, 0:256].rearrange("p (c k) -> p c k", c=CT), DI[:, 1], ALU.add), "Mt")
            dve.wait_ge(*at("Q_ps", 1))
            r_v = AR[:, 1].rearrange("p c (n s) -> p c n s", s=CH)
            for n in (1, 2, 3):
                src = PS[4 + n % 2][:, (n // 2) * 256:(n // 2) * 256 + 256].rearrange("p (c k) -> p c k", c=CT)
                done(v.tensor_tensor(Q[:, n], src, r_v[:, :, n, :], ALU.add), "Q")
            for n in (1, 2):
                dve.wait_ge(*at("S_ps", n))
                done(v.tensor_copy(St[0:64, n - 1], PS[0][0:64, 0:256].rearrange("p (c k) -> p c k", c=CT)), "St_v")
            for i in range(TT):
                dve.wait_ge(*at("Ys_ps", i + 1))
                dve.wait_ge(*at("Yuv", 4))
                s = slice(64, P) if i == 0 else slice(0, P)
                if i == 0:
                    done(v.tensor_copy(Y[0:64, 0], Yuv[0:64, 0]))
                for hp in range(2):
                    e = lambda t: t[s, i].rearrange("p (c e) k -> p c e k", e=2)[:, :, hp]
                    done(v.tensor_tensor(e(Y), PS[4 - 2 * i + hp][s, 0:256].rearrange("p (c k) -> p c k", c=CT),
                                         e(Yuv), ALU.add), "Y")
            bc = lambda x: x.unsqueeze(3).broadcast_to([P, TT, NH, HEAD])
            done(v.tensor_reduce(gst[:, 0], Y, AX_X, ALU.add))
            done(v.tensor_scalar(gst[:, 1], gst[:, 0], 1.0 / HEAD, None, ALU.mult))
            done(v.tensor_tensor(Y, Y, bc(gst[:, 1]), ALU.subtract))
            done(v.tensor_tensor(Yt1, Y, Y, ALU.mult))
            done(v.tensor_reduce(gst[:, 2], Yt1, AX_X, ALU.add), "gn_ss")
            dve.wait_ge(*at("gn_rs", 1))
            done(v.tensor_scalar(gst[:, 3], gst[:, 4], ROOT_HEAD, None, ALU.mult))
            done(v.tensor_tensor(Y, Y, bc(gst[:, 3]), ALU.mult))
            dve.wait_ge(*at("ld_late", 64))
            lx = lambda w: lnx[:, w, :].rearrange("p (h k) -> p h k", h=NH)
            for i in range(TT):
                done(v.tensor_tensor(Y[:, i], Y[:, i], lx(0), ALU.mult))
                done(v.tensor_tensor(Y[:, i], Y[:, i], lx(1), ALU.add))
            done(v.tensor_tensor(Yt1, v_t, bc(gst[:, 7]), ALU.mult))
            done(v.tensor_tensor(Y, Y, Yt1, ALU.add))
            dve.wait_ge(*at("g_t", 2))
            done(v.tensor_tensor(Y, Y, g_t, ALU.mult), "y_rwkv")
            dve.wait_ge(*at("yT_ps", 1))
            done(v.tensor_copy(YT[:, 4:6, :], PS[0][:, :].rearrange("p (c t) -> p c t", c=2)), "yT_v")

            def add_to_x(ps_name, made_name):
                for u in range(4):
                    dve.wait_ge(*at(ps_name, u + 1))
                    i, h = u // 2, u % 2
                    xs = X[:, i, h * 512:(h + 1) * 512]
                    done(v.tensor_tensor(xs, PS[4 + u][:, :], xs, ALU.add), made_name)

            def norm_rows(r, made_name, dst):
                for i in range(TT):
                    dve.wait_ge(S(f"rs_x{r}"), i + 1)
                    at_ = 6 + 4 * r + i
                    done(v.tensor_scalar(dst[:, i, :], X[:, i, :], st[:, at_:at_ + 1], ROOT_D, ALU.mult, ALU.mult), made_name)

            def turned(ps_name, gain, made_name):
                dve.wait_ge(*at(ps_name, 2))
                for c in range(4):
                    done(v.tensor_scalar(MT[:, c, :], PS[c // 2][:, (c % 2) * 256:(c % 2) * 256 + 256],
                                         col(gain, c), None, ALU.mult), made_name)

            add_to_x("pe_wout", "x1")
            norm_rows(1, "x1n", xm)
            turned("t_x1", "norm_xa_g", "x1T_v")
            for c in range(0, KT, 2):
                dve.wait_ge(*at("pe_q", c + 1))
                done(v.tensor_scalar(YT[:, c, :], PS[4 + c % 4][:, 0:T], float(XD) ** -0.5, None, ALU.mult), "q_v")

            def row_max(u):
                dve.wait_ge(*at("sc_ps", u + 1))
                done(v.tensor_reduce(ast[:, 0, u:u + 1], PS[u % 4][:, 0:T], AX_X, ALU.max))
                done(v.tensor_scalar(ast[:, 1, u:u + 1], ast[:, 0, u:u + 1], -1.0, None, ALU.mult), "nmax")

            def normed(u):
                dve.wait_ge(*at("expd", u + 1))
                done(v.reciprocal(ast[:, 3, u:u + 1], ast[:, 2, u:u + 1]))
                done(v.tensor_scalar(prob(u), prob(u), ast[:, 3, u:u + 1], None, ALU.mult), "prob")

            for u in range(2 * XH + 1):
                if u < 2 * XH:
                    row_max(u)
                if u >= 1:
                    normed(u - 1)
            for u in range(XH):
                dve.wait_ge(*at("pT_ps", u + 1))
                done(v.tensor_copy(prob_t(u)[:, 0], PS[4 + 2 * (u % 2)][:, 0:T]), "pT_v")
            for u in range(XH):
                dve.wait_ge(*at("o_ps", 2 * u + 1))
                done(v.tensor_copy(YT[:, 2 * u, :], PS[2 * (u % 2)][:, 0:T]), "oT_v")
            add_to_x("pe_wo", "x2")
            norm_rows(2, "x2n", x3n)
            turned("t_x2", "norm_ffn_g", "x2T_v")
            for i in range(TT):
                dve.wait_ge(*at("rl_ps", i + 1))
                done(v.tensor_tensor(rt[:, 0, i, :], PS[4 + i][:, 0:NE], b_rt[:], ALU.add))
                done(v.max(top[:, i, :], rt[:, 0, i, :]))
                thr = top[:, i, 3:4]
                done(v.tensor_scalar(rt[:, 2, i, :], rt[:, 0, i, :], thr, None, ALU.is_gt))
                done(v.tensor_scalar(rt[:, 3, i, :], rt[:, 0, i, :], thr, None, ALU.is_equal))
                done(v.tensor_reduce(cnt[:, i:i + 1], rt[:, 2, i, :], AX_X, ALU.add))
                done(v.tensor_scalar(cnt[:, i:i + 1], cnt[:, i:i + 1], -1.0, 4.0, ALU.mult, ALU.add))
                done(v.tensor_tensor_scan(rt[:, 4, i, :], ones[:, 0:NE], rt[:, 3, i, :], 0.0, ALU.mult, ALU.add))
                done(v.tensor_scalar(rt[:, 4, i, :], rt[:, 4, i, :], cnt[:, i:i + 1], None, ALU.is_le))
                done(v.tensor_tensor(rt[:, 3, i, :], rt[:, 3, i, :], rt[:, 4, i, :], ALU.mult))
                done(v.tensor_tensor(rt[:, 5, i, :], rt[:, 2, i, :], rt[:, 3, i, :], ALU.add), "picked")
                done(v.tensor_scalar(top[:, i, 7:8], top[:, i, 0:1], -1.0, None, ALU.mult), "nl")
            for i in range(TT):
                dve.wait_ge(*at("r_exp", i + 1))
                done(v.tensor_tensor(rt[:, 1, i, :], rt[:, 1, i, :], rt[:, 5, i, :], ALU.mult))
                done(v.tensor_reduce(cnt[:, 2 + i:3 + i], rt[:, 1, i, :], AX_X, ALU.add))
                done(v.reciprocal(cnt[:, 2 + i:3 + i], cnt[:, 2 + i:3 + i]))
                done(v.tensor_scalar(gate[:, i, :], rt[:, 1, i, :], cnt[:, 2 + i:3 + i], None, ALU.mult), "gate")
            dve.wait_ge(*at("rank_ps", 3))
            for i in range(TT):
                done(v.scalar_tensor_tensor(out=key[:, i, :], in0=PS[6][:, i * NE:(i + 1) * NE], scalar=1.0,
                                            in1=rt[:, 5, i, :], op0=ALU.add, op1=ALU.mult))
            done(v.tensor_scalar(key[:], key[:], -1.0, None, ALU.add), "key")
            done(v.tensor_reduce(cnt[:, 4:5], PS[6][:, 2 * NE:3 * NE], AX_X, ALU.max))
            done(v.tensor_scalar(cnt[:, 5:6], cnt[:, 4:5], float(SLOTS), None, ALU.is_gt))
            for r in range(2, ROUNDS):
                done(v.scalar_tensor_tensor(out=cnt[:, 5:6], in0=cnt[:, 4:5], scalar=float(r * SLOTS),
                                            in1=cnt[:, 5:6], op0=ALU.is_gt, op1=ALU.add))
            done(v.tensor_scalar(cnt[:, 5:6], cnt[:, 5:6], float(NE), float(NE), ALU.mult, ALU.add))
            done(v.tensor_copy(steps_i[:], cnt[:, 5:6]), "steps_v")
            dve.wait_ge(*at("gt_ps", 2))
            done(v.tensor_copy(gate_t[:], PS[7][0:NE, 0:T]), "gate_t")
            dve.sem_inc(S("steps"), 1)
            v.memset(y_e, 0.0).then_inc(S("y_sb"), 1)
            v.memset(yt_f[:, 512:768], 0.0).then_inc(S("sel_t"), 1)
            total = dve.value_load(steps_i[0:1, 0:1], min_val=NE, max_val=NE * ROUNDS)
            dve.sem_inc(S("act_sb"), 1)
            gcol = par[:, COL["norm_ffn_g"]:COL["norm_ffn_g"] + KT].unsqueeze(2).broadcast_to([P, KT, SLOTS])

            def select(e):
                for t in range(TT):
                    v.tensor_scalar(self_[:, t, :], slot_no[:, 0, :], key[:, t, bass.ds(e, 1)], None,
                                    ALU.is_equal).then_inc(S("self_sb"), 1)

            def spread():
                v.tensor_tensor(xg, PS[7][:, :].rearrange("p (c s) -> p c s", c=KT), gcol, ALU.mult).then_inc(S("xg"), 1)

            select(0)
            dve.wait_ge(S("gathered"), 1)
            spread()
            with dve.Fori(0, total) as i:
                dve.wait_ge(S("turned"), i + 1)
                e = i % NE
                for t in range(TT):
                    v.tensor_scalar(sel[:, t], slot_no[:], key[:, t, bass.ds(e, 1)], gate[:, t, bass.ds(e, 1)],
                                    ALU.is_equal, ALU.mult).then_inc(S("sel_sb"), 1)
                dve.wait_ge(S("sel_sb"), TT * (i + 1))
                for t in range(TT):
                    k_e = key[:, t, bass.ds(e, 1)]
                    v.tensor_scalar(k_e, k_e, float(SLOTS), None, ALU.subtract).then_inc(S("key_moved"), 1)
                dve.wait_ge(S("key_moved"), TT * (i + 1))
                select((i + 1) % NE)
                dve.wait_ge(S("used_gu3"), i + 1)
                v.tensor_scalar(m_g, PS[4][:, :], LIMIT, None, ALU.min).then_inc(S("gate_in"), 1)
                v.tensor_scalar(m_u, PS[5][:, :], LIMIT, -LIMIT, ALU.min, ALU.max).then_inc(S("up_in"), 1)
                dve.wait_ge(S("up_in"), i + 1)
                v.scalar_tensor_tensor(out=m_a, in0=m_u, scalar=1.0, in1=m_g, op0=ALU.add, op1=ALU.mult).then_inc(S("up_gate"), 1)
                dve.wait_ge(S("up_gate"), i + 1)
                dve.wait_ge(S("gate_sig"), i + 1)
                v.tensor_tensor(m_a, m_a, m_s, ALU.mult).then_inc(S("act_sb"), 1)
                dve.wait_ge(S("gathered"), i + 2)
                spread()
                dve.wait_ge(S("act_ps"), i + 1)
                v.tensor_copy(act_t, PS[6][:, :].rearrange("p (f m) -> p f m", f=4)).then_inc(S("act_t"), 1)
            dve.wait_ge(*at("scattered", total + 1))
            for u in range(4):
                i, h = u // 2, u % 2
                xs = X[:, i, h * 512:(h + 1) * 512]
                done(v.tensor_tensor(xs, PS[u][:, :], xs, ALU.add), "x3")
            dve.wait_ge(*at("ld_fing", 16))
            for i in range(TT):
                dve.wait_ge(S("rs_x3"), i + 1)
                done(v.tensor_scalar(X[:, i, :], X[:, i, :], st[:, 18 + i:19 + i], ROOT_D, ALU.mult, ALU.mult))
                done(v.tensor_tensor(fin[:, i, :], X[:, i, :], fin_g, ALU.mult), "y_out")

        @block.tensor
        def _(pe):
            mm, tr = nc.tensor.matmul, nc.tensor.transpose

            def turn(src, name, banks=0):
                for q in range(4):
                    for c in (2 * q, 2 * q + 1):
                        for i in range(TT):
                            x = tr(PS[q][:, (c % 2) * 256 + i * P:(c % 2) * 256 + i * P + P],
                                   src[:, i, c * P:(c + 1) * P], ident[:])
                    x.then_inc(S(name), 1)

            pe.wait_ge(*at("ident", 1))
            pe.wait_ge(*at("ld_par", 16 * len(PARAM_ROWS)))
            tr(PS[7][:, 0:NPAR], par_rows[0:NPAR, :], ident[0:NPAR, 0:NPAR]).then_inc(S("par_ps"), 1)
            pe.wait_ge(*at("xn", 2))
            turn(xn, "t_x")
            pe.wait_ge(*at("memn", 2))
            pe.wait_ge(*at("hT_v", 4))
            pe.wait_ge(*at("hT_a", 4))
            turn(mem, "t_mem")

            def u_tiles(name, lo, hi, free):
                w, _ = WV[name]
                pe.wait_ge(*at("ld_" + name, 16))
                for c in range(lo, hi):
                    if free:
                        pe.wait_ge(*at(free, c + 1))
                    for k in range(KT):
                        x = mm(PS[4 + c][:, 0:T], w[:, k, c * P:(c + 1) * P], HT[:, k, :], start=(k == 0), stop=(k == KT - 1))
                    x.then_inc(S("u_" + name), 1)

            pe.wait_ge(*at("par", 1))
            u_tiles("xl", 0, CT, None)
            u_tiles("gl", 0, CT, "xl")
            u_tiles("r", 0, CT, "gelu")
            u_tiles("k", 0, CT, "sv_r")
            pe.wait_ge(*at("ld_lruw", 64))
            pe.wait_ge(*at("mT_a", 4))
            pe.wait_ge(*at("mT_v", 4))
            for c in range(CT):
                pe.wait_ge(*at("conv", 4 * c + 4))
                mm(PS[c][:, 0:T], wx_bd[:, c, :], xc[:, c, :], start=True, stop=True)
                mm(PS[c][:, T:2 * T], wa_bd[:, c, :], xc[:, c, :], start=True, stop=True).then_inc(S("lru_gates"), 1)
            u_tiles("lora", 0, 2, "sv_k")
            pe.wait_ge(*at("sv_k", 4))
            pe.wait_ge(*at("sv_lora", 2))
            u_tiles("v", 0, CT, None)
            pe.wait_ge(*at("ld_lora_up", 48))
            pe.wait_ge(*at("lora_f", 2))
            pe.wait_ge(*at("ga", CT))
            for c in range(CT):
                for h in range(2):
                    x = mm(PS[2 * h + c // 2][:, (c % 2) * T:(c % 2) * T + T], wa_up[64 * h:64 * h + 64, c * P:(c + 1) * P],
                           lora[64 * h:64 * h + 64, 0, :], start=True, stop=True)
            x.then_inc(S("z_a"), 1)
            pe.wait_ge(*at("sv_v", CT))
            for i in range(TT):
                mm(PS[4 + i][:, :], lora[:, 1, i * P:(i + 1) * P], g_up[:], start=True, stop=True).then_inc(S("g_ps"), 1)

            def k_tile(c):
                if c == 0:
                    pe.wait_ge(*at("ld_wk", 16))
                    pe.wait_ge(*at("sv_v", CT))
                if c >= 2:
                    pe.wait_ge(*at("K", c - 1))
                for k in range(KT):
                    x = mm(PS[6 + c % 2][:, 0:T], WB[:, k, c * P:(c + 1) * P], MT[:, k, :], start=(k == 0), stop=(k == KT - 1))
                x.then_inc(S("pe_k"), 1)

            def v_part(q):
                m, h = q // 2, q % 2
                if q == 0:
                    pe.wait_ge(*at("ld_wv", 16))
                    pe.wait_ge(*at("K", KT))
                if q >= 2:
                    pe.wait_ge(*at("V", q - 1))
                for k in range(KT):
                    x = mm(PS[6 + q % 2][:, :], MT[:, k, m * P:(m + 1) * P], WB[:, k, h * 512:(h + 1) * 512],
                           start=(k == 0), stop=(k == KT - 1))
                x.then_inc(S("pe_v"), 1)

            pe.wait_ge(*at("kk_sq", 1))
            pe.wait_ge(*at("sig", CT))
            pe.wait_ge(*at("consts_all", 1))
            for c in range(2):
                mm(PS[c][:, :], head_ones[:], U(1)[:, c * 512:(c + 1) * 512], start=True, stop=True).then_inc(S("kk_ss"), 1)
            for c in range(KT):
                k_tile(c)

            def to_tokens(src, banks):
                for i in range(TT):
                    for c in range(CT):
                        x = tr(PS[banks + i][:, c * P:(c + 1) * P], src[:, c, i * P:(i + 1) * P], ident[:])
                    x.then_inc(S("tok_ps"), 1)

            pe.wait_ge(*at("kk_rn", 2))
            pe.wait_ge(*at("a_c", CT))
            to_tokens(v_c, 0)
            pe.wait_ge(*at("al_c", 1))
            to_tokens(AR[:, 0], 2)
            pe.wait_ge(*at("bh_c", 1))
            pe.wait_ge(*at("g_t", 2))
            to_tokens(bh_c, 4)
            pe.wait_ge(*at("kh_c", 1))
            pe.wait_ge(*at("tok", 2))
            to_tokens(kh_c, 0)
            v_part(0)
            pe.wait_ge(*at("rkk", CT))
            pe.wait_ge(*at("tok", 4))
            for i in range(TT):
                for c in range(CT):
                    x = mm(PS[2][:, i * NH + 2 * c:i * NH + 2 * c + 2], rkk[:, c, i * P:(i + 1) * P],
                           head_ones[:, 0:P:64], start=True, stop=True)
            x.then_inc(S("bonus_ps"), 1)
            for q in range(4):
                kind, i = q // 2, q % 2
                src = (bt_c, kt_c)[kind]
                if q == 0:
                    pe.wait_ge(*at("bonus", 1))
                    pe.wait_ge(*at("r_til", 1))
                if q == 1:
                    pe.wait_ge(*at("tok_v", 2))
                if q >= 2:
                    pe.wait_ge(*at("st", 2 * q - 2))
                for np_ in range(2):
                    t0 = (2 * i + np_) * CH
                    for c in range(CT):
                        for hp in range(2):
                            h = slice(64 * hp, 64 * hp + 64)
                            x = mm(PS[2 + 2 * (q % 2) + hp][64 * np_:64 * np_ + 64, c * 128:(c + 1) * 128].rearrange("p (w k) -> p w k", w=2),
                                   src[h, c, t0:t0 + CH], AR[h, :, c, t0:t0 + CH], start=True, stop=True)
                            if np_ == 1 and c == CT - 1:
                                x.then_inc(S("st_ps"), 1)
            pe.wait_ge(*at("tok_v", 4))
            for i in range(TT):
                if i == 1:
                    pe.wait_ge(*at("st", 6))
                for np_ in range(2):
                    t0 = (2 * i + np_) * CH
                    for c in range(CT):
                        for hp in range(2):
                            h = slice(64 * hp, 64 * hp + 64)
                            x = mm(PS[2 * i + hp][64 * np_:64 * np_ + 64, c * 64:(c + 1) * 64],
                                   AR[h, 0, c, t0:t0 + CH], bt_c[h, c, t0:t0 + CH], start=True, stop=True)
                            if np_ == 1 and c == CT - 1:
                                x.then_inc(S("n_ps"), 1)

            def product(bank, name, *terms):
                for flip in range(2):
                    for h in range(NH):
                        for np_ in range(2):
                            j = np_ ^ flip
                            rows = slice(64 * np_, 64 * np_ + 64)
                            for n, (l, r) in enumerate(terms):
                                x = mm(PS[bank + j][rows, h * 64:(h + 1) * 64], l(rows, np_, j)[:, h], r(rows, np_, j)[:, h],
                                       start=(n == 0), stop=(n == len(terms) - 1))
                x.then_inc(S(name), 1)

            by_j = lambda t: (lambda rows, np_, j: t[rows, j])
            by_i = lambda t: (lambda rows, np_, j: t[rows, j ^ np_])
            part = lambda t, w: (lambda rows, np_, j: t[rows, j ^ np_, :, w])

            pe.wait_ge(*at("st", 8))
            pe.wait_ge(*at("tok", 4))
            product(4, "G_ps", (part(STk, 0), by_i(v_t)))
            pe.wait_ge(*at("n_sb", 4))
            pe.wait_ge(*at("nt_sb", 2))
            product(0, "N2_ps", (by_i(Ntm), by_i(Nm)))
            product(2, "N2t_ps", (by_i(Nm), by_i(Ntm)))
            pe.wait_ge(*at("N2", 2))
            pe.wait_ge(*at("P1", 4))
            pe.wait_ge(*at("G", 2))
            product(4, "P2_ps", (by_j(N2), by_j(P1)))
            pe.wait_ge(*at("N2t", 2))
            product(0, "N4_ps", (by_j(N2t), by_j(N2)))
            product(2, "N4t_ps", (by_j(N2), by_j(N2t)))
            v_part(1)
            pe.wait_ge(*at("N4", 2))
            pe.wait_ge(*at("P2", 2))
            product(4, "P4_ps", (by_j(N4), by_j(P2)))
            pe.wait_ge(*at("N4t", 2))
            product(2, "N8_ps", (by_j(N4t), by_j(N4)))
            v_part(2)
            pe.wait_ge(*at("N8", 2))
            pe.wait_ge(*at("P4", 2))
            product(0, "T16_ps", (by_j(N8), by_j(P4)))
            v_part(3)
            pe.wait_ge(*at("T16", 2))
            product(0, "E_ps", (by_j(T16), by_i(Om)))
            product(2, "Et_ps", (by_i(Om), by_j(T16)))
            product(4, "YW_ps", (by_j(T16), by_i(al_t)))
            pe.wait_ge(*at("E", 2))
            product(0, "YG_ps", (by_j(T16), by_j(G)))
            pe.wait_ge(*at("Et", 2))
            pe.wait_ge(*at("Y1", 2))
            product(4, "E2t_ps", (by_j(E), by_j(Et)))
            pe.wait_ge(*at("E2t", 2))
            pe.wait_ge(*at("Y1g", 2))
            product(0, "Y2w_ps", (by_j(E2t), by_j(Y1[0])))
            product(2, "Y2g_ps", (by_j(E2t), by_j(Y1[1])))
            pe.wait_ge(*at("Y2", 2))
            product(4, "XW_ps", (by_j(Et), by_j(Y2[0])))
            pe.wait_ge(*at("Y2", 4))
            product(0, "XU_ps", (by_j(Et), by_j(Y2[1])))
            pe.wait_ge(*at("XU", 2))
            pe.wait_ge(*at("XW", 2))

            def by_chunk(chunks, bank, name, width, *terms):
                for c in range(CT):
                    for hp in range(2):
                        for k in range(2):
                            for n in chunks:
                                if n // 2 != k:
                                    continue
                                np_, i = n % 2, n // 2
                                j = i ^ np_
                                rows = slice(64 * np_, 64 * np_ + 64)
                                o = PS[bank + np_][64 * hp:64 * hp + 64, (i * width + c) * 64:(i * width + c + 1) * 64]
                                for m, (l, r) in enumerate(terms):
                                    x = mm(o, l(rows, np_, j)[:, 2 * c + hp], r(rows, np_, j)[:, 2 * c + hp],
                                           start=(m == 0), stop=(m == len(terms) - 1))
                x.then_inc(S(name), 1)

            by_chunk((0, 1, 2), 4, "NS_ps", CT, (by_i(bh_t), by_j(XU)), (by_i(kh_t), by_i(v_t)))
            by_chunk((1, 2), 0, "M_ps", 0, (by_j(XW), by_i(bh_t)))
            product(2, "Yuv_ps", (part(STb, 1), by_j(XU)), (part(STk, 1), by_i(v_t)))
            pe.wait_ge(*at("NS", 2))
            by_chunk((1, 2, 3), 4, "Q_ps", CT, (by_j(XW), part(STb, 1)))
            pe.wait_ge(*at("Mt", 2))
            for n in (1, 2):
                if n == 2:
                    pe.wait_ge(*at("St_a", 1))
                    pe.wait_ge(*at("St_v", 1))
                prev = NS[:, 0] if n == 1 else St[:, 0]
                for c in range(CT):
                    for hp in range(2):
                        h = slice(64 * hp, 64 * hp + 64)
                        o = PS[hp][h, c * 64:(c + 1) * 64]
                        mm(o, ident[h, h], NS[h, n, c, :], start=True, stop=False)
                        x = mm(o, Mt[h, n - 1, c, :], prev[h, c, :], start=False, stop=True)
                x.then_inc(S("S_ps"), 1)
            pe.wait_ge(*at("Q", 3))
            pe.wait_ge(*at("St_a", 2))
            pe.wait_ge(*at("St_v", 2))
            for i in range(TT):
                if i == 1:
                    pe.wait_ge(*at("Yuv", 4))
                for c in range(CT):
                    for np_ in range(2):
                        n = 2 * i + np_
                        if n == 0:
                            continue
                        state = NS[:, 0] if n == 1 else St[:, n - 2]
                        for hp in range(2):
                            h = slice(64 * hp, 64 * hp + 64)
                            x = mm(PS[4 - 2 * i + hp][64 * np_:64 * np_ + 64, c * 64:(c + 1) * 64],
                                   Q[h, n, c, :], state[h, c, :], start=True, stop=True)
                x.then_inc(S("Ys_ps"), 1)
            pe.wait_ge(*at("y_rwkv", 1))
            y_tok = R[:, 0, :].rearrange("p (i d) -> p i d", i=TT)
            for q in range(2):
                for c in (2 * q, 2 * q + 1):
                    for i in range(TT):
                        x = tr(PS[q][:, (c % 2) * 256 + i * P:(c % 2) * 256 + i * P + P], y_tok[:, i, c * P:(c + 1) * P], ident[:])
                x.then_inc(S("yT_ps"), 1)

            def project(src, w, name):
                for u in range(4):
                    i, h = u // 2, u % 2
                    for k in range(KT):
                        x = mm(PS[4 + u][:, :], src[:, k, i * P:(i + 1) * P], w[:, k, h * 512:(h + 1) * 512],
                               start=(k == 0), stop=(k == KT - 1))
                    x.then_inc(S(name), 1)

            pe.wait_ge(*at("ld_wo1", 16))
            pe.wait_ge(*at("y_lru", 1))
            pe.wait_ge(*at("yT_a", 1))
            pe.wait_ge(*at("yT_v", 1))
            pe.wait_ge(*at("V", 4))
            project(YT, W2, "pe_wout")
            pe.wait_ge(*at("x1n", 2))
            turn(xm, "t_x1")
            pe.wait_ge(*at("x1T_a", 4))
            pe.wait_ge(*at("x1T_v", 4))
            pe.wait_ge(*at("ld_wq", 16))
            for c in range(KT):
                if c >= 4:
                    pe.wait_ge(*at("q_a" if c % 2 else "q_v", (c - 4) // 2 + 1))
                for k in range(KT):
                    x = mm(PS[4 + c % 4][:, 0:T], W1[:, k, c * P:(c + 1) * P], MT[:, k, :], start=(k == 0), stop=(k == KT - 1))
                x.then_inc(S("pe_q"), 1)
            pe.wait_ge(*at("q_a", 4))
            pe.wait_ge(*at("q_v", 4))
            for u in range(2 * XH):
                h, i = u // 2, u % 2
                if u >= 4:
                    pe.wait_ge(*at("expd", u - 3))
                for k in range(2):
                    x = mm(PS[u % 4][:, 0:T], YT[:, 2 * h + k, i * P:(i + 1) * P], HT[:, 2 * h + k, :], start=(k == 0), stop=(k == 1))
                x.then_inc(S("sc_ps"), 1)

            def turn_prob(h):
                pe.wait_ge(*at("prob", 2 * h + 2))
                if h >= 2:
                    pe.wait_ge(*at("pT_a", h - 1))
                    pe.wait_ge(*at("pT_v", h - 1))
                for m in range(2):
                    for i in range(TT):
                        x = tr(PS[4 + 2 * (h % 2) + m][:, i * P:(i + 1) * P], prob(2 * h + i)[:, m * P:(m + 1) * P], ident[:])
                x.then_inc(S("pT_ps"), 1)

            def head_out(h):
                pe.wait_ge(*at("pT_a", h + 1))
                pe.wait_ge(*at("pT_v", h + 1))
                if h == 0:
                    pe.wait_ge(*at("expd", 2 * XH))
                if h >= 2:
                    pe.wait_ge(*at("oT_a", h - 1))
                    pe.wait_ge(*at("oT_v", h - 1))
                for d in range(2):
                    for m in range(2):
                        x = mm(PS[2 * (h % 2) + d][:, 0:T], V[:, m, (2 * h + d) * P:(2 * h + d + 1) * P], prob_t(h)[:, m],
                               start=(m == 0), stop=(m == 1))
                    x.then_inc(S("o_ps"), 1)

            turn_prob(0)
            turn_prob(1)
            head_out(0)
            head_out(1)
            turn_prob(2)
            turn_prob(3)
            head_out(2)
            head_out(3)
            pe.wait_ge(*at("oT_a", 4))
            pe.wait_ge(*at("oT_v", 4))
            pe.wait_ge(*at("ld_wo2", 16))
            project(YT, WB, "pe_wo")
            pe.wait_ge(*at("x2n", 2))
            turn(x3n, "t_x2")
            pe.wait_ge(*at("x2T_a", 4))
            pe.wait_ge(*at("x2T_v", 4))
            pe.wait_ge(*at("ld_late", 64))
            for i in range(TT):
                for k in range(KT):
                    x = mm(PS[4 + i][:, 0:NE], MT[:, k, i * P:(i + 1) * P], w_rt[:, k, :], start=(k == 0), stop=(k == KT - 1))
                x.then_inc(S("rl_ps"), 1)
            pe.wait_ge(*at("picked", 2))
            m0, m1 = rt[:, 5, 0, :], rt[:, 5, 1, :]
            mm(PS[6][:, 0:NE], before[:], m0, start=True, stop=True).then_inc(S("rank_ps"), 1)
            mm(PS[6][:, NE:2 * NE], ones[:], m0, start=True, stop=False)
            mm(PS[6][:, NE:2 * NE], before[:], m1, start=False, stop=True).then_inc(S("rank_ps"), 1)
            mm(PS[6][:, 2 * NE:3 * NE], ones[:], m0, start=True, stop=False)
            mm(PS[6][:, 2 * NE:3 * NE], ones[:], m1, start=False, stop=True).then_inc(S("rank_ps"), 1)
            pe.wait_ge(*at("gate", 2))
            for i in range(TT):
                tr(PS[7][0:NE, i * P:(i + 1) * P], gate[:, i, :], ident[:]).then_inc(S("gt_ps"), 1)
            pe.wait_ge(*at("gate_t", 1))
            pe.wait_ge(*at("ld_bdn", 16))
            for u in range(4):
                mm(PS[u][:, :], gate_t[:, (u // 2) * P:(u // 2) * P + P], bdn[:, (u % 2) * 512:(u % 2) * 512 + 512],
                   start=True, stop=True).then_inc(S("bias_out"), 1)
            pe.wait_ge(*at("steps", 1))
            total = pe.value_load(steps_i[0:1, 0:1], min_val=NE, max_val=NE * ROUNDS)
            pe.sem_inc(S("turned"), 1)

            def gather(n):
                pe.wait_ge(S("self_sb"), TT * (n + 1))
                for c in range(KT):
                    for t in range(TT):
                        x = mm(PS[7][:, c * SLOTS:(c + 1) * SLOTS], x3n[:, t, c * P:(c + 1) * P], self_[:, t, :],
                               start=(t == 0), stop=(t == TT - 1))
                x.then_inc(S("gathered"), 1)

            def scatter(n):
                pe.wait_ge(S("y_sb"), n + 1)
                pe.wait_ge(S("sel_t"), n + 1)
                for t in range(TT):
                    for g in range(2):
                        h = slice(64 * g, 64 * g + 64)
                        x = mm(PS[2 * t + g][:, :], sel_t[h, t, :], y_e[h, :], start=False, stop=True,
                               skip_group_check=True)
                x.then_inc(S("scattered"), 1)

            gather(0)
            with pe.Fori(0, total) as i:
                pe.wait_ge(S("ld_bgu"), 16 * (i + 1))
                pe.wait_ge(S("act_sb"), i + 1)
                for w in range(2):
                    for g in range(2):
                        x = mm(PS[4 + w][64 * g:64 * g + 64, :], ones[0:1, 0:SLOTS], bgu[:, w, g, :], start=True, stop=False)
                x.then_inc(S("used_b"), 1)
                pe.wait_ge(S("xg"), i + 1)
                for q in range(4):
                    pe.wait_ge(S(f"ld_gu{q}"), 16 * (i + 1))
                    for c in range(2):
                        for w in range(2):
                            for g in range(2):
                                x = mm(PS[4 + w][64 * g:64 * g + 64, :], xg[:, 2 * q + c, :], gu[q][:, c, w, g, :],
                                       start=False, stop=(q == 3 and c == 1))
                    x.then_inc(S(f"used_gu{q}"), 1)
                scatter(i)
                pe.wait_ge(S("sel_sb"), TT * (i + 1))
                for t in range(TT):
                    x = tr(PS[6][:, t * P:(t + 1) * P], sel[:, t].rearrange("p w s -> p (w s)"), ident[:])
                x.then_inc(S("turned"), 1)
                gather(i + 1)
                pe.wait_ge(S("act_sb"), i + 2)
                pe.wait_ge(S("sel_t"), i + 2)
                for f in range(4):
                    x = tr(PS[6][:, f * P:(f + 1) * P], m_a[:, f * P:(f + 1) * P], ident[:])
                x.then_inc(S("act_ps"), 1)
                pe.wait_ge(S("act_t"), i + 1)
                for q in range(2):
                    pe.wait_ge(S(f"ld_dn{q}"), 16 * (i + 1))
                    for c in range(4):
                        for g in range(2):
                            x = mm(PS[6][64 * g:64 * g + 64, :], act_t[:, c, 64 * q:64 * q + 64], dn[q][:, c, g, :],
                                   start=(q == 0 and c == 0), stop=(q == 1 and c == 3))
                    x.then_inc(S(f"used_dn{q}"), 1)
            scatter(total)


_NAMES = ['x', 'mem', 'norm_mix_g', 'w_in', 'conv_w', 'conv_b', 'lru_wx', 'lru_bx', 'lru_wa', 'lru_ba',
          'lru_lambda', 'rwkv_mu', 'rwkv_w0', 'rwkv_w_up', 'rwkv_a0', 'rwkv_a_up', 'rwkv_g_up', 'rwkv_k_k',
          'rwkv_k_a', 'rwkv_r_k', 'rwkv_lnx_g', 'rwkv_lnx_b', 'w_out', 'norm_xa_g', 'norm_mem_g', 'xa_wq',
          'xa_wk', 'xa_wv', 'xa_wo', 'norm_ffn_g', 'w_router', 'b_router', 'w_gu', 'b_gu', 'w_dn', 'b_dn',
          'final_norm_g']


def kernel(**inputs):
    import numpy as _np
    import concourse.bacc as _bacc
    from concourse import mybir as _mybir
    from concourse.bass_utils import run_bass_kernel_spmd as _run

    nc = _bacc.Bacc("TRN2", target_bir_lowering=False, num_devices=1)
    arrays, aps = {}, {}
    for name in _NAMES:
        arr = _np.ascontiguousarray(inputs[name])
        arrays[f"in_{name}"] = arr
        aps[name] = nc.dram_tensor(f"in_{name}", arr.shape, _mybir.dt.from_np(arr.dtype), kind="ExternalInput").ap()
    out = nc.dram_tensor("out", (1, T, D), _mybir.dt.float32, kind="ExternalOutput").ap()
    build(nc, aps, out)
    r = _run(nc, [arrays], core_ids=[0])
    return r.results[0]["out"]
```

```python
from contextlib import ExitStack

import numpy as np

import concourse.bass as bass
from concourse import mybir

ALU = mybir.AluOpType
ACT = mybir.ActivationFunctionType
F32 = mybir.dt.float32
I32 = mybir.dt.int32
AX_X = mybir.AxisListType.X

P = 128
T, D = 256, 1024
TT = T // P
KT = D // P
LRU_W = RW = 512
CT = RW // P
IN_W = 2816
HEAD = 64
NH = RW // HEAD
CH = 64
NCH = T // CH
BL = 16
ST_BANKS = (0, 2, 4, 0)
X_BANKS = (4, 0, 4, 0)
XH, XD = 4, 256
NE = 32
SLOTS = 64
ROUNDS = T // SLOTS
EPS, GN_EPS = 1e-6, 64e-5
ROOT_D, ROOT_HEAD = float(np.sqrt(D)), float(np.sqrt(HEAD))
DECAY = float(np.exp(-0.5))
LIMIT, ALPHA = 7.0, 1.702
UNIT = 1024
CHUNK = 4096
PER_EXPERT = 6
RING = 8
GROUP = 4
TURNS = GROUP * PER_EXPERT // RING

PARAM_ROWS = [("norm_mix_g", KT), ("norm_mem_g", KT), ("norm_xa_g", KT), ("norm_ffn_g", KT),
              ("conv_w", 4 * CT), ("conv_b", CT), ("lru_bx", CT), ("lru_ba", CT), ("lru_lambda", CT),
              ("rwkv_mu", 14), ("rwkv_w0", CT), ("rwkv_a0", CT), ("rwkv_k_k", CT), ("rwkv_k_a", CT),
              ("rwkv_r_k", CT)]
PAR_SPLIT = 6
COL, NPAR = {}, 0
for _name, _rows in PARAM_ROWS:
    COL[_name] = NPAR
    NPAR += _rows


SHARED = {}
for _sem, _steps in (
    ("early_pe", [("par_ps", 1), ("t_x", 4), ("u_xl", 4), ("u_gl", 4), ("u_r", 4), ("t_mem", 4), ("u_k", 4),
                  ("lru_gates", 4), ("u_lora", 2), ("u_v", 4), ("z_a", 1), ("g_ps", 2)]),
    ("early_dve", [("xl_pads", 1), ("xn", 2), ("par", 1), ("hT_v", 4), ("omu", 1), ("lam_abs", 1), ("lam_w", 1),
                   ("lam_rate", 2), ("conv", 16), ("memn", 2), ("mT_v", 4)]),
    ("early_act", [("ss_x", 2), ("hT_a", 4), ("lam_e", 1), ("lam_ln", 1), ("xl", 4), ("ss_mem", 2),
                   ("gelu", 4), ("sa_r", 4), ("mT_a", 4), ("sa_k", 4)]),
    ("router_pe", [("rl_ps", 2), ("rank_ps", 3), ("gt_ps", 4)]),
    ("router_dve", [("banks_cleared", 4), ("gate", 2), ("key", 1), ("steps_v", 1)]),
    ("rwkv_pe", [("kk_ss", 2), ("n_ps", 4), ("tok_v_ps", 2), ("tok_al_ps", 2), ("tok_bh_ps", 2), ("tok_kh_ps", 2),
                 ("st_ps", 8), ("bonus_ps", 1), ("G_ps", 1), ("Et_ps", 4), ("X0_ps", 4), ("X1_ps", 4), ("X2_ps", 4),
                 ("X3_ps", 4), ("NS_ps", 1), ("M_ps", 1), ("Yuv_ps", 1), ("Q_ps", 1), ("S_ps", 2),
                 ("Ys_ps", 2), ("yT_ps", 2)]),
    ("rwkv_dve", [("al_c", 1), ("bt_c", 1), ("kt_c", 1), ("bh_c", 1), ("kh_c", 1), ("r_til", 1), ("N_flat", 1),
                  ("O", 8), ("rkk", 4), ("tok_v", 4), ("st", 8), ("bonus", 1)]),
    ("solve_dve", [("T_flat", 1), ("DI", 2), ("T16", 2), ("X0", 4), ("X1", 4), ("X2", 4), ("X3", 4), ("NS", 2),
                   ("Mt", 2), ("Q", 3), ("St_v", 2), ("Y", 4)]),
    ("solve_act", [("tok", 4), ("G", 4), ("Et", 4), ("Yuv", 4), ("St_a", 2)]),
):
    _at = 0
    for _name, _n in _steps:
        SHARED[_name] = (_sem, _at)
        _at += _n


def build(nc, a, out):
    with ExitStack() as ctx:
        def sb(name, shape, dt=F32):
            return ctx.enter_context(nc.sbuf_tensor(name, shape, dt))

        sems = {}

        def S(name):
            name = SHARED.get(name, (name, 0))[0]
            if name not in sems:
                sems[name] = ctx.enter_context(nc.semaphore(name))
            return sems[name]

        def at(name, n):
            return S(name), SHARED[name][1] + n if name in SHARED else n

        AB = sb("AB", [P, RING * CHUNK])
        A = AB[:, 0:24576]
        B = AB[:, 24576:32768]
        X = sb("X", [P, TT, D])
        HT = sb("HT", [P, KT, T])
        MT = sb("MT", [P, KT, T])
        VX = sb("VX", [P, 2048])
        YT = sb("YT", [P, KT, T])
        R = sb("R", [P, 2, UNIT])
        par_rows = sb("par_rows", [P, P])
        par = sb("par", [P, P])
        omu = sb("omu", [P, 14])
        ident = sb("ident", [P, P])
        ones = sb("ones", [P, P])
        neg_half = sb("neg_half", [P, TT * NH])
        before = sb("before", [P, P])
        head_ones = sb("head_ones", [P, P])
        M = sb("M", [P, 2560])
        m8 = [M[:, i * 512:(i + 1) * 512].rearrange("p (e k) -> p e k", e=8) for i in range(5)]
        eye8, mask_n, mask_o = m8[:3]
        eye16 = M[:, 1536:1792].rearrange("p (s t) -> p s t", s=BL)
        own_block = M[:, 1792:1796]
        mask_ar = M[:, 2048:2560].rearrange("p (c w k) -> p c w k", c=4, w=2)
        restart = sb("restart", [P, T])
        slot_no = sb("slot_no", [P, 2, SLOTS])
        w_bd = sb("w_bd", [P, 2 * CT * P])
        wx_bd, wa_bd = (w_bd[:, i * 512:(i + 1) * 512].rearrange("p (c j) -> p c j", c=CT) for i in range(2))
        ups = sb("ups", [P, 2 * RW])
        wa_up = ups[:, 0:RW]
        g_up = ups[:, RW:2 * RW]
        lnx = sb("lnx", [P, 2, RW])
        w_rt = sb("w_rt", [P, KT, NE])
        b_rt = sb("b_rt", [P, NE])
        st = sb("st", [P, 32])
        lam = sb("lam", [P, 8, CT])
        dc = sb("dc", [P, CT, NCH])
        gst = sb("gst", [P, 8, TT, NH])
        ast = sb("ast", [P, 4, 2 * XH])
        rt = M[:, 1024:1664].rearrange("p (w i e) -> p w i e", w=10, i=TT)
        top = sb("top", [P, TT, 8])
        key, gate = (M[:, 1664 + i * 64:1728 + i * 64].rearrange("p (i e) -> p i e", i=TT) for i in range(2))

        cnt = sb("cnt", [P, 8])
        steps_i = sb("steps_i", [P, 1], I32)
        PS = [ctx.enter_context(nc.psum_tensor(f"PS{i}", [P, 512], F32)) for i in range(8)]

        def U(i, n=1):
            return A[:, i * UNIT:(i + n) * UNIT]

        def chan(ap):
            return ap.rearrange("p (c t) -> p c t", c=CT)

        def heads(ap):
            return ap.rearrange("p (j h k) -> p j h k", j=2, h=NH)

        def col(name, c=0):
            return par[:, COL[name] + c:COL[name] + c + 1]

        w_in_q = [A[:, q * 4096:(q + 1) * 4096].rearrange("p (c n) -> p c n", c=KT) for q in range(5)]
        w_lora = A[:, 5 * 4096:5 * 4096 + 2048].rearrange("p (c n) -> p c n", c=KT)
        W2 = A[:, 16384:24576].rearrange("p (c n) -> p c n", c=KT)
        W1 = A[:, 8192:16384].rearrange("p (c n) -> p c n", c=KT)
        WB = B[:, :].rearrange("p (c n) -> p c n", c=KT)
        WV = {"xl": (w_in_q[0], 0), "gl": (w_in_q[1], 512), "r": (w_in_q[2], 1024),
              "k": (w_in_q[3], 1536), "v": (w_in_q[4], 2048), "lora": (w_lora, 2560)}
        xl_pad = VX[:, 0:CT * 260].rearrange("p (c t) -> p c t", c=CT)
        mem = R
        lora = R[:, 0, 0:512].rearrange("p (c t) -> p c t", c=2)
        V = VX[:, :].rearrange("p (m d) -> p m d", m=2)

        xc, gx, ga, th = chan(U(0)), chan(U(1)), chan(U(2)), chan(U(3))
        dec = chan(U(4))
        r_c, k_c, v_c = chan(U(5)), chan(U(6)), chan(U(7))
        sig, a_c, Z = chan(U(8)), chan(U(9)), chan(U(10))
        Dt, inv_d, d_prev, kk, zp = chan(U(11)), chan(U(12)), chan(U(13)), chan(U(14)), chan(U(15))
        sq, beta = chan(U(1)), chan(U(2))
        AR = U(3, 2).rearrange("p (w c t) -> p w c t", w=2, c=CT)
        bt_c, kt_c = chan(U(8)), chan(U(15))
        bh_c, kh_c = chan(U(0)), chan(U(1))
        rkk = chan(U(2))
        v_t, bh_t, kh_t = heads(U(10)), heads(U(13)), heads(U(14))
        STb = U(5, 2).rearrange("p (j h w k) -> p j h w k", j=2, h=NH, w=2)
        STk = U(11, 2).rearrange("p (j h w k) -> p j h w k", j=2, h=NH, w=2)
        Nm = heads(U(22))
        N_flat, N_own, T_own, T_tmp, T_flat = (R[:, 1, 0:256], R[:, 0, 0:256], R[:, 0, 256:512], R[:, 0, 512:768],
                                               R[:, 0, 768:1024])

        def pairs(ap):
            return ap.rearrange("p (i h k) -> p i h k", i=TT, h=NH)

        RG, O_bd, T16, Et = pairs(U(16, 2)), pairs(U(18, 2)), pairs(U(20, 2)), pairs(U(22, 2))
        Xs = [pairs(U(0, 2)), pairs(U(7, 2)), pairs(U(16, 2)), pairs(U(7, 2))]
        XW, XU = Xs[3][:, :, :, 0:64], Xs[3][:, :, :, 64:128]
        DI = U(9)[:, 0:512].rearrange("p (n c k) -> p n c k", n=2, c=CT)
        Mt = U(9)[:, 512:1024].rearrange("p (n c k) -> p n c k", n=2, c=CT)
        NS = U(0)[:, 0:768].rearrange("p (n c k) -> p n c k", n=3, c=CT)
        Q = U(1).rearrange("p (n c k) -> p n c k", n=NCH, c=CT)
        St = U(15)[:, 0:512].rearrange("p (n c k) -> p n c k", n=2, c=CT)
        Yuv = heads(U(2))
        Y, Ysq = heads(R[:, 0, :]), heads(R[:, 1, :])
        y_add = heads(U(3))
        g_t = heads(w_bd[:, :])
        A_prob = R[:, :, :].rearrange("p a (b t) -> p (a b) t", b=4)
        A_probt = M[:, 0:1024].rearrange("p (h m t) -> p h m t", h=2, m=2)
        xn = B[:, 0:2048].rearrange("p (i d) -> p i d", i=TT)
        xm = R

        def prob(u):
            return A_prob[:, u, :]

        def prob_t(h):
            return A_probt[:, h % 2]

        ring = [AB[:, s * CHUNK:(s + 1) * CHUNK] for s in range(RING)]
        as_gu = lambda ap: ap.rearrange("p (c w g n) -> p c w g n", c=2, w=2, g=2)
        as_dn = lambda ap: ap.rearrange("p (c g n) -> p c g n", c=4, g=2)
        bgu = MT[0:1, :, :].rearrange("p c t -> p (c t)").rearrange("p (w g n) -> p w g n", w=2, g=2)

        fin_g = lnx[:, :, :].rearrange("p w k -> p (w k)")
        x3n = HT[:, :, :].rearrange("p c t -> p (c t)").rearrange("p (i d) -> p i d", i=TT)
        x3t = MT
        yt_f = YT[:, :, :].rearrange("p c t -> p (c t)")
        sel = yt_f[:, 0:256].rearrange("p (i w s) -> p i w s", i=TT, w=2)
        self_ = yt_f[:, 256:384].rearrange("p (i s) -> p i s", i=TT)
        sel_t = yt_f[:, 512:768].rearrange("p (i t) -> p i t", i=TT)
        xg = yt_f[:, 1024:1536].rearrange("p (c s) -> p c s", c=KT)
        act_t = yt_f[:, 1536:2048].rearrange("p (f m) -> p f m", f=4)
        vx_f = VX[:, :]
        m_g, m_s, m_u, m_a = (vx_f[:, i * 512:(i + 1) * 512] for i in range(4))
        y_e = R[:, 0, 0:512]
        picked_rows = R[:, 0, 512:1024]
        fin = R[:, :, :]

        dram = {k: (v[0] if k not in ("x", "mem", "final_norm_g") else v) for k, v in a.items()}
        krows = lambda w: w.rearrange("(c p) n -> p c n", p=P)
        par_loads = []
        for name, rows in PARAM_ROWS:
            src = dram[name] if len(dram[name].shape) == 1 else dram[name].rearrange("a b -> (a b)")
            par_loads.append((COL[name], rows, src.rearrange("(r p) -> r p", p=P)))

        scratch = nc.dram_tensor("scratch", (2, P, 2 * P), F32, kind="Internal").ap()
        block = ctx.enter_context(nc.Block())

        @block.sync
        def _(sp):
            for i in range(TT):
                sp.dma_start(X[:, i, :], dram["x"][0, i * P:(i + 1) * P, :]).then_inc(S(f"ld_x{i}"), 16)

            def load_in(name):
                w, at = WV[name]
                n = w.shape[2]
                sp.dma_start(w, krows(dram["w_in"][:, at:at + n])).then_inc(S("ld_" + name), 16)

            for r0, rows, src in par_loads[PAR_SPLIT:]:
                sp.dma_start(par_rows[r0:r0 + rows, :], src).then_inc(S("ld_par"), 16)
            load_in("xl")
            load_in("gl")
            sp.dma_start(mem[:], dram["mem"][0].rearrange("(i p) d -> p i d", p=P)).then_inc(S("ld_mem"), 16)
            for name in ("r", "k", "lora", "v"):
                load_in(name)
            sp.dma_start(wa_up[0:64, :], dram["rwkv_w_up"]).then_inc(S("ld_lora_up"), 16)
            sp.dma_start(wa_up[64:128, :], dram["rwkv_a_up"]).then_inc(S("ld_lora_up"), 16)
            sp.dma_start(g_up[:], dram["rwkv_g_up"]).then_inc(S("ld_lora_up"), 16)
            sp.dma_start(lnx[:, 0, :], dram["rwkv_lnx_g"].partition_broadcast(P)).then_inc(S("ld_late"), 16)
            sp.dma_start(lnx[:, 1, :], dram["rwkv_lnx_b"].partition_broadcast(P)).then_inc(S("ld_late"), 16)
            sp.dma_start(b_rt[:], dram["b_router"].partition_broadcast(P)).then_inc(S("ld_late"), 16)
            sp.dma_start(w_rt[:], krows(dram["w_router"])).then_inc(S("ld_late"), 16)
            sp.wait_ge(*at("t_x", 4))
            sp.dma_start(WB, krows(dram["xa_wk"])).then_inc(S("ld_wk"), 16)
            sp.wait_ge(*at("pe_k", KT))
            sp.dma_start(WB, krows(dram["xa_wv"])).then_inc(S("ld_wv"), 16)
            blocks = [slice(BL * g, BL * g + BL) for g in range(P // BL)]
            sp.wait_ge(*at("N_flat", 1))
            sp.dma_start(scratch[0], N_flat).then_inc(S("st_N"), 16)
            sp.wait_ge(*at("st_N", 16))
            for g in blocks:
                sp.dma_start(N_own[g].rearrange("x (t s) -> x t s", t=BL),
                             scratch[0, g].rearrange("t (x s) -> x t s", x=BL)).then_inc(S("ld_N"), 16)
            sp.wait_ge(*at("T_flat", 1))
            sp.dma_start(scratch[1], T_own).then_inc(S("st_T"), 16)
            sp.wait_ge(*at("st_T", 16))
            for g in blocks:
                sp.dma_start(T_flat[g].rearrange("s (x t) -> s x t", x=BL),
                             scratch[1, g].rearrange("x (s t) -> s x t", s=BL)).then_inc(S("ld_T"), 16)
            sp.wait_ge(*at("X3_ps", 4))
            sp.dma_start(W2, krows(dram["w_out"])).then_inc(S("ld_wo1"), 16)
            sp.wait_ge(*at("yT_ps", 2))
            sp.dma_start(W1, krows(dram["xa_wq"])).then_inc(S("ld_wq"), 16)
            sp.wait_ge(*at("pe_v", 4))
            sp.dma_start(WB, krows(dram["xa_wo"])).then_inc(S("ld_wo2"), 16)

            sp.dma_start(fin_g, a["final_norm_g"].partition_broadcast(P)).then_inc(S("ld_fing"), 16)

            def load_chunk(e, m):
                q = m % PER_EXPERT
                if q < 4:
                    src, n = dram["w_gu"][bass.ds(e, 1), q * 256:(q + 1) * 256, :], 2
                else:
                    src, n = dram["w_dn"][bass.ds(e, 1), (q - 4) * 512:(q - 3) * 512, :], 4
                sp.dma_start(ring[m % RING].rearrange("p (c n) -> p c n", c=n),
                             src[0].rearrange("(c p) n -> p c n", p=P)).then_inc(S(f"ld_ring{m % RING}"), 16)

            def load_bgu(e):
                sp.dma_start(bgu, dram["b_gu"][bass.ds(e, 1), :].rearrange("p (w g n) -> p w g n", w=2, g=2)).then_inc(S("ld_bgu"), 16)

            for m in (0, 1):
                load_chunk(0, m)
            sp.wait_ge(*at("pe_wout", 4))
            for m in (4, 5):
                load_chunk(0, m)
            sp.wait_ge(*at("pe_q", KT))
            for m in (2, 3):
                load_chunk(0, m)
            sp.wait_ge(*at("pe_wo", 4))
            for m in (6, 7):
                load_chunk(m // PER_EXPERT, m)
            sp.wait_ge(*at("y_cleared", 1))
            for g in range(2):
                sp.dma_start(y_e[64 * g:64 * g + NE, :], dram["b_dn"][:, g * 512:(g + 1) * 512]).then_inc(S("ld_bdn"), 16)
            sp.wait_ge(*at("rl_ps", 2))
            load_bgu(0)

            def load_group(i, first):
                for m in range(first, GROUP * PER_EXPERT):
                    e = (i % (NE // GROUP)) * GROUP + m // PER_EXPERT
                    sp.wait_ge(S("used_ring"), i * (GROUP * PER_EXPERT) + (m - RING + 1))
                    load_chunk(e, m)
                    if m % PER_EXPERT == (1 if first == 0 or m >= 2 * PER_EXPERT else 2):
                        sp.wait_ge(S("used_b"), i * GROUP + m // PER_EXPERT)
                        load_bgu(e)

            load_group(0, RING)
            with sp.Fori(1, NE // GROUP) as i:
                load_group(i, 0)
            sp.wait_ge(*at("steps", 1))
            groups = sp.value_load(steps_i[0:1, 0:1], min_val=NE // GROUP, max_val=NE * ROUNDS // GROUP)
            with sp.If(groups > NE // GROUP):
                with sp.Fori(NE // GROUP, groups) as i:
                    load_group(i, 0)
            for i in range(TT):
                sp.wait_ge(*at("y_out", i + 1))
                sp.dma_start(out[0, i * P:(i + 1) * P, :], fin[:, i, :]).then_inc(S("stored"), 16)
            sp.wait_ge(*at("stored", 16 * TT))

        @block.gpsimd
        def _(pool):
            pg = nc.gpsimd
            n = [0]

            def c(ins):
                n[0] += 1
                ins.then_inc(S("consts"), 1)
                pool.wait_ge(*at("consts", n[0]))

            c(pg.memset(neg_half[:], -0.5))
            c(pg.memset(ident[:], 0.0))
            c(pg.affine_select(out=ident[:], in_=ident[:], compare_op=ALU.not_equal, fill=1.0, base=0,
                               pattern=[[-1, P]], channel_multiplier=1))
            pool.sem_inc(S("ident"), 1)

            def inv_root(dst, ss, shift, name, half):
                c(pg.tensor_scalar(dst, ss, shift, None, ALU.add))
                pg.tensor_tensor(dst, dst, half, ALU.pow).then_inc(S(name), 1)

            for i in range(TT):
                pool.wait_ge(*at("ss_x", i + 1))
                inv_root(st[:, 2 + i:3 + i], st[:, i:i + 1], D * EPS, "rs_x", neg_half[:, 0:1])
            for w in (wx_bd, wa_bd):
                pg.memset(w, 0.0).then_inc(S("bd_zero"), 1)
            pool.wait_ge(*at("bd_zero", 2))
            for name, w in (("lru_wx", wx_bd), ("lru_wa", wa_bd)):
                for half in range(2):
                    src = dram[name].rearrange("(c w) i j -> w i c j", w=2)[half]
                    pool.dma_start(w[64 * half:64 * half + 64, :, 64 * half:64 * half + 64], src).then_inc(S("ld_lruw"), 16)
            c(pg.memset(ones[:], 1.0))
            c(pg.memset(before[:], 1.0))
            c(pg.affine_select(out=before[:], in_=before[:], compare_op=ALU.is_gt, fill=0.0, base=0,
                               pattern=[[1, P]], channel_multiplier=-1))
            c(pg.memset(head_ones[:], 0.0))
            for h in range(2):
                c(pg.memset(head_ones[64 * h:64 * h + 64, 64 * h:64 * h + 64], 1.0))
            c(pg.memset(restart[:], 1.0))
            c(pg.memset(restart[:].rearrange("p (n t) -> p n t", t=CH)[:, :, 0:1], 0.0))
            c(pg.memset(eye8, 0.0))
            for h in range(2):
                s = slice(64 * h, 64 * h + 64)
                c(pg.affine_select(out=eye8[s], in_=eye8[s], compare_op=ALU.not_equal, fill=1.0, base=0,
                                   pattern=[[0, 8], [-1, 64]], channel_multiplier=1))
            for m in (mask_ar, mask_n, mask_o, own_block):
                c(pg.memset(m, 1.0))
            c(pg.memset(eye16, 0.0))
            c(pg.affine_select(out=eye16, in_=eye16, compare_op=ALU.not_equal, fill=1.0, base=0,
                               pattern=[[1, BL], [-1, BL]], channel_multiplier=0))
            for h in range(2):
                s = slice(64 * h, 64 * h + 64)
                for w, op in ((0, ALU.is_gt), (1, ALU.is_ge)):
                    v = mask_ar[s, :, w, :]
                    c(pg.affine_select(out=v, in_=v, compare_op=op, fill=0.0, base=0,
                                       pattern=[[0, 4], [1, 64]], channel_multiplier=-1))
                v = mask_o[s].rearrange("p e (b j) -> p e b j", j=16)
                c(pg.affine_select(out=v, in_=v, compare_op=ALU.is_ge, fill=0.0, base=-16,
                                   pattern=[[0, 8], [-16, 4], [0, 16]], channel_multiplier=1))
                v = mask_n[s].rearrange("p e (b j) -> p e b j", j=16)
                c(pg.affine_select(out=v, in_=v, compare_op=ALU.is_gt, fill=0.0, base=16,
                                   pattern=[[0, 8], [16, 4], [0, 16]], channel_multiplier=-1))
                c(pg.affine_select(out=mask_n[s], in_=mask_n[s], compare_op=ALU.is_gt, fill=0.0, base=0,
                                   pattern=[[0, 8], [-1, 64]], channel_multiplier=1))
                c(pg.affine_select(out=own_block[s], in_=own_block[s], compare_op=ALU.is_ge, fill=0.0, base=0,
                                   pattern=[[-BL, CH // BL]], channel_multiplier=1))
                c(pg.affine_select(out=own_block[s], in_=own_block[s], compare_op=ALU.is_gt, fill=0.0, base=BL,
                                   pattern=[[BL, CH // BL]], channel_multiplier=-1))
            c(pg.iota(slot_no[:], pattern=[[0, 2], [1, SLOTS]], base=0, channel_multiplier=0,
                      allow_small_or_imprecise_dtypes=True))
            pool.sem_inc(S("consts_all"), 1)
            pool.wait_ge(*at("ss_mem", 2))
            inv_root(st[:, 6:8], st[:, 4:6], D * EPS, "rs_mem", neg_half[:, 0:2])
            pool.wait_ge(*at("u_v", CT))
            pg.memset(U(18, 4), 0.0).then_inc(S("bd_cleared"), 1)
            pool.wait_ge(*at("gn_ss", 1))
            inv_root(gst[:, 4], gst[:, 2], HEAD * GN_EPS, "gn_rs", neg_half[:, :].rearrange("p (i h) -> p i h", i=TT))
            for r in range(3):
                if r == 1:
                    pool.wait_ge(*at("pT_ps", XH))
                    pg.memset(y_e, 0.0).then_inc(S("y_cleared"), 1)
                for i in range(TT):
                    pool.wait_ge(S(f"ss_x{r + 1}"), i + 1)
                    inv_root(st[:, 10 + 4 * r + i:11 + 4 * r + i], st[:, 8 + 4 * r + i:9 + 4 * r + i], D * EPS, f"rs_x{r + 1}", neg_half[:, 0:1])

        @block.scalar
        def _(act):
            ac = nc.scalar
            made = {}

            def done(ins, name):
                sem = S(name)
                made[sem.name] = made.get(sem.name, 0) + 1
                ins.then_inc(sem, 1)
                act.wait_ge(sem, made[sem.name])

            for r0, rows, src in par_loads[:PAR_SPLIT]:
                act.dma_start(par_rows[r0:r0 + rows, :], src).then_inc(S("ld_par"), 16)

            def k_copy(lo, hi):
                for c in range(lo, hi):
                    act.wait_ge(*at("pe_k", c + 1))
                    done(ac.copy(HT[:, c, :], PS[6 + c % 2][:, 0:T]), "K")

            def v_copy(lo, hi):
                for q in range(lo, hi):
                    act.wait_ge(*at("pe_v", q + 1))
                    done(ac.copy(V[:, q // 2, (q % 2) * 512:(q % 2) * 512 + 512], PS[6 + q % 2][:, :]), "V")

            for i in range(TT):
                act.wait_ge(*at(f"ld_x{i}", 16))
                done(ac.activation(YT[:, 4 * i:4 * i + 4, :], X[:, i, :].rearrange("p (c t) -> p c t", c=4), ACT.Square,
                                   accum_out=st[:, i:i + 1]), "ss_x")
            act.wait_ge(*at("par", 1))
            act.wait_ge(*at("t_x", 4))
            for c in (4, 5, 6, 7):
                done(ac.activation(HT[:, c, :], PS[c // 2][:, (c % 2) * 256:(c % 2) * 256 + 256], ACT.Identity,
                                   scale=col("norm_mix_g", c)), "hT_a")
            act.wait_ge(*at("lam_abs", 1))
            done(ac.activation(lam[:, 1, :], lam[:, 0, :], ACT.Exp, scale=-1.0), "lam_e")
            act.wait_ge(*at("lam_w", 1))
            done(ac.activation(lam[:, 3, :], lam[:, 2, :], ACT.Ln), "lam_ln")
            act.wait_ge(*at("xl_pads", 1))
            for c in range(CT):
                act.wait_ge(*at("u_xl", c + 1))
                done(ac.copy(xl_pad[:, c, 3:3 + T], PS[4 + c][:, 0:T]), "xl")
            act.wait_ge(*at("ld_mem", 16))
            for i in range(TT):
                done(ac.activation(YT[:, 4 * i:4 * i + 4, :], mem[:, i, :].rearrange("p (c t) -> p c t", c=4), ACT.Square,
                                   accum_out=st[:, 4 + i:5 + i]), "ss_mem")
            for c in range(CT):
                act.wait_ge(*at("u_gl", c + 1))
                done(ac.activation(YT[:, c, :], PS[4 + c][:, 0:T], ACT.Gelu_apprx_tanh), "gelu")

            def shift_a(name, dst, mu0):
                n = 2 if name == "lora" else CT
                for c in range(n):
                    act.wait_ge(*at("u_" + name, c + 1))
                    b = PS[4 + c]
                    done(ac.activation(dst[:, c, :], b[:, 0:T], ACT.Identity, scale=omu[:, mu0 + c:mu0 + c + 1]),
                         "sa_" + name)

            act.wait_ge(*at("omu", 1))
            shift_a("r", r_c, 0)
            act.wait_ge(*at("t_mem", 4))
            for c in (4, 5, 6, 7):
                done(ac.activation(MT[:, c, :], PS[c // 2][:, (c % 2) * 256:(c % 2) * 256 + 256], ACT.Identity,
                                   scale=col("norm_mem_g", c)), "mT_a")
            shift_a("k", k_c, 4)
            for c in range(CT):
                act.wait_ge(*at("lru_gates", c + 1))
                done(ac.activation(gx[:, c, :], PS[c][:, 0:T], ACT.Sigmoid, bias=col("lru_bx", c)), "gx")
                done(ac.activation(ga[:, c, :], PS[c][:, T:2 * T], ACT.Sigmoid, bias=col("lru_ba", c)), "ga")
            shift_a("lora", lora, 12)
            act.wait_ge(*at("sv_lora", 2))
            done(ac.activation(lora[0:64, 0, :], lora[0:64, 0, :], ACT.Tanh), "lora_f")
            done(ac.activation(lora[:, 1, :], lora[:, 1, :], ACT.Sigmoid), "lora_f")
            act.wait_ge(*at("lam_rate", 2))
            for c in range(CT):
                done(ac.activation(th[:, c, :], ga[:, c, :], ACT.Tanh, scale=lam[:, 6, c:c + 1]), "lru_th")
            for c in range(CT):
                done(ac.activation(dec[:, c, :], ga[:, c, :], ACT.Exp, scale=lam[:, 7, c:c + 1]), "lru_dec")
            shift_a("v", v_c, 8)
            act.wait_ge(*at("lru_b2", 1))
            done(ac.activation(th, th, ACT.Sqrt), "lru_root")
            for c in range(CT):
                act.wait_ge(*at("z_a", 1))
                done(ac.activation(sig[:, c, :], PS[c // 2][:, (c % 2) * T:(c % 2) * T + T], ACT.Sigmoid,
                                   bias=col("rwkv_w0", c)), "sig")
            for c in range(CT):
                done(ac.activation(a_c[:, c, :], PS[2 + c // 2][:, (c % 2) * T:(c % 2) * T + T], ACT.Sigmoid,
                                   bias=col("rwkv_a0", c)), "a_c")
            act.wait_ge(*at("g_ps", 2))
            for i in range(TT):
                done(ac.copy(g_t[:, i], PS[4 + i][:, :].rearrange("p (h k) -> p h k", h=NH)), "g_t")
            k_copy(0, 2)
            act.wait_ge(*at("kk", 1))
            act.wait_ge(*at("lru_in", 1))
            done(ac.activation(sq, kk, ACT.Square), "kk_sq")
            for c in range(2):
                act.wait_ge(*at("kk_ss", c + 1))
                done(ac.activation(U(1)[:, c * 512:(c + 1) * 512], PS[c][:, :], ACT.Sqrt), "kk_rn")
            act.wait_ge(*at("Z", CT))
            done(ac.activation(Dt, Z, ACT.Exp, scale=-DECAY), "exps")
            done(ac.activation(inv_d, Z, ACT.Exp, scale=DECAY), "exps")
            act.wait_ge(*at("zp", 1))
            done(ac.activation(d_prev, zp, ACT.Exp, scale=-DECAY), "exps")



            k_copy(2, 8)
            for name, dst in (("tok_v_ps", v_t), ("tok_al_ps", RG[:, :, :, 0:64])):
                for i in range(TT):
                    act.wait_ge(*at(name, i + 1))
                    done(ac.copy(dst[:, i], PS[i][:, :].rearrange("p (h k) -> p h k", h=NH)), "tok")
            act.wait_ge(*at("G_ps", 1))
            for j in range(2):
                for np_ in range(2):
                    s = slice(64 * np_, 64 * np_ + 64)
                    done(ac.copy(RG[s, j ^ np_, :, 64:128], PS[4 + j][s, :].rearrange("p (h k) -> p h k", h=NH)), "G")
            v_copy(0, 2)
            for g in range(4):
                act.wait_ge(*at("Et_ps", g + 1))
                done(ac.copy(Et[:, g // 2, 4 * (g % 2):4 * (g % 2) + 4, :],
                             PS[g][:, :].rearrange("p (h k) -> p h k", h=4)), "Et")
            act.wait_ge(*at("Yuv_ps", 1))
            for j in range(2):
                for np_ in range(2):
                    s = slice(64 * np_, 64 * np_ + 64)
                    done(ac.copy(Yuv[s, j ^ np_], PS[2 + j][s, :].rearrange("p (h k) -> p h k", h=NH)), "Yuv")
            for n in (1, 2):
                act.wait_ge(*at("S_ps", n))
                done(ac.copy(St[64:128, n - 1], PS[1][64:128, 0:256].rearrange("p (c k) -> p c k", c=CT)), "St_a")
            v_copy(2, 4)
            act.wait_ge(*at("yT_ps", 2))
            done(ac.copy(YT[:, 6:8, :], PS[1][:, :].rearrange("p (c t) -> p c t", c=2)), "yT_a")

            def square(name, r):
                for i in range(TT):
                    act.wait_ge(*at(name, i * 2 + 2))
                    done(ac.activation(YT[:, 4 * i:4 * i + 4, :], X[:, i, :].rearrange("p (c t) -> p c t", c=4),
                                       ACT.Square, accum_out=st[:, 4 + 4 * r + i:5 + 4 * r + i]), f"ss_x{r}")

            act.wait_ge(*at("pe_wout", 4))
            square("x1", 1)

            def turned(ps_name, gain, made_name):
                act.wait_ge(*at(ps_name, 4))
                for c in (4, 5, 6, 7):
                    done(ac.activation(MT[:, c, :], PS[c // 2][:, (c % 2) * 256:(c % 2) * 256 + 256], ACT.Identity,
                                       scale=col(gain, c)), made_name)

            turned("t_x1", "norm_xa_g", "x1T_a")
            for c in range(1, KT, 2):
                act.wait_ge(*at("pe_q", c + 1))
                done(ac.activation(YT[:, c, :], PS[4 + c % 4][:, 0:T], ACT.Identity, scale=float(XD) ** -0.5), "q_a")
            for u in range(2 * XH):
                act.wait_ge(*at("nmax", u + 1))
                done(ac.activation(prob(u), PS[u % 4][:, 0:T], ACT.Exp, bias=ast[:, 1, u:u + 1],
                                   accum_out=ast[:, 2, u:u + 1]), "expd")
            for u in range(XH):
                act.wait_ge(*at("pT_ps", u + 1))
                done(ac.copy(prob_t(u)[:, 1], PS[4 + 2 * (u % 2) + 1][:, 0:T]), "pT_a")
            for u in range(XH):
                act.wait_ge(*at("o_ps", 2 * u + 2))
                done(ac.copy(YT[:, 2 * u + 1, :], PS[2 * (u % 2) + 1][:, 0:T]), "oT_a")
            act.wait_ge(*at("pe_wo", 4))
            square("x2", 2)
            turned("t_x2", "norm_ffn_g", "x2T_a")
            for i in range(TT):
                act.wait_ge(*at("nl", i + 1))
                done(ac.activation(rt[:, 1, i, :], rt[:, 0, i, :], ACT.Exp, bias=top[:, i, 7:8]), "r_exp")

            act.wait_ge(S("rows_ps"), 1)
            ac.copy(picked_rows, PS[7][:, :]).then_inc(S("rows_sb"), 1)
            act.wait_ge(*at("steps", 1))
            groups = act.value_load(steps_i[0:1, 0:1], min_val=NE // GROUP, max_val=NE * ROUNDS // GROUP)
            with act.Fori(0, groups * GROUP) as i:
                act.wait_ge(S("gate_in"), i + 1)
                ac.activation(m_s, m_g, ACT.Sigmoid, scale=ALPHA).then_inc(S("gate_sig"), 1)
                act.wait_ge(S("turned"), i + 2)
                ac.copy(sel_t, PS[6][:, 0:256].rearrange("p (i t) -> p i t", i=TT)).then_inc(S("sel_t"), 1)
                act.wait_ge(S("rows_ps"), i + 2)
                ac.copy(picked_rows, PS[7][:, :]).then_inc(S("rows_sb"), 1)
                act.wait_ge(S("used_ring"), (i + 1) * PER_EXPERT)
                ac.copy(y_e, PS[6][:, :]).then_inc(S("y_sb"), 1)
            for i in range(TT):
                act.wait_ge(*at("x3", 2 * i + 2))
                done(ac.activation(yt_f[:, 1024:2048], X[:, i, :], ACT.Square, accum_out=st[:, 16 + i:17 + i]), "ss_x3")

        @block.vector
        def _(dve):
            v = nc.vector
            made = {}

            def done(ins, name="dve_step"):
                sem = S(name)
                made[sem.name] = made.get(sem.name, 0) + 1
                ins.then_inc(sem, 1)
                dve.wait_ge(sem, made[sem.name])

            done(v.memset(VX[:], 0.0), "xl_pads")
            for i in range(TT):
                dve.wait_ge(*at("rs_x", i + 1))
                done(v.tensor_scalar(xn[:, i, :], X[:, i, :],
                                     st[:, 2 + i:3 + i], ROOT_D, ALU.mult, ALU.mult), "xn")
            dve.wait_ge(*at("par_ps", 1))
            done(v.tensor_copy(par[:, 0:NPAR], PS[7][:, 0:NPAR]), "par")
            dve.wait_ge(*at("t_x", 2))
            for c in range(4):
                done(v.tensor_scalar(HT[:, c, :], PS[c // 2][:, (c % 2) * 256:(c % 2) * 256 + 256],
                                     col("norm_mix_g", c), None, ALU.mult), "hT_v")
            done(v.tensor_scalar(omu[:], par[:, COL["rwkv_mu"]:COL["rwkv_mu"] + 14], -1.0, 1.0, ALU.mult, ALU.add), "omu")
            lm = par[:, COL["lru_lambda"]:COL["lru_lambda"] + CT]
            done(v.tensor_scalar(lam[:, 4, :], lm, -1.0, None, ALU.mult))
            done(v.tensor_tensor(lam[:, 0, :], lam[:, 4, :], lm, ALU.max), "lam_abs")
            dve.wait_ge(*at("lam_e", 1))
            done(v.tensor_scalar(lam[:, 2, :], lam[:, 1, :], 1.0, None, ALU.add), "lam_w")
            done(v.tensor_scalar(lam[:, 5, :], lam[:, 2, :], -1.0, None, ALU.add))

            dve.wait_ge(*at("lam_ln", 1))
            done(v.tensor_scalar(lam[:, 0, :], lam[:, 5, :], 0.0, None, ALU.is_equal))
            done(v.tensor_tensor(lam[:, 5, :], lam[:, 5, :], lam[:, 0, :], ALU.add))
            done(v.reciprocal(lam[:, 5, :], lam[:, 5, :]))
            done(v.tensor_tensor(lam[:, 3, :], lam[:, 3, :], lam[:, 5, :], ALU.mult))
            done(v.tensor_tensor(lam[:, 3, :], lam[:, 3, :], lam[:, 0, :], ALU.add))
            done(v.tensor_tensor(lam[:, 3, :], lam[:, 3, :], lam[:, 1, :], ALU.mult))
            done(v.scalar_tensor_tensor(out=lam[:, 3, :], in0=lam[:, 4, :], scalar=0.0, in1=lam[:, 3, :],
                                        op0=ALU.max, op1=ALU.add))
            done(v.tensor_scalar(lam[:, 6, :], lam[:, 3, :], 8.0, None, ALU.mult), "lam_rate")
            done(v.tensor_scalar(lam[:, 7, :], lam[:, 3, :], -8.0, None, ALU.mult), "lam_rate")
            dve.wait_ge(*at("u_gl", CT))
            for c in range(CT):
                dve.wait_ge(*at("xl", c + 1))
                done(v.tensor_scalar(xc[:, c, :], xl_pad[:, c, 0:T], col("conv_w", c), col("conv_b", c),
                                     ALU.mult, ALU.add), "conv")
                for j in range(1, 4):
                    done(v.scalar_tensor_tensor(out=xc[:, c, :], in0=xl_pad[:, c, j:j + T],
                                                scalar=col("conv_w", 4 * j + c), in1=xc[:, c, :],
                                                op0=ALU.mult, op1=ALU.add), "conv")

            def shift_v(name, dst, mu0):
                n = 2 if name == "lora" else CT
                for c in range(n):
                    dve.wait_ge(*at("sa_" + name, c + 1))
                    done(v.scalar_tensor_tensor(out=dst[:, c, 1:T], in0=PS[4 + c][:, 0:T - 1],
                                                scalar=col("rwkv_mu", mu0 + c), in1=dst[:, c, 1:T],
                                                op0=ALU.mult, op1=ALU.add), "sv_" + name)

            dve.wait_ge(*at("rs_mem", 1))
            for i in range(TT):
                done(v.tensor_scalar(mem[:, i, :], mem[:, i, :], st[:, 6 + i:7 + i], ROOT_D, ALU.mult, ALU.mult), "memn")
            shift_v("r", r_c, 0)
            dve.wait_ge(*at("t_mem", 2))
            for c in range(4):
                done(v.tensor_scalar(MT[:, c, :], PS[c // 2][:, (c % 2) * 256:(c % 2) * 256 + 256],
                                     col("norm_mem_g", c), None, ALU.mult), "mT_v")
            shift_v("k", k_c, 4)
            dve.wait_ge(*at("u_k", CT))
            for c in range(CT):
                done(v.tensor_scalar(kk[:, c, :], k_c[:, c, :], col("rwkv_k_k", c), None, ALU.mult),
                     "kk" if c == CT - 1 else "dve_step")
            shift_v("lora", lora, 12)
            dve.wait_ge(*at("lru_dec", CT))
            done(v.tensor_scalar(ga, th, 1.0, None, ALU.add))
            done(v.reciprocal(ga, ga))
            done(v.scalar_tensor_tensor(out=U(3), in0=U(3), scalar=2.0, in1=U(2), op0=ALU.mult, op1=ALU.mult))
            done(v.tensor_tensor(gx, gx, xc, ALU.mult), "lru_b2")
            shift_v("v", v_c, 8)
            dve.wait_ge(*at("lru_root", 1))
            done(v.tensor_tensor(th, th, gx, ALU.mult), "lru_in")
            for c in range(CT):
                done(v.tensor_tensor_scan(ga[:, c, :], dec[:, c, :], th[:, c, :], 0.0, ALU.mult, ALU.add))
            done(v.tensor_tensor(YT[:, 0:CT, :], YT[:, 0:CT, :], ga, ALU.mult), "y_lru")
            dve.wait_ge(*at("sig", CT))
            for c in range(CT):
                done(v.tensor_tensor_scan(Z[:, c, :], restart[:], sig[:, c, :], 0.0, ALU.mult, ALU.add), "Z")
            done(v.tensor_tensor(zp, Z, sig, ALU.subtract), "zp")
            dve.wait_ge(*at("kk_rn", 2))
            done(v.tensor_scalar(sq, sq, 1e-12, None, ALU.max))
            done(v.reciprocal(sq, sq))
            done(v.tensor_tensor(kk, kk, sq, ALU.mult))
            dve.wait_ge(*at("a_c", CT))
            done(v.tensor_tensor(beta, kk, a_c, ALU.mult))
            for c in range(CT):
                done(v.tensor_scalar(a_c[:, c, :], a_c[:, c, :], 1.0, col("rwkv_k_a", c), ALU.subtract, ALU.mult))
            done(v.scalar_tensor_tensor(out=U(6), in0=U(9), scalar=1.0, in1=U(6), op0=ALU.add, op1=ALU.mult))
            dve.wait_ge(*at("exps", 3))
            done(v.scalar_tensor_tensor(out=U(3), in0=U(14), scalar=-1.0, in1=U(13), op0=ALU.mult, op1=ALU.mult), "al_c")
            done(v.tensor_tensor(bt_c, beta, inv_d, ALU.mult), "bt_c")
            done(v.tensor_tensor(kt_c, k_c, inv_d, ALU.mult), "kt_c")
            last_d = Dt.rearrange("p c (n s) -> p c n s", s=CH)[:, :, :, CH - 1:CH]
            done(v.tensor_copy(dc[:].unsqueeze(3), last_d))
            dcb = dc[:].unsqueeze(3).broadcast_to([P, CT, NCH, CH])
            done(v.tensor_tensor(bh_c.rearrange("p c (n s) -> p c n s", s=CH),
                                 bt_c.rearrange("p c (n s) -> p c n s", s=CH), dcb, ALU.mult), "bh_c")
            done(v.tensor_tensor(kh_c.rearrange("p c (n s) -> p c n s", s=CH),
                                 kt_c.rearrange("p c (n s) -> p c n s", s=CH), dcb, ALU.mult), "kh_c")
            done(v.tensor_tensor(AR[:, 1], r_c, Dt, ALU.mult), "r_til")
            by_half = lambda ap: ap.rearrange("p (c e) k -> p c e k", e=2)
            for i in range(TT):
                dve.wait_ge(*at("n_ps", 2 * i + 2))
                for hp in range(2):
                    done(v.tensor_tensor(by_half(Nm[:, i])[:, :, hp], PS[2 + 2 * i + hp][:, 0:256].rearrange("p (c k) -> p c k", c=CT),
                                         mask_n[:, 0:4, :], ALU.mult))
            done(v.tensor_reduce(N_flat.rearrange("p (x s) -> p x s", x=BL),
                                 U(22).rearrange("p (x b s) -> p x s b", b=CH // BL, s=BL), AX_X, ALU.add), "N_flat")
            dve.wait_ge(*at("bd_cleared", 1))
            for i in range(TT):
                for hp in range(2):
                    for np_ in range(2):
                        s = slice(64 * np_, 64 * np_ + 64)
                        done(v.tensor_tensor(by_half(O_bd[s, i])[:, :, hp, s],
                                             PS[2 + 2 * i + hp][s, 0:256].rearrange("p (c k) -> p c k", c=CT),
                                             mask_o[s, 0:4, :], ALU.mult), "O")
            for c in range(CT):
                done(v.scalar_tensor_tensor(out=rkk[:, c, :], in0=r_c[:, c, :], scalar=col("rwkv_r_k", c),
                                            in1=k_c[:, c, :], op0=ALU.mult, op1=ALU.mult), "rkk")
            for name, dst, b in (("tok_bh_ps", bh_t, 2), ("tok_kh_ps", kh_t, 4)):
                for i in range(TT):
                    dve.wait_ge(*at(name, i + 1))
                    done(v.tensor_copy(dst[:, i], PS[b + i][:, :].rearrange("p (h k) -> p h k", h=NH)), "tok_v")
            for u in range(8):
                kind, i, hp = u // 4, (u // 2) % 2, u % 2
                dst = (STb, STk)[kind]
                dve.wait_ge(*at("st_ps", 2 * (u // 2) + 2))
                done(v.tensor_tensor(dst[:, i].rearrange("p (c e) w k -> p c e w k", e=2)[:, :, hp],
                                     PS[ST_BANKS[u // 2] + u % 2][:, :].rearrange("p (c w k) -> p c w k", c=CT, w=2),
                                     mask_ar, ALU.mult), "st")
            dve.wait_ge(*at("bonus_ps", 1))
            done(v.tensor_copy(gst[:, 7], PS[2][:, 0:TT * NH].rearrange("p (i h) -> p i h", i=TT)), "bonus")
            own_n = N_own.rearrange("p (t s) -> p t s", t=BL)
            own_t, tmp = (ap.rearrange("p (s t) -> p s t", s=BL) for ap in (T_own, T_tmp))
            done(v.tensor_copy(own_t, eye16))
            dve.wait_ge(*at("ld_N", 16 * (P // BL)))
            for k in range(BL - 1):
                size = [P, k + 1, BL - 1 - k]
                new, part = own_t[:, 0:k + 1, k + 1:BL], tmp[:, 0:k + 1, k + 1:BL]
                n_col = own_n[:, k + 1:BL, k:k + 1].rearrange("p t s -> p s t").broadcast_to(size)
                done(v.tensor_tensor(part, own_t[:, 0:k + 1, k:k + 1].broadcast_to(size), n_col, ALU.mult))
                done(v.tensor_tensor(new, new, part, ALU.add), "T_flat" if k == BL - 2 else "dve_step")
            for n in (1, 2):
                done(v.tensor_tensor(DI[:, n - 1], eye8[:, 0:CT, :],
                                     dc[:, :, n:n + 1].broadcast_to([P, CT, CH]), ALU.mult), "DI")
            bc = lambda x: x.unsqueeze(3).broadcast_to([P, TT, NH, HEAD])
            lx = lambda w: lnx[:, w, :].rearrange("p (h k) -> p h k", h=NH)
            dve.wait_ge(*at("ld_late", 64))
            dve.wait_ge(*at("tok", 2))
            dve.wait_ge(*at("g_t", 2))
            done(v.tensor_tensor(y_add, v_t, bc(gst[:, 7]), ALU.mult))
            for i in range(TT):
                done(v.tensor_tensor(y_add[:, i], y_add[:, i], lx(1), ALU.add))
            done(v.tensor_tensor(y_add, y_add, g_t, ALU.mult))
            for i in range(TT):
                done(v.tensor_tensor(g_t[:, i], g_t[:, i], lx(0), ALU.mult))
            dve.wait_ge(*at("ld_T", 16 * (P // BL)))
            for np_ in range(2):
                s = slice(64 * np_, 64 * np_ + 64)
                size = [64, TT * NH, CH // BL, BL]
                done(v.tensor_tensor(T16[s, :, :, s].rearrange("p i h (b t) -> p (i h) b t", b=CH // BL),
                                     T_flat[s].rearrange("p (x t) -> p x t", x=BL).unsqueeze(2).broadcast_to(size),
                                     own_block[s].unsqueeze(1).unsqueeze(3).broadcast_to(size), ALU.mult), "T16")
            for m in range(4):
                for g in range(4):
                    dve.wait_ge(*at(f"X{m}_ps", g + 1))
                    quarter = lambda x: x[:, g // 2, 4 * (g % 2):4 * (g % 2) + 4, :]
                    src = PS[X_BANKS[m] + g][:, :].rearrange("p (h k) -> p h k", h=4)
                    if m == 0:
                        done(v.tensor_copy(quarter(Xs[0]), src), "X0")
                    else:
                        done(v.tensor_tensor(quarter(Xs[m]), src, quarter(Xs[0]), ALU.add), f"X{m}")
            dve.wait_ge(*at("NS_ps", 1))
            done(v.tensor_copy(NS[:, 0:3:2], PS[4][:, :].rearrange("p (i c k) -> p i c k", i=2, c=CT)), "NS")
            done(v.tensor_copy(NS[:, 1], PS[5][:, 0:256].rearrange("p (c k) -> p c k", c=CT)), "NS")
            dve.wait_ge(*at("M_ps", 1))
            done(v.tensor_tensor(Mt[:, 0], PS[1][:, 0:256].rearrange("p (c k) -> p c k", c=CT), DI[:, 0], ALU.add), "Mt")
            done(v.tensor_tensor(Mt[:, 1], PS[0][:, 0:256].rearrange("p (c k) -> p c k", c=CT), DI[:, 1], ALU.add), "Mt")
            dve.wait_ge(*at("Q_ps", 1))
            r_v = AR[:, 1].rearrange("p c (n s) -> p c n s", s=CH)
            for n in (1, 2, 3):
                src = PS[4 + n % 2][:, (n // 2) * 256:(n // 2) * 256 + 256].rearrange("p (c k) -> p c k", c=CT)
                done(v.tensor_tensor(Q[:, n], src, r_v[:, :, n, :], ALU.add), "Q")
            for n in (1, 2):
                dve.wait_ge(*at("S_ps", n))
                done(v.tensor_copy(St[0:64, n - 1], PS[0][0:64, 0:256].rearrange("p (c k) -> p c k", c=CT)), "St_v")
            for i in range(TT):
                dve.wait_ge(*at("Ys_ps", i + 1))
                dve.wait_ge(*at("Yuv", 4))
                s = slice(64, P) if i == 0 else slice(0, P)
                if i == 0:
                    done(v.tensor_copy(Y[0:64, 0], Yuv[0:64, 0]))
                for hp in range(2):
                    e = lambda t: t[s, i].rearrange("p (c e) k -> p c e k", e=2)[:, :, hp]
                    done(v.tensor_tensor(e(Y), PS[4 - 2 * i + hp][s, 0:256].rearrange("p (c k) -> p c k", c=CT),
                                         e(Yuv), ALU.add), "Y")
            done(v.tensor_reduce(gst[:, 0], Y, AX_X, ALU.add))
            done(v.tensor_scalar(gst[:, 1], gst[:, 0], 1.0 / HEAD, None, ALU.mult))
            done(v.tensor_tensor(Y, Y, bc(gst[:, 1]), ALU.subtract))
            done(v.tensor_tensor(Ysq, Y, Y, ALU.mult))
            done(v.tensor_reduce(gst[:, 2], Ysq, AX_X, ALU.add), "gn_ss")
            dve.wait_ge(*at("gn_rs", 1))
            done(v.tensor_scalar(gst[:, 3], gst[:, 4], ROOT_HEAD, None, ALU.mult))
            done(v.tensor_tensor(Y, Y, bc(gst[:, 3]), ALU.mult))
            done(v.tensor_tensor(Y, Y, g_t, ALU.mult))
            done(v.tensor_tensor(Y, Y, y_add, ALU.add), "y_rwkv")
            dve.wait_ge(*at("yT_ps", 1))
            done(v.tensor_copy(YT[:, 4:6, :], PS[0][:, :].rearrange("p (c t) -> p c t", c=2)), "yT_v")

            def add_to_x(ps_name, made_name):
                for u in range(4):
                    dve.wait_ge(*at(ps_name, u + 1))
                    i, h = u // 2, u % 2
                    xs = X[:, i, h * 512:(h + 1) * 512]
                    done(v.tensor_tensor(xs, PS[4 + u][:, :], xs, ALU.add), made_name)

            def norm_rows(r, made_name, dst):
                for i in range(TT):
                    dve.wait_ge(S(f"rs_x{r}"), i + 1)
                    at_ = 6 + 4 * r + i
                    done(v.tensor_scalar(dst[:, i, :], X[:, i, :], st[:, at_:at_ + 1], ROOT_D, ALU.mult, ALU.mult), made_name)

            def turned(ps_name, gain, made_name):
                dve.wait_ge(*at(ps_name, 2))
                for c in range(4):
                    done(v.tensor_scalar(MT[:, c, :], PS[c // 2][:, (c % 2) * 256:(c % 2) * 256 + 256],
                                         col(gain, c), None, ALU.mult), made_name)

            add_to_x("pe_wout", "x1")
            norm_rows(1, "x1n", xm)
            turned("t_x1", "norm_xa_g", "x1T_v")
            for c in range(0, KT, 2):
                dve.wait_ge(*at("pe_q", c + 1))
                done(v.tensor_scalar(YT[:, c, :], PS[4 + c % 4][:, 0:T], float(XD) ** -0.5, None, ALU.mult), "q_v")

            def row_max(u):
                dve.wait_ge(*at("sc_ps", u + 1))
                done(v.tensor_reduce(ast[:, 0, u:u + 1], PS[u % 4][:, 0:T], AX_X, ALU.max))
                done(v.tensor_scalar(ast[:, 1, u:u + 1], ast[:, 0, u:u + 1], -1.0, None, ALU.mult), "nmax")

            def normed(u):
                dve.wait_ge(*at("expd", u + 1))
                done(v.reciprocal(ast[:, 3, u:u + 1], ast[:, 2, u:u + 1]))
                done(v.tensor_scalar(prob(u), prob(u), ast[:, 3, u:u + 1], None, ALU.mult), "prob")

            for u in range(2 * XH + 1):
                if u < 2 * XH:
                    row_max(u)
                if u >= 1:
                    normed(u - 1)
            for u in range(XH):
                dve.wait_ge(*at("pT_ps", u + 1))
                done(v.tensor_copy(prob_t(u)[:, 0], PS[4 + 2 * (u % 2)][:, 0:T]), "pT_v")
            for u in range(XH):
                dve.wait_ge(*at("o_ps", 2 * u + 1))
                done(v.tensor_copy(YT[:, 2 * u, :], PS[2 * (u % 2)][:, 0:T]), "oT_v")
            add_to_x("pe_wo", "x2")
            norm_rows(2, "x2n", x3n)
            turned("t_x2", "norm_ffn_g", "x2T_v")
            dve.wait_ge(*at("x2T_a", 4))
            for u in range(4):
                done(v.memset(PS[u][:, :], 0.0), "banks_cleared")
            for i in range(TT):
                dve.wait_ge(*at("rl_ps", i + 1))
                done(v.tensor_tensor(rt[:, 0, i, :], PS[4 + i][:, 0:NE], b_rt[:], ALU.add))
                done(v.max(top[:, i, :], rt[:, 0, i, :]))
                thr = top[:, i, 3:4]
                done(v.tensor_scalar(rt[:, 2, i, :], rt[:, 0, i, :], thr, None, ALU.is_gt))
                done(v.tensor_scalar(rt[:, 3, i, :], rt[:, 0, i, :], thr, None, ALU.is_equal))
                done(v.tensor_reduce(cnt[:, i:i + 1], rt[:, 2, i, :], AX_X, ALU.add))
                done(v.tensor_scalar(cnt[:, i:i + 1], cnt[:, i:i + 1], -1.0, 4.0, ALU.mult, ALU.add))
                done(v.tensor_tensor_scan(rt[:, 4, i, :], ones[:, 0:NE], rt[:, 3, i, :], 0.0, ALU.mult, ALU.add))
                done(v.tensor_scalar(rt[:, 4, i, :], rt[:, 4, i, :], cnt[:, i:i + 1], None, ALU.is_le))
                done(v.tensor_tensor(rt[:, 3, i, :], rt[:, 3, i, :], rt[:, 4, i, :], ALU.mult))
                done(v.tensor_tensor(rt[:, 5, i, :], rt[:, 2, i, :], rt[:, 3, i, :], ALU.add), "picked")
                done(v.tensor_scalar(top[:, i, 7:8], top[:, i, 0:1], -1.0, None, ALU.mult), "nl")
            for i in range(TT):
                dve.wait_ge(*at("r_exp", i + 1))
                done(v.tensor_tensor(rt[:, 1, i, :], rt[:, 1, i, :], rt[:, 5, i, :], ALU.mult))
                done(v.tensor_reduce(cnt[:, 2 + i:3 + i], rt[:, 1, i, :], AX_X, ALU.add))
                done(v.reciprocal(cnt[:, 2 + i:3 + i], cnt[:, 2 + i:3 + i]))
                done(v.tensor_scalar(gate[:, i, :], rt[:, 1, i, :], cnt[:, 2 + i:3 + i], None, ALU.mult), "gate")
            dve.wait_ge(*at("rank_ps", 3))
            for i in range(TT):
                done(v.scalar_tensor_tensor(out=key[:, i, :], in0=PS[6][:, i * NE:(i + 1) * NE], scalar=1.0,
                                            in1=rt[:, 5, i, :], op0=ALU.add, op1=ALU.mult))
            done(v.tensor_scalar(key[:], key[:], -1.0, None, ALU.add), "key")

            def select(e):
                for t in range(TT):
                    v.tensor_scalar(self_[:, t, :], slot_no[:, 0, :], key[:, t, bass.ds(e, 1)], None,
                                    ALU.is_equal).then_inc(S("self_sb"), 1)

            select(0)
            done(v.memset(yt_f[:, 512:768], 0.0))
            dve.wait_ge(*at("gt_ps", 4))
            for g in range(2):
                s = slice(64 * g, 64 * g + NE)
                done(v.tensor_copy(yt_f[s, 512:768], PS[4 + g][s, 0:T]))
            dve.sem_inc(S("sel_t"), 1)
            dve.sem_inc(S("y_sb"), 1)
            done(v.tensor_reduce(cnt[:, 4:5], PS[6][:, 2 * NE:3 * NE], AX_X, ALU.max))
            done(v.tensor_scalar(cnt[:, 5:6], cnt[:, 4:5], float(SLOTS), None, ALU.is_gt))
            for r in range(2, ROUNDS):
                done(v.scalar_tensor_tensor(out=cnt[:, 5:6], in0=cnt[:, 4:5], scalar=float(r * SLOTS),
                                            in1=cnt[:, 5:6], op0=ALU.is_gt, op1=ALU.add))
            done(v.tensor_scalar(cnt[:, 5:6], cnt[:, 5:6], float(NE // GROUP), float(NE // GROUP), ALU.mult, ALU.add))
            done(v.tensor_copy(steps_i[:], cnt[:, 5:6]), "steps_v")
            dve.sem_inc(S("steps"), 1)
            groups = dve.value_load(steps_i[0:1, 0:1], min_val=NE // GROUP, max_val=NE * ROUNDS // GROUP)
            dve.sem_inc(S("act_sb"), 1)
            gcol = par[:, COL["norm_ffn_g"]:COL["norm_ffn_g"] + KT].rearrange("p (h b) -> p h b", h=2) \
                .unsqueeze(3).broadcast_to([P, 2, 4, SLOTS])

            def spread():
                v.tensor_tensor(xg.rearrange("p (h b) s -> p h b s", h=2),
                                PS[7][:, :].rearrange("p (b h s) -> p h b s", b=4, h=2), gcol, ALU.mult).then_inc(S("xg"), 1)

            dve.wait_ge(*at("ld_fing", 16))
            done(v.tensor_scalar(fin_g, fin_g, ROOT_D, None, ALU.mult))
            dve.wait_ge(S("gathered"), 1)
            spread()
            with dve.Fori(0, groups * GROUP) as i:
                dve.wait_ge(S("turned"), i + 1)
                e = i % NE
                for t in range(TT):
                    v.tensor_scalar(sel[:, t], slot_no[:], key[:, t, bass.ds(e, 1)], gate[:, t, bass.ds(e, 1)],
                                    ALU.is_equal, ALU.mult).then_inc(S("sel_sb"), 1)
                dve.wait_ge(S("sel_sb"), TT * (i + 1))
                for t in range(TT):
                    k_e = key[:, t, bass.ds(e, 1)]
                    v.tensor_scalar(k_e, k_e, float(SLOTS), None, ALU.subtract).then_inc(S("key_moved"), 1)
                dve.wait_ge(S("key_moved"), TT * (i + 1))
                select((i + 1) % NE)
                dve.wait_ge(S("used_ring"), i * PER_EXPERT + 4)
                v.tensor_scalar(m_g, PS[4][:, :], LIMIT, None, ALU.min).then_inc(S("gate_in"), 1)
                v.tensor_scalar(m_u, PS[5][:, :], LIMIT, -LIMIT, ALU.min, ALU.max).then_inc(S("up_in"), 1)
                dve.wait_ge(S("up_in"), i + 1)
                v.scalar_tensor_tensor(out=m_a, in0=m_u, scalar=1.0, in1=m_g, op0=ALU.add, op1=ALU.mult).then_inc(S("up_gate"), 1)
                dve.wait_ge(S("up_gate"), i + 1)
                dve.wait_ge(S("gate_sig"), i + 1)
                v.tensor_tensor(m_a, m_a, m_s, ALU.mult).then_inc(S("act_sb"), 1)
                dve.wait_ge(S("act_ps"), i + 1)
                v.tensor_copy(act_t, PS[6][:, :].rearrange("p (f m) -> p f m", f=4)).then_inc(S("act_t"), 1)
                dve.wait_ge(S("gathered"), i + 2)
                spread()
            for u in range(4):
                i, h = u // 2, u % 2
                dve.wait_ge(S("scattered"), groups * (GROUP * TT) + i + 1)
                xs = X[:, i, h * 512:(h + 1) * 512]
                done(v.tensor_tensor(xs, PS[u][:, :], xs, ALU.add), "x3")
            for i in range(TT):
                dve.wait_ge(S("rs_x3"), i + 1)
                done(v.scalar_tensor_tensor(out=fin[:, i, :], in0=X[:, i, :], scalar=st[:, 18 + i:19 + i], in1=fin_g,
                                            op0=ALU.mult, op1=ALU.mult), "y_out")

        @block.tensor
        def _(pe):
            mm, tr = nc.tensor.matmul, nc.tensor.transpose

            def turn(src, name, banks=0):
                for q in range(4):
                    for c in (2 * q, 2 * q + 1):
                        for i in range(TT):
                            x = tr(PS[q][:, (c % 2) * 256 + i * P:(c % 2) * 256 + i * P + P],
                                   src[:, i, c * P:(c + 1) * P], ident[:])
                    x.then_inc(S(name), 1)

            pe.wait_ge(*at("ident", 1))
            pe.wait_ge(*at("ld_par", 16 * len(PARAM_ROWS)))
            tr(PS[7][:, 0:NPAR], par_rows[0:NPAR, :], ident[0:NPAR, 0:NPAR]).then_inc(S("par_ps"), 1)
            pe.wait_ge(*at("xn", 2))
            turn(xn, "t_x")
            pe.wait_ge(*at("hT_v", 4))
            pe.wait_ge(*at("hT_a", 4))

            def u_tiles(name, lo, hi, free):
                w, _ = WV[name]
                pe.wait_ge(*at("ld_" + name, 16))
                for c in range(lo, hi):
                    if free:
                        pe.wait_ge(*at(free, c + 1))
                    for k in range(KT):
                        x = mm(PS[4 + c][:, 0:T], w[:, k, c * P:(c + 1) * P], HT[:, k, :], start=(k == 0), stop=(k == KT - 1))
                    x.then_inc(S("u_" + name), 1)

            pe.wait_ge(*at("par", 1))
            u_tiles("xl", 0, CT, None)
            u_tiles("gl", 0, CT, "xl")
            u_tiles("r", 0, CT, "gelu")
            pe.wait_ge(*at("memn", 2))
            turn(mem, "t_mem")
            u_tiles("k", 0, CT, "sv_r")
            pe.wait_ge(*at("ld_lruw", 64))
            pe.wait_ge(*at("mT_a", 4))
            pe.wait_ge(*at("mT_v", 4))
            for c in range(CT):
                pe.wait_ge(*at("conv", 4 * c + 4))
                mm(PS[c][:, 0:T], wx_bd[:, c, :], xc[:, c, :], start=True, stop=True)
                mm(PS[c][:, T:2 * T], wa_bd[:, c, :], xc[:, c, :], start=True, stop=True).then_inc(S("lru_gates"), 1)
            u_tiles("lora", 0, 2, "sv_k")
            pe.wait_ge(*at("sv_k", 4))
            pe.wait_ge(*at("sv_lora", 2))
            u_tiles("v", 0, CT, None)
            pe.wait_ge(*at("ld_lora_up", 48))
            pe.wait_ge(*at("lora_f", 2))
            pe.wait_ge(*at("ga", CT))
            for c in range(CT):
                for h in range(2):
                    x = mm(PS[2 * h + c // 2][:, (c % 2) * T:(c % 2) * T + T], wa_up[64 * h:64 * h + 64, c * P:(c + 1) * P],
                           lora[64 * h:64 * h + 64, 0, :], start=True, stop=True)
            x.then_inc(S("z_a"), 1)
            pe.wait_ge(*at("sv_v", CT))
            for i in range(TT):
                mm(PS[4 + i][:, :], lora[:, 1, i * P:(i + 1) * P], g_up[:], start=True, stop=True).then_inc(S("g_ps"), 1)

            def k_tile(c):
                if c == 0:
                    pe.wait_ge(*at("ld_wk", 16))
                    pe.wait_ge(*at("sv_v", CT))
                if c >= 2:
                    pe.wait_ge(*at("K", c - 1))
                for k in range(KT):
                    x = mm(PS[6 + c % 2][:, 0:T], WB[:, k, c * P:(c + 1) * P], MT[:, k, :], start=(k == 0), stop=(k == KT - 1))
                x.then_inc(S("pe_k"), 1)

            def v_part(q):
                m, h = q // 2, q % 2
                if q == 0:
                    pe.wait_ge(*at("ld_wv", 16))
                    pe.wait_ge(*at("K", KT))
                if q >= 2:
                    pe.wait_ge(*at("V", q - 1))
                for k in range(KT):
                    x = mm(PS[6 + q % 2][:, :], MT[:, k, m * P:(m + 1) * P], WB[:, k, h * 512:(h + 1) * 512],
                           start=(k == 0), stop=(k == KT - 1))
                x.then_inc(S("pe_v"), 1)

            k_tile(0)
            k_tile(1)
            pe.wait_ge(*at("kk_sq", 1))
            pe.wait_ge(*at("sig", CT))
            pe.wait_ge(*at("consts_all", 1))
            for c in range(2):
                mm(PS[c][:, :], head_ones[:], U(1)[:, c * 512:(c + 1) * 512], start=True, stop=True).then_inc(S("kk_ss"), 1)
            for c in range(2, KT):
                k_tile(c)

            def to_tokens(src, banks, name):
                for i in range(TT):
                    for c in range(CT):
                        x = tr(PS[banks + i][:, c * P:(c + 1) * P], src[:, c, i * P:(i + 1) * P], ident[:])
                    x.then_inc(S(name), 1)

            pe.wait_ge(*at("a_c", CT))
            pe.wait_ge(*at("al_c", 1))
            pe.wait_ge(*at("bt_c", 1))
            pe.wait_ge(*at("g_t", 2))
            for i in range(TT):
                for np_ in range(2):
                    t0 = (2 * i + np_) * CH
                    for c in range(CT):
                        for hp in range(2):
                            h = slice(64 * hp, 64 * hp + 64)
                            x = mm(PS[2 + 2 * i + hp][64 * np_:64 * np_ + 64, c * 64:(c + 1) * 64],
                                   AR[h, 0, c, t0:t0 + CH], bt_c[h, c, t0:t0 + CH], start=True, stop=True)
                            if np_ == 1 and c == CT - 1:
                                x.then_inc(S("n_ps"), 1)
            pe.wait_ge(*at("kk_rn", 2))
            to_tokens(v_c, 0, "tok_v_ps")
            pe.wait_ge(*at("tok", 2))
            to_tokens(AR[:, 0], 0, "tok_al_ps")
            pe.wait_ge(*at("bh_c", 1))
            pe.wait_ge(*at("O", 4))
            to_tokens(bh_c, 2, "tok_bh_ps")
            pe.wait_ge(*at("kh_c", 1))
            pe.wait_ge(*at("O", 8))
            to_tokens(kh_c, 4, "tok_kh_ps")
            for q in range(4):
                kind, i = q // 2, q % 2
                src = (bt_c, kt_c)[kind]
                if q == 0:
                    pe.wait_ge(*at("r_til", 1))
                    pe.wait_ge(*at("tok", 4))
                if q in (1, 2):
                    pe.wait_ge(*at("tok_v", 2 * q))
                if q == 3:
                    pe.wait_ge(*at("st", 2))
                for np_ in range(2):
                    t0 = (2 * i + np_) * CH
                    for c in range(CT):
                        for hp in range(2):
                            h = slice(64 * hp, 64 * hp + 64)
                            x = mm(PS[ST_BANKS[q] + hp][64 * np_:64 * np_ + 64, c * 128:(c + 1) * 128].rearrange("p (w k) -> p w k", w=2),
                                   src[h, c, t0:t0 + CH], AR[h, :, c, t0:t0 + CH], start=True, stop=True)
                            if np_ == 1 and c == CT - 1:
                                x.then_inc(S("st_ps"), 1)
            pe.wait_ge(*at("rkk", CT))
            pe.wait_ge(*at("st", 4))
            for i in range(TT):
                for c in range(CT):
                    x = mm(PS[2][:, i * NH + 2 * c:i * NH + 2 * c + 2], rkk[:, c, i * P:(i + 1) * P],
                           head_ones[:, 0:P:64], start=True, stop=True)
            x.then_inc(S("bonus_ps"), 1)

            def product(bank, name, *terms):
                for flip in range(2):
                    for h in range(NH):
                        for np_ in range(2):
                            j = np_ ^ flip
                            rows = slice(64 * np_, 64 * np_ + 64)
                            for n, (l, r) in enumerate(terms):
                                x = mm(PS[bank + j][rows, h * 64:(h + 1) * 64], l(rows, np_, j)[:, h], r(rows, np_, j)[:, h],
                                       start=(n == 0), stop=(n == len(terms) - 1))
                x.then_inc(S(name), 1)


            by_i = lambda t: (lambda rows, np_, j: t[rows, j ^ np_])
            part = lambda t, w: (lambda rows, np_, j: t[rows, j ^ np_, :, w])

            pe.wait_ge(*at("st", 8))
            product(4, "G_ps", (part(STk, 0), by_i(v_t)))
            v_part(0)
            v_part(1)

            def pair_product(l, r, bank, name, before=None):
                for g in range(4):
                    if before:
                        before(g)
                    for h in range(4):
                        i, hh = g // 2, 4 * (g % 2) + h
                        x = mm(PS[bank + g][:, h * P:(h + 1) * P], l[:, i, hh, :], r[:, i, hh, :], start=True, stop=True)
                    x.then_inc(S(name), 1)

            pe.wait_ge(*at("T16", 2))
            pe.wait_ge(*at("bonus", 1))
            pair_product(O_bd, T16, 0, "Et_ps")
            pe.wait_ge(*at("G", 4))
            pe.wait_ge(*at("V", 2))
            pair_product(T16, RG, X_BANKS[0], "X0_ps")

            def step_in(m):
                def before(g):
                    if m == 1:
                        pe.wait_ge(*at("Et", g + 1))
                    pe.wait_ge(*at(f"X{m - 1}", g + 1))
                return before

            for m in range(1, 4):
                pair_product(Et, Xs[m - 1], X_BANKS[m], f"X{m}_ps", step_in(m))
            pe.wait_ge(*at("X3", 4))

            def by_chunk(chunks, bank, name, width, *terms):
                for c in range(CT):
                    for hp in range(2):
                        for k in range(2):
                            for n in chunks:
                                if n // 2 != k:
                                    continue
                                np_, i = n % 2, n // 2
                                j = i ^ np_
                                rows = slice(64 * np_, 64 * np_ + 64)
                                o = PS[bank + np_][64 * hp:64 * hp + 64, (i * width + c) * 64:(i * width + c + 1) * 64]
                                for m, (l, r) in enumerate(terms):
                                    x = mm(o, l(rows, np_, j)[:, 2 * c + hp], r(rows, np_, j)[:, 2 * c + hp],
                                           start=(m == 0), stop=(m == len(terms) - 1))
                x.then_inc(S(name), 1)

            by_chunk((0, 1, 2), 4, "NS_ps", CT, (by_i(bh_t), by_i(XU)), (by_i(kh_t), by_i(v_t)))
            by_chunk((1, 2), 0, "M_ps", 0, (by_i(XW), by_i(bh_t)))
            product(2, "Yuv_ps", (part(STb, 1), by_i(XU)), (part(STk, 1), by_i(v_t)))
            pe.wait_ge(*at("NS", 2))
            by_chunk((1, 2, 3), 4, "Q_ps", CT, (by_i(XW), part(STb, 1)))
            pe.wait_ge(*at("Mt", 2))
            for n in (1, 2):
                if n == 2:
                    pe.wait_ge(*at("St_a", 1))
                    pe.wait_ge(*at("St_v", 1))
                prev = NS[:, 0] if n == 1 else St[:, 0]
                for c in range(CT):
                    for hp in range(2):
                        h = slice(64 * hp, 64 * hp + 64)
                        o = PS[hp][h, c * 64:(c + 1) * 64]
                        mm(o, ident[h, h], NS[h, n, c, :], start=True, stop=False)
                        x = mm(o, Mt[h, n - 1, c, :], prev[h, c, :], start=False, stop=True)
                x.then_inc(S("S_ps"), 1)
            pe.wait_ge(*at("Q", 3))
            pe.wait_ge(*at("St_a", 2))
            pe.wait_ge(*at("St_v", 2))
            for i in range(TT):
                if i == 1:
                    pe.wait_ge(*at("Yuv", 4))
                for c in range(CT):
                    for np_ in range(2):
                        n = 2 * i + np_
                        if n == 0:
                            continue
                        state = NS[:, 0] if n == 1 else St[:, n - 2]
                        for hp in range(2):
                            h = slice(64 * hp, 64 * hp + 64)
                            x = mm(PS[4 - 2 * i + hp][64 * np_:64 * np_ + 64, c * 64:(c + 1) * 64],
                                   Q[h, n, c, :], state[h, c, :], start=True, stop=True)
                x.then_inc(S("Ys_ps"), 1)
            v_part(2)
            v_part(3)
            pe.wait_ge(*at("y_rwkv", 1))
            y_tok = R[:, 0, :].rearrange("p (i d) -> p i d", i=TT)
            for q in range(2):
                for c in (2 * q, 2 * q + 1):
                    for i in range(TT):
                        x = tr(PS[q][:, (c % 2) * 256 + i * P:(c % 2) * 256 + i * P + P], y_tok[:, i, c * P:(c + 1) * P], ident[:])
                x.then_inc(S("yT_ps"), 1)

            def project(src, w, name):
                for u in range(4):
                    i, h = u // 2, u % 2
                    for k in range(KT):
                        x = mm(PS[4 + u][:, :], src[:, k, i * P:(i + 1) * P], w[:, k, h * 512:(h + 1) * 512],
                               start=(k == 0), stop=(k == KT - 1))
                    x.then_inc(S(name), 1)

            pe.wait_ge(*at("ld_wo1", 16))
            pe.wait_ge(*at("y_lru", 1))
            pe.wait_ge(*at("yT_a", 1))
            pe.wait_ge(*at("yT_v", 1))
            pe.wait_ge(*at("V", 4))
            project(YT, W2, "pe_wout")
            pe.wait_ge(*at("x1n", 2))
            turn(xm, "t_x1")
            pe.wait_ge(*at("x1T_a", 4))
            pe.wait_ge(*at("x1T_v", 4))
            pe.wait_ge(*at("ld_wq", 16))
            for c in range(KT):
                if c >= 4:
                    pe.wait_ge(*at("q_a" if c % 2 else "q_v", (c - 4) // 2 + 1))
                for k in range(KT):
                    x = mm(PS[4 + c % 4][:, 0:T], W1[:, k, c * P:(c + 1) * P], MT[:, k, :], start=(k == 0), stop=(k == KT - 1))
                x.then_inc(S("pe_q"), 1)
            pe.wait_ge(*at("q_a", 4))
            pe.wait_ge(*at("q_v", 4))
            for u in range(2 * XH):
                h, i = u // 2, u % 2
                if u >= 4:
                    pe.wait_ge(*at("expd", u - 3))
                for k in range(2):
                    x = mm(PS[u % 4][:, 0:T], YT[:, 2 * h + k, i * P:(i + 1) * P], HT[:, 2 * h + k, :], start=(k == 0), stop=(k == 1))
                x.then_inc(S("sc_ps"), 1)

            def turn_prob(h):
                pe.wait_ge(*at("prob", 2 * h + 2))
                if h >= 2:
                    pe.wait_ge(*at("pT_a", h - 1))
                    pe.wait_ge(*at("pT_v", h - 1))
                for m in range(2):
                    for i in range(TT):
                        x = tr(PS[4 + 2 * (h % 2) + m][:, i * P:(i + 1) * P], prob(2 * h + i)[:, m * P:(m + 1) * P], ident[:])
                x.then_inc(S("pT_ps"), 1)

            def head_out(h):
                pe.wait_ge(*at("pT_a", h + 1))
                pe.wait_ge(*at("pT_v", h + 1))
                if h == 0:
                    pe.wait_ge(*at("expd", 2 * XH))
                if h >= 2:
                    pe.wait_ge(*at("oT_a", h - 1))
                    pe.wait_ge(*at("oT_v", h - 1))
                for d in range(2):
                    for m in range(2):
                        x = mm(PS[2 * (h % 2) + d][:, 0:T], V[:, m, (2 * h + d) * P:(2 * h + d + 1) * P], prob_t(h)[:, m],
                               start=(m == 0), stop=(m == 1))
                    x.then_inc(S("o_ps"), 1)

            turn_prob(0)
            turn_prob(1)
            head_out(0)
            head_out(1)
            turn_prob(2)
            turn_prob(3)
            head_out(2)
            head_out(3)
            pe.wait_ge(*at("oT_a", 4))
            pe.wait_ge(*at("oT_v", 4))
            pe.wait_ge(*at("ld_wo2", 16))
            project(YT, WB, "pe_wo")
            pe.wait_ge(*at("x2n", 2))
            turn(x3n, "t_x2")
            pe.wait_ge(*at("x2T_a", 4))
            pe.wait_ge(*at("x2T_v", 4))
            pe.wait_ge(*at("ld_late", 64))
            for i in range(TT):
                for k in range(KT):
                    x = mm(PS[4 + i][:, 0:NE], MT[:, k, i * P:(i + 1) * P], w_rt[:, k, :], start=(k == 0), stop=(k == KT - 1))
                x.then_inc(S("rl_ps"), 1)
            pe.wait_ge(*at("picked", 2))
            m0, m1 = rt[:, 5, 0, :], rt[:, 5, 1, :]
            mm(PS[6][:, 0:NE], before[:], m0, start=True, stop=True).then_inc(S("rank_ps"), 1)
            mm(PS[6][:, NE:2 * NE], ones[:], m0, start=True, stop=False)
            mm(PS[6][:, NE:2 * NE], before[:], m1, start=False, stop=True).then_inc(S("rank_ps"), 1)
            mm(PS[6][:, 2 * NE:3 * NE], ones[:], m0, start=True, stop=False)
            mm(PS[6][:, 2 * NE:3 * NE], ones[:], m1, start=False, stop=True).then_inc(S("rank_ps"), 1)
            pe.wait_ge(*at("gate", 2))
            for g in range(2):
                for i in range(TT):
                    mm(PS[4 + g][64 * g:64 * g + NE, i * P:(i + 1) * P], gate[:, i, :], ident[:],
                       start=True, stop=True).then_inc(S("gt_ps"), 1)
            pe.sem_inc(S("turned"), 1)

            def pick(n):
                pe.wait_ge(S("self_sb"), TT * (n + 1))
                for t in range(TT):
                    for h in range(2):
                        x = mm(PS[7][64 * h:64 * h + 64, :], self_[:, t, :], x3n[:, t, h * 512:(h + 1) * 512],
                               start=(t == 0), stop=(t == TT - 1))
                x.then_inc(S("rows_ps"), 1)

            def gather(n):
                pe.wait_ge(S("rows_sb"), n + 1)
                for b in range(4):
                    x = tr(PS[7][:, b * P:(b + 1) * P], picked_rows[:, b * P:(b + 1) * P], ident[:])
                x.then_inc(S("gathered"), 1)

            def scatter(n):
                pe.wait_ge(S("y_sb"), n + 1)
                pe.wait_ge(S("sel_t"), n + 1)
                for t in range(TT):
                    for g in range(2):
                        h = slice(64 * g, 64 * g + 64)
                        x = mm(PS[2 * t + g][:, :], sel_t[h, t, :], y_e[h, :], start=False, stop=True,
                               skip_group_check=True)
                    x.then_inc(S("scattered"), 1)

            pick(0)
            gather(0)
            pe.wait_ge(*at("banks_cleared", 4))
            pe.wait_ge(*at("ld_bdn", 32))
            pe.wait_ge(*at("steps", 1))
            groups = pe.value_load(steps_i[0:1, 0:1], min_val=NE // GROUP, max_val=NE * ROUNDS // GROUP)

            def expert_pass(group, u):
                i = group * GROUP + u

                def chunk(q):
                    m = PER_EXPERT * u + q
                    pe.wait_ge(S(f"ld_ring{m % RING}"), (group * TURNS + m // RING + 1) * 16)
                    return ring[m % RING]

                pe.wait_ge(S("ld_bgu"), 16 * (i + 1))
                pe.wait_ge(S("act_sb"), i + 1)
                for w in range(2):
                    for g in range(2):
                        x = mm(PS[4 + w][64 * g:64 * g + 64, :], ones[0:1, 0:SLOTS], bgu[:, w, g, :], start=True, stop=False)
                x.then_inc(S("used_b"), 1)
                pe.wait_ge(S("xg"), i + 1)
                for q in range(4):
                    gu = as_gu(chunk(q))
                    for c in range(2):
                        for w in range(2):
                            for g in range(2):
                                x = mm(PS[4 + w][64 * g:64 * g + 64, :], xg[:, 2 * q + c, :], gu[:, c, w, g, :],
                                       start=False, stop=(q == 3 and c == 1))
                    x.then_inc(S("used_ring"), 1)
                scatter(i)
                pe.wait_ge(S("sel_sb"), TT * (i + 1))
                for t in range(TT):
                    x = tr(PS[6][:, t * P:(t + 1) * P], sel[:, t].rearrange("p w s -> p (w s)"), ident[:])
                x.then_inc(S("turned"), 1)
                pe.wait_ge(S("act_sb"), i + 2)
                pe.wait_ge(S("sel_t"), i + 2)
                for f in range(4):
                    x = tr(PS[6][:, f * P:(f + 1) * P], m_a[:, f * P:(f + 1) * P], ident[:])
                x.then_inc(S("act_ps"), 1)
                pick(i + 1)
                pe.wait_ge(S("act_t"), i + 1)
                for q in range(2):
                    dn = as_dn(chunk(4 + q))
                    for c in range(4):
                        for g in range(2):
                            x = mm(PS[6][64 * g:64 * g + 64, :], act_t[:, c, 64 * q:64 * q + 64], dn[:, c, g, :],
                                   start=(q == 0 and c == 0), stop=(q == 1 and c == 3))
                    x.then_inc(S("used_ring"), 1)
                gather(i + 1)

            with pe.Fori(0, groups) as group:
                for u in range(GROUP):
                    expert_pass(group, u)
            scatter(groups * GROUP)


_NAMES = ['x', 'mem', 'norm_mix_g', 'w_in', 'conv_w', 'conv_b', 'lru_wx', 'lru_bx', 'lru_wa', 'lru_ba',
          'lru_lambda', 'rwkv_mu', 'rwkv_w0', 'rwkv_w_up', 'rwkv_a0', 'rwkv_a_up', 'rwkv_g_up', 'rwkv_k_k',
          'rwkv_k_a', 'rwkv_r_k', 'rwkv_lnx_g', 'rwkv_lnx_b', 'w_out', 'norm_xa_g', 'norm_mem_g', 'xa_wq',
          'xa_wk', 'xa_wv', 'xa_wo', 'norm_ffn_g', 'w_router', 'b_router', 'w_gu', 'b_gu', 'w_dn', 'b_dn',
          'final_norm_g']


def kernel(**inputs):
    import numpy as _np
    import concourse.bacc as _bacc
    from concourse import mybir as _mybir
    from concourse.bass_utils import run_bass_kernel_spmd as _run

    nc = _bacc.Bacc("TRN2", target_bir_lowering=False, num_devices=1)
    arrays, aps = {}, {}
    for name in _NAMES:
        arr = _np.ascontiguousarray(inputs[name])
        arrays[f"in_{name}"] = arr
        aps[name] = nc.dram_tensor(f"in_{name}", arr.shape, _mybir.dt.from_np(arr.dtype), kind="ExternalInput").ap()
    out = nc.dram_tensor("out", (1, T, D), _mybir.dt.float32, kind="ExternalOutput").ap()
    build(nc, aps, out)
    r = _run(nc, [arrays], core_ids=[0])
    return r.results[0]["out"]
```

```python
from contextlib import ExitStack

import numpy as np

import concourse.bass as bass
from concourse import mybir

ALU = mybir.AluOpType
ACT = mybir.ActivationFunctionType
F32 = mybir.dt.float32
I32 = mybir.dt.int32
AX_X = mybir.AxisListType.X

P = 128
T, D = 256, 1024
TT = T // P
KT = D // P
LRU_W = RW = 512
CT = RW // P
IN_W = 2816
HEAD = 64
NH = RW // HEAD
CH = 64
NCH = T // CH
BL = 16
ST_BANKS = (0, 2, 4, 0)
X_BANKS = (4, 0, 4, 0)
XH, XD = 4, 256
NE = 32
SLOTS = 64
ROUNDS = T // SLOTS
EPS, GN_EPS = 1e-6, 64e-5
ROOT_D, ROOT_HEAD = float(np.sqrt(D)), float(np.sqrt(HEAD))
DECAY = float(np.exp(-0.5))
LIMIT, ALPHA = 7.0, 1.702
UNIT = 1024
CHUNK = 2048
GU_CHUNKS, DN_CHUNKS = KT, KT // 2
PER_EXPERT = GU_CHUNKS + DN_CHUNKS
RING = 16
GROUP = 4
TURNS = GROUP * PER_EXPERT // RING

PARAM_ROWS = [("norm_mix_g", KT), ("norm_mem_g", KT), ("norm_xa_g", KT), ("norm_ffn_g", KT),
              ("conv_w", 4 * CT), ("conv_b", CT), ("lru_bx", CT), ("lru_ba", CT), ("lru_lambda", CT),
              ("rwkv_mu", 14), ("rwkv_w0", CT), ("rwkv_a0", CT), ("rwkv_k_k", CT), ("rwkv_k_a", CT),
              ("rwkv_r_k", CT)]
PAR_SPLIT = 3
TURNED_V, TURNED_A = (0, 1, 4, 5), (2, 3, 6, 7)
COL, NPAR = {}, 0
for _name, _rows in PARAM_ROWS:
    COL[_name] = NPAR
    NPAR += _rows


SHARED = {}
for _sem, _steps in (
    ("early_pe", [("t_x", 4), ("par_ps", 1), ("u_xl", 4), ("u_gl", 4), ("u_r", 4), ("t_mem", 4), ("u_k", 4),
                  ("lru_gates", 4), ("u_lora", 2), ("u_v", 4), ("z_a", 1), ("g_ps", 2)]),
    ("early_dve", [("xl_pads", 1), ("xn", 2), ("par", 1), ("hT_v", 4), ("omu", 1), ("lam_abs", 1), ("lam_w", 1),
                   ("lam_rate", 2), ("conv", 16), ("memn", 2), ("mT_v", 4)]),
    ("early_act", [("ss_x", 2), ("hT_a", 4), ("lam_e", 1), ("lam_ln", 1), ("xl", 4), ("ss_mem", 2),
                   ("gelu", 4), ("sa_r", 4), ("mT_a", 4), ("sa_k", 4)]),
    ("router_pe", [("rl_ps", 2), ("rank_ps", 3), ("gt_ps", 4)]),
    ("router_dve", [("gate", 1), ("key", 1), ("steps_v", 1), ("banks_cleared", 4)]),
    ("rwkv_pe", [("kk_ss", 2), ("n_ps", 4), ("tok_v_ps", 2), ("tok_al_ps", 2), ("tok_bh_ps", 2), ("tok_kh_ps", 2),
                 ("st_ps", 8), ("bonus_ps", 1), ("G_ps", 1), ("Et_ps", 4), ("X0_ps", 4), ("X1_ps", 4), ("X2_ps", 4),
                 ("X3_ps", 4), ("NS_ps", 1), ("M_ps", 1), ("Yuv_ps", 1), ("Q_ps", 1), ("S_ps", 2),
                 ("Ys_ps", 2), ("yT_ps", 2)]),
    ("rwkv_dve", [("al_c", 1), ("bt_c", 1), ("kt_c", 1), ("bh_c", 1), ("kh_c", 1), ("r_til", 1), ("N_flat", 1),
                  ("O", 8), ("rkk", 4), ("tok_v", 4), ("st", 8), ("bonus", 1)]),
    ("solve_dve", [("T_flat", 1), ("DI", 2), ("T16", 2), ("X0", 4), ("X1", 4), ("X2", 4), ("X3", 4), ("NS", 2),
                   ("Mt", 2), ("Q", 3), ("St_v", 2), ("Y", 4)]),
    ("solve_act", [("tok", 4), ("G", 4), ("Et", 4), ("Yuv", 4), ("St_a", 2)]),
):
    _at = 0
    for _name, _n in _steps:
        SHARED[_name] = (_sem, _at)
        _at += _n


def build(nc, a, out):
    with ExitStack() as ctx:
        def sb(name, shape, dt=F32):
            return ctx.enter_context(nc.sbuf_tensor(name, shape, dt))

        sems = {}

        def S(name):
            name = SHARED.get(name, (name, 0))[0]
            if name not in sems:
                sems[name] = ctx.enter_context(nc.semaphore(name))
            return sems[name]

        def at(name, n):
            return S(name), SHARED[name][1] + n if name in SHARED else n

        AB = sb("AB", [P, RING * CHUNK])
        A = AB[:, 0:24576]
        B = AB[:, 24576:32768]
        X = sb("X", [P, TT, D])
        HT = sb("HT", [P, KT, T])
        MT = sb("MT", [P, KT, T])
        VX = sb("VX", [P, 2048])
        YT = sb("YT", [P, KT, T])
        R = sb("R", [P, 2, UNIT])
        par_rows = sb("par_rows", [P, P])
        par = sb("par", [P, P])
        omu = sb("omu", [P, 14])
        ident = sb("ident", [P, P])
        ones = sb("ones", [P, P])
        neg_half = sb("neg_half", [P, TT * NH])
        before = sb("before", [P, P])
        head_ones = sb("head_ones", [P, P])
        M = sb("M", [P, 2560])
        eye8, mask_n, mask_o = (M[:, i * 512:(i + 1) * 512].rearrange("p (e k) -> p e k", e=8) for i in range(3))
        eye16 = M[:, 1536:1792].rearrange("p (s t) -> p s t", s=BL)
        own_block = M[:, 1792:1796]
        mask_ar = M[:, 2048:2560].rearrange("p (c w k) -> p c w k", c=4, w=2)
        restart = sb("restart", [P, T])
        slot_no = sb("slot_no", [P, 2, SLOTS])
        half_rows = sb("half_rows", [2, P])
        w_bd = sb("w_bd", [P, 2 * CT * P])
        wx_bd, wa_bd = (w_bd[:, i * 512:(i + 1) * 512].rearrange("p (c j) -> p c j", c=CT) for i in range(2))
        ups = sb("ups", [P, 2 * RW])
        wa_up = ups[:, 0:RW]
        g_up = ups[:, RW:2 * RW]
        lnx = sb("lnx", [P, 2, RW])
        w_rt = sb("w_rt", [P, KT, NE])
        b_rt = sb("b_rt", [P, NE])
        st = sb("st", [P, 32])
        halves = sb("halves", [P, 12])
        lam = sb("lam", [P, 8, CT])
        dc = sb("dc", [P, CT, NCH])
        gst = sb("gst", [P, 8, TT, NH])
        ast = sb("ast", [P, 4, 2 * XH])
        rt = M[:, 1024:1664].rearrange("p (w i e) -> p w i e", w=10, i=TT)
        top = sb("top", [P, TT, 8])
        key, gate = (M[:, 1664 + i * 64:1728 + i * 64].rearrange("p (i e) -> p i e", i=TT) for i in range(2))

        cnt = sb("cnt", [P, 8])
        steps_i = sb("steps_i", [P, 1], I32)
        PS = [ctx.enter_context(nc.psum_tensor(f"PS{i}", [P, 512], F32)) for i in range(8)]

        def U(i, n=1):
            return A[:, i * UNIT:(i + n) * UNIT]

        def chan(ap):
            return ap.rearrange("p (c t) -> p c t", c=CT)

        def heads(ap):
            return ap.rearrange("p (j h k) -> p j h k", j=2, h=NH)

        def col(name, c=0):
            return par[:, COL[name] + c:COL[name] + c + 1]

        w_in_q = [A[:, q * 4096:(q + 1) * 4096].rearrange("p (c n) -> p c n", c=KT) for q in range(5)]
        w_lora = A[:, 5 * 4096:5 * 4096 + 2048].rearrange("p (c n) -> p c n", c=KT)
        W2 = A[:, 16384:24576].rearrange("p (c n) -> p c n", c=KT)
        W1 = A[:, 8192:16384].rearrange("p (c n) -> p c n", c=KT)
        WB = B[:, :].rearrange("p (c n) -> p c n", c=KT)
        WV = {"xl": (w_in_q[0], 0), "gl": (w_in_q[1], 512), "r": (w_in_q[2], 1024),
              "k": (w_in_q[3], 1536), "v": (w_in_q[4], 2048), "lora": (w_lora, 2560)}
        xl_pad = VX[:, 0:CT * 260].rearrange("p (c t) -> p c t", c=CT)
        mem = R
        lora = R[:, 0, 0:512].rearrange("p (c t) -> p c t", c=2)
        V = VX[:, :].rearrange("p (m d) -> p m d", m=2)

        xc, gx, ga, th = chan(U(0)), chan(U(1)), chan(U(2)), chan(U(3))
        dec = chan(U(4))
        r_c, k_c, v_c = chan(U(5)), chan(U(6)), chan(U(7))
        sig, a_c, Z = chan(U(8)), chan(U(9)), chan(U(10))
        Dt, inv_d, d_prev, kk, zp = chan(U(11)), chan(U(12)), chan(U(13)), chan(U(14)), chan(U(15))
        sq, beta = chan(U(1)), chan(U(2))
        AR = U(3, 2).rearrange("p (w c t) -> p w c t", w=2, c=CT)
        bt_c, kt_c = chan(U(8)), chan(U(15))
        bh_c, kh_c = chan(U(0)), chan(U(1))
        rkk = chan(U(2))
        v_t, bh_t, kh_t = heads(U(10)), heads(U(13)), heads(U(14))
        STb = U(5, 2).rearrange("p (j h w k) -> p j h w k", j=2, h=NH, w=2)
        STk = U(11, 2).rearrange("p (j h w k) -> p j h w k", j=2, h=NH, w=2)
        Nm = heads(U(22))
        N_flat, N_own, T_own, T_tmp, T_flat = (R[:, 1, 0:256], R[:, 0, 0:256], R[:, 0, 256:512], R[:, 0, 512:768],
                                               R[:, 0, 768:1024])

        def pairs(ap):
            return ap.rearrange("p (i h k) -> p i h k", i=TT, h=NH)

        RG, O_bd, T16, Et = pairs(U(16, 2)), pairs(U(18, 2)), pairs(U(20, 2)), pairs(U(22, 2))
        Xs = [pairs(U(0, 2)), pairs(U(7, 2)), pairs(U(16, 2)), pairs(U(7, 2))]
        XW, XU = Xs[3][:, :, :, 0:64], Xs[3][:, :, :, 64:128]
        DI = U(9)[:, 0:512].rearrange("p (n c k) -> p n c k", n=2, c=CT)
        Mt = U(9)[:, 512:1024].rearrange("p (n c k) -> p n c k", n=2, c=CT)
        NS = U(0)[:, 0:768].rearrange("p (n c k) -> p n c k", n=3, c=CT)
        Q = U(1).rearrange("p (n c k) -> p n c k", n=NCH, c=CT)
        St = U(15)[:, 0:512].rearrange("p (n c k) -> p n c k", n=2, c=CT)
        Yuv = heads(U(2))
        Y, Ysq = heads(R[:, 0, :]), heads(R[:, 1, :])
        y_add = heads(U(3))
        g_t = heads(w_bd[:, :])
        A_prob = R[:, :, :].rearrange("p a (b t) -> p (a b) t", b=4)
        A_probt = M[:, 0:1024].rearrange("p (h m t) -> p h m t", h=2, m=2)
        xn = B[:, 0:2048].rearrange("p (i d) -> p i d", i=TT)
        xm = R

        def prob(u):
            return A_prob[:, u, :]

        def prob_t(h):
            return A_probt[:, h % 2]

        ring = [AB[:, s * CHUNK:(s + 1) * CHUNK] for s in range(RING)]
        as_gu = lambda ap: ap.rearrange("p (w g n) -> p w g n", w=2, g=2)
        as_dn = lambda ap: ap.rearrange("p (c g n) -> p c g n", c=2, g=2)
        bgu = MT[0:2, :, :].rearrange("p c t -> p (c t)").rearrange("p (b w n) -> p b w n", b=2, w=2)

        fin_g = lnx[:, :, :].rearrange("p w k -> p (w k)")
        x3n = HT[:, :, :].rearrange("p c t -> p (c t)").rearrange("p (i d) -> p i d", i=TT)

        yt_f = YT[:, :, :].rearrange("p c t -> p (c t)")
        sel = yt_f[:, 0:256].rearrange("p (i w s) -> p i w s", i=TT, w=2)
        self_ = yt_f[:, 256:384].rearrange("p (i s) -> p i s", i=TT)
        sel_t = yt_f[:, 512:768].rearrange("p (i t) -> p i t", i=TT)
        xg = yt_f[:, 1024:1536].rearrange("p (c s) -> p c s", c=KT)
        act_t = yt_f[:, 1536:2048].rearrange("p (f m) -> p f m", f=4)
        vx_f = VX[:, :]
        m_g, m_s, m_u, m_a = (vx_f[:, i * 512:(i + 1) * 512] for i in range(4))
        y_e = R[:, 0, 0:512]
        picked_rows = R[:, 0, 512:1024]
        fin = R[:, :, :]

        dram = {k: (v[0] if k not in ("x", "mem", "final_norm_g") else v) for k, v in a.items()}
        krows = lambda w: w.rearrange("(c p) n -> p c n", p=P)
        par_loads = []
        for name, rows in PARAM_ROWS:
            src = dram[name] if len(dram[name].shape) == 1 else dram[name].rearrange("a b -> (a b)")
            par_loads.append((COL[name], rows, src.rearrange("(r p) -> r p", p=P)))

        scratch = nc.dram_tensor("scratch", (2, P, 2 * P), F32, kind="Internal").ap()
        block = ctx.enter_context(nc.Block())

        @block.sync
        def _(sp):
            for i in range(TT):
                sp.dma_start(X[:, i, :], dram["x"][0, i * P:(i + 1) * P, :]).then_inc(S(f"ld_x{i}"), 16)

            def load_in(name):
                w, at = WV[name]
                n = w.shape[2]
                sp.dma_start(w, krows(dram["w_in"][:, at:at + n])).then_inc(S("ld_" + name), 16)

            load_in("xl")
            for r0, rows, src in par_loads[PAR_SPLIT:]:
                sp.dma_start(par_rows[r0:r0 + rows, :], src).then_inc(S("ld_par"), 16)
            load_in("gl")
            sp.dma_start(mem[:], dram["mem"][0].rearrange("(i p) d -> p i d", p=P)).then_inc(S("ld_mem"), 16)
            for name in ("r", "k", "lora", "v"):
                load_in(name)
            sp.dma_start(wa_up[0:64, :], dram["rwkv_w_up"]).then_inc(S("ld_lora_up"), 16)
            sp.dma_start(wa_up[64:128, :], dram["rwkv_a_up"]).then_inc(S("ld_lora_up"), 16)
            sp.dma_start(g_up[:], dram["rwkv_g_up"]).then_inc(S("ld_lora_up"), 16)
            sp.dma_start(lnx[:, 0, :], dram["rwkv_lnx_g"].partition_broadcast(P)).then_inc(S("ld_late"), 16)
            sp.dma_start(lnx[:, 1, :], dram["rwkv_lnx_b"].partition_broadcast(P)).then_inc(S("ld_late"), 16)
            sp.dma_start(b_rt[:], dram["b_router"].partition_broadcast(P)).then_inc(S("ld_late"), 16)
            sp.dma_start(w_rt[:], krows(dram["w_router"])).then_inc(S("ld_late"), 16)
            sp.wait_ge(*at("t_x", 4))
            sp.dma_start(WB, krows(dram["xa_wk"])).then_inc(S("ld_wk"), 16)
            sp.wait_ge(*at("pe_k", KT))
            sp.dma_start(WB, krows(dram["xa_wv"])).then_inc(S("ld_wv"), 16)
            blocks = [slice(BL * g, BL * g + BL) for g in range(P // BL)]
            sp.wait_ge(*at("N_flat", 1))
            sp.dma_start(scratch[0], N_flat).then_inc(S("st_N"), 16)
            sp.wait_ge(*at("st_N", 16))
            for g in blocks:
                sp.dma_start(N_own[g].rearrange("x (t s) -> x t s", t=BL),
                             scratch[0, g].rearrange("t (x s) -> x t s", x=BL)).then_inc(S("ld_N"), 16)
            sp.wait_ge(*at("T_flat", 1))
            sp.dma_start(scratch[1], T_own).then_inc(S("st_T"), 16)
            sp.wait_ge(*at("st_T", 16))
            for g in blocks:
                sp.dma_start(T_flat[g].rearrange("s (x t) -> s x t", x=BL),
                             scratch[1, g].rearrange("x (s t) -> s x t", s=BL)).then_inc(S("ld_T"), 16)
            sp.wait_ge(*at("X3_ps", 4))
            sp.dma_start(W2, krows(dram["w_out"])).then_inc(S("ld_wo1"), 16)
            sp.wait_ge(*at("yT_ps", 2))
            sp.dma_start(W1, krows(dram["xa_wq"])).then_inc(S("ld_wq"), 16)
            sp.wait_ge(*at("pe_v", 4))
            sp.dma_start(WB, krows(dram["xa_wo"])).then_inc(S("ld_wo2"), 16)

            sp.dma_start(fin_g, a["final_norm_g"].partition_broadcast(P)).then_inc(S("ld_fing"), 16)

            def load_chunk(e, m):
                q = m % PER_EXPERT
                if q < GU_CHUNKS:
                    src, n = dram["w_gu"][bass.ds(e, 1), q * P:(q + 1) * P, :], 1
                else:
                    k = 2 * (q - GU_CHUNKS)
                    src, n = dram["w_dn"][bass.ds(e, 1), k * P:(k + 2) * P, :], 2
                sp.dma_start(ring[m % RING].rearrange("p (c n) -> p c n", c=n),
                             src[0].rearrange("(c p) n -> p c n", p=P)).then_inc(S(f"ld_ring{m % RING}"), 16)

            def load_bgu(e, b):
                src = dram["b_gu"][bass.ds(e, 1), :].rearrange("p (w g n) -> p g w n", w=2, g=2)
                sp.dma_start(bgu[:, b], src[0]).then_inc(S(f"ld_bgu{b}"), 16)

            for m in range(0, 4):
                load_chunk(0, m)
            sp.wait_ge(*at("pe_wout", 4))
            for m in range(8, 12):
                load_chunk(0, m)
            sp.wait_ge(*at("pe_q", KT))
            for m in range(4, 8):
                load_chunk(0, m)
            sp.wait_ge(*at("pe_wo", 4))
            for m in range(12, 16):
                load_chunk(m // PER_EXPERT, m)
            sp.wait_ge(*at("y_cleared", 1))
            for g in range(2):
                sp.dma_start(y_e[64 * g:64 * g + NE, :], dram["b_dn"][:, g * 512:(g + 1) * 512]).then_inc(S("ld_bdn"), 16)
            sp.wait_ge(*at("rl_ps", 2))
            load_bgu(0, 0)
            load_bgu(1, 1)

            def load_group(i, first):
                for m in range(first, GROUP * PER_EXPERT):
                    e = (i % (NE // GROUP)) * GROUP + m // PER_EXPERT
                    if m % PER_EXPERT == 0:
                        sp.wait_ge(S("used_b"), i * GROUP + (m // PER_EXPERT - 1))
                        load_bgu(e, m // PER_EXPERT % 2)
                    sp.wait_ge(S("used_ring"), i * (GROUP * PER_EXPERT) + (m - RING + 1))
                    load_chunk(e, m)

            load_group(0, RING)
            with sp.Fori(1, NE // GROUP) as i:
                load_group(i, 0)
            sp.wait_ge(*at("steps", 1))
            groups = sp.value_load(steps_i[0:1, 0:1], min_val=NE // GROUP, max_val=NE * ROUNDS // GROUP)
            with sp.If(groups > NE // GROUP):
                with sp.Fori(NE // GROUP, groups) as i:
                    load_group(i, 0)
            for i in range(TT):
                sp.wait_ge(*at("y_out", i + 1))
                sp.dma_start(out[0, i * P:(i + 1) * P, :], fin[:, i, :]).then_inc(S("stored"), 16)
            sp.wait_ge(*at("stored", 16 * TT))

        @block.gpsimd
        def _(pool):
            pg = nc.gpsimd
            n = [0]

            def c(ins):
                n[0] += 1
                ins.then_inc(S("consts"), 1)
                pool.wait_ge(*at("consts", n[0]))

            c(pg.memset(neg_half[:], -0.5))
            c(pg.memset(ident[:], 0.0))
            c(pg.affine_select(out=ident[:], in_=ident[:], compare_op=ALU.not_equal, fill=1.0, base=0,
                               pattern=[[-1, P]], channel_multiplier=1))
            pool.sem_inc(S("ident"), 1)

            def inv_root(dst, ss, shift, name, half, ss_2=None):
                if ss_2 is None:
                    c(pg.tensor_scalar(dst, ss, shift, None, ALU.add))
                else:
                    c(pg.tensor_scalar(dst, ss, ss_2, shift, ALU.add, ALU.add))
                pg.tensor_tensor(dst, dst, half, ALU.pow).then_inc(S(name), 1)

            for i in range(TT):
                pool.wait_ge(*at("ss_x", i + 1))
                inv_root(st[:, 2 + i:3 + i], st[:, i:i + 1], D * EPS, "rs_x", neg_half[:, 0:1])
            for w in (wx_bd, wa_bd):
                pg.memset(w, 0.0).then_inc(S("bd_zero"), 1)
            pool.wait_ge(*at("bd_zero", 2))
            for name, w in (("lru_wx", wx_bd), ("lru_wa", wa_bd)):
                for half in range(2):
                    src = dram[name].rearrange("(c w) i j -> w i c j", w=2)[half]
                    pool.dma_start(w[64 * half:64 * half + 64, :, 64 * half:64 * half + 64], src).then_inc(S("ld_lruw"), 16)
            c(pg.memset(ones[:], 1.0))
            c(pg.memset(before[:], 1.0))
            c(pg.affine_select(out=before[:], in_=before[:], compare_op=ALU.is_gt, fill=0.0, base=0,
                               pattern=[[1, P]], channel_multiplier=-1))
            c(pg.memset(head_ones[:], 0.0))
            for h in range(2):
                c(pg.memset(head_ones[64 * h:64 * h + 64, 64 * h:64 * h + 64], 1.0))
            c(pg.memset(half_rows[:], 1.0))
            c(pg.affine_select(out=half_rows[:], in_=half_rows[:], compare_op=ALU.is_ge, fill=0.0, base=0,
                               pattern=[[1, P]], channel_multiplier=-64))
            c(pg.affine_select(out=half_rows[:], in_=half_rows[:], compare_op=ALU.is_gt, fill=0.0, base=64,
                               pattern=[[-1, P]], channel_multiplier=64))
            c(pg.memset(restart[:], 1.0))
            c(pg.memset(restart[:].rearrange("p (n t) -> p n t", t=CH)[:, :, 0:1], 0.0))
            c(pg.memset(eye8, 0.0))
            for h in range(2):
                s = slice(64 * h, 64 * h + 64)
                c(pg.affine_select(out=eye8[s], in_=eye8[s], compare_op=ALU.not_equal, fill=1.0, base=0,
                                   pattern=[[0, 8], [-1, 64]], channel_multiplier=1))
            for m in (mask_ar, mask_n, mask_o, own_block):
                c(pg.memset(m, 1.0))
            c(pg.memset(eye16, 0.0))
            c(pg.affine_select(out=eye16, in_=eye16, compare_op=ALU.not_equal, fill=1.0, base=0,
                               pattern=[[1, BL], [-1, BL]], channel_multiplier=0))
            for h in range(2):
                s = slice(64 * h, 64 * h + 64)
                for w, op in ((0, ALU.is_gt), (1, ALU.is_ge)):
                    v = mask_ar[s, :, w, :]
                    c(pg.affine_select(out=v, in_=v, compare_op=op, fill=0.0, base=0,
                                       pattern=[[0, 4], [1, 64]], channel_multiplier=-1))
                v = mask_o[s].rearrange("p e (b j) -> p e b j", j=16)
                c(pg.affine_select(out=v, in_=v, compare_op=ALU.is_ge, fill=0.0, base=-16,
                                   pattern=[[0, 8], [-16, 4], [0, 16]], channel_multiplier=1))
                v = mask_n[s].rearrange("p e (b j) -> p e b j", j=16)
                c(pg.affine_select(out=v, in_=v, compare_op=ALU.is_gt, fill=0.0, base=16,
                                   pattern=[[0, 8], [16, 4], [0, 16]], channel_multiplier=-1))
                c(pg.affine_select(out=mask_n[s], in_=mask_n[s], compare_op=ALU.is_gt, fill=0.0, base=0,
                                   pattern=[[0, 8], [-1, 64]], channel_multiplier=1))
                c(pg.affine_select(out=own_block[s], in_=own_block[s], compare_op=ALU.is_ge, fill=0.0, base=0,
                                   pattern=[[-BL, CH // BL]], channel_multiplier=1))
                c(pg.affine_select(out=own_block[s], in_=own_block[s], compare_op=ALU.is_gt, fill=0.0, base=BL,
                                   pattern=[[BL, CH // BL]], channel_multiplier=-1))
            c(pg.iota(slot_no[:], pattern=[[0, 2], [1, SLOTS]], base=0, channel_multiplier=0,
                      allow_small_or_imprecise_dtypes=True))
            pool.sem_inc(S("consts_all"), 1)
            pool.wait_ge(*at("ss_mem", 2))
            inv_root(st[:, 6:8], st[:, 4:6], D * EPS, "rs_mem", neg_half[:, 0:2])
            pool.wait_ge(*at("u_v", CT))
            pg.memset(U(18, 4), 0.0).then_inc(S("bd_cleared"), 1)
            pool.wait_ge(*at("gn_ss", 1))
            inv_root(gst[:, 4], gst[:, 2], HEAD * GN_EPS, "gn_rs", neg_half[:, :].rearrange("p (i h) -> p i h", i=TT))
            for r in range(2):
                if r == 1:
                    pool.wait_ge(*at("pT_ps", XH))
                    pg.memset(y_e, 0.0).then_inc(S("y_cleared"), 1)
                for i in range(TT):
                    pool.wait_ge(S(f"ss_x{r + 1}"), 2 * i + 2)
                    inv_root(st[:, 10 + 4 * r + i:11 + 4 * r + i], halves[:, 4 * r + 2 * i:4 * r + 2 * i + 1], D * EPS,
                             f"rs_x{r + 1}", neg_half[:, 0:1], halves[:, 4 * r + 2 * i + 1:4 * r + 2 * i + 2])
            for i in range(TT):
                pool.wait_ge(S("ss_x3"), 2 * i + 2)
                inv_root(st[:, 18 + i:19 + i], halves[:, 8 + 2 * i:9 + 2 * i], D * EPS, "rs_x3", neg_half[:, 0:1],
                         halves[:, 9 + 2 * i:10 + 2 * i])

        @block.scalar
        def _(act):
            ac = nc.scalar
            made = {}

            def done(ins, name):
                sem = S(name)
                made[sem.name] = made.get(sem.name, 0) + 1
                ins.then_inc(sem, 1)
                act.wait_ge(sem, made[sem.name])

            for r0, rows, src in par_loads[:PAR_SPLIT]:
                act.dma_start(par_rows[r0:r0 + rows, :], src).then_inc(S("ld_par"), 16)

            def k_copy(lo, hi):
                for c in range(lo, hi):
                    act.wait_ge(*at("pe_k", c + 1))
                    done(ac.copy(HT[:, c, :], PS[6 + c % 2][:, 0:T]), "K")

            def v_copy(lo, hi):
                for q in range(lo, hi):
                    act.wait_ge(*at("pe_v", q + 1))
                    done(ac.copy(V[:, q // 2, (q % 2) * 512:(q % 2) * 512 + 512], PS[6 + q % 2][:, :]), "V")

            for i in range(TT):
                act.wait_ge(*at(f"ld_x{i}", 16))
                done(ac.activation(YT[:, 4 * i:4 * i + 4, :], X[:, i, :].rearrange("p (c t) -> p c t", c=4), ACT.Square,
                                   accum_out=st[:, i:i + 1]), "ss_x")
            act.wait_ge(*at("par", 1))
            act.wait_ge(*at("t_x", 4))
            for c in TURNED_A:
                done(ac.activation(HT[:, c, :], PS[c // 2][:, (c % 2) * 256:(c % 2) * 256 + 256], ACT.Identity,
                                   scale=col("norm_mix_g", c)), "hT_a")
            act.wait_ge(*at("lam_abs", 1))
            done(ac.activation(lam[:, 1, :], lam[:, 0, :], ACT.Exp, scale=-1.0), "lam_e")
            act.wait_ge(*at("lam_w", 1))
            done(ac.activation(lam[:, 3, :], lam[:, 2, :], ACT.Ln), "lam_ln")
            act.wait_ge(*at("xl_pads", 1))
            for c in range(CT):
                act.wait_ge(*at("u_xl", c + 1))
                done(ac.copy(xl_pad[:, c, 3:3 + T], PS[4 + c][:, 0:T]), "xl")
            act.wait_ge(*at("ld_mem", 16))
            for i in range(TT):
                done(ac.activation(YT[:, 4 * i:4 * i + 4, :], mem[:, i, :].rearrange("p (c t) -> p c t", c=4), ACT.Square,
                                   accum_out=st[:, 4 + i:5 + i]), "ss_mem")
            for c in range(CT):
                act.wait_ge(*at("u_gl", c + 1))
                done(ac.activation(YT[:, c, :], PS[4 + c][:, 0:T], ACT.Gelu_apprx_tanh), "gelu")

            def shift_a(name, dst, mu0):
                n = 2 if name == "lora" else CT
                for c in range(n):
                    act.wait_ge(*at("u_" + name, c + 1))
                    b = PS[4 + c]
                    done(ac.activation(dst[:, c, :], b[:, 0:T], ACT.Identity, scale=omu[:, mu0 + c:mu0 + c + 1]),
                         "sa_" + name)

            act.wait_ge(*at("omu", 1))
            shift_a("r", r_c, 0)
            act.wait_ge(*at("t_mem", 4))
            for c in TURNED_A:
                done(ac.activation(MT[:, c, :], PS[c // 2][:, (c % 2) * 256:(c % 2) * 256 + 256], ACT.Identity,
                                   scale=col("norm_mem_g", c)), "mT_a")
            shift_a("k", k_c, 4)
            for c in range(CT):
                act.wait_ge(*at("lru_gates", c + 1))
                done(ac.activation(gx[:, c, :], PS[c][:, 0:T], ACT.Sigmoid, bias=col("lru_bx", c)), "gx")
                done(ac.activation(ga[:, c, :], PS[c][:, T:2 * T], ACT.Sigmoid, bias=col("lru_ba", c)), "ga")
            shift_a("lora", lora, 12)
            act.wait_ge(*at("sv_lora", 2))
            done(ac.activation(lora[0:64, 0, :], lora[0:64, 0, :], ACT.Tanh), "lora_f")
            done(ac.activation(lora[:, 1, :], lora[:, 1, :], ACT.Sigmoid), "lora_f")
            act.wait_ge(*at("lam_rate", 2))
            for c in range(CT):
                done(ac.activation(th[:, c, :], ga[:, c, :], ACT.Tanh, scale=lam[:, 6, c:c + 1]), "lru_th")
            for c in range(CT):
                done(ac.activation(dec[:, c, :], ga[:, c, :], ACT.Exp, scale=lam[:, 7, c:c + 1]), "lru_dec")
            shift_a("v", v_c, 8)
            act.wait_ge(*at("lru_b2", 1))
            done(ac.activation(th, th, ACT.Sqrt), "lru_root")
            for c in range(CT):
                act.wait_ge(*at("z_a", 1))
                done(ac.activation(sig[:, c, :], PS[c // 2][:, (c % 2) * T:(c % 2) * T + T], ACT.Sigmoid,
                                   bias=col("rwkv_w0", c)), "sig")
            for c in range(CT):
                done(ac.activation(a_c[:, c, :], PS[2 + c // 2][:, (c % 2) * T:(c % 2) * T + T], ACT.Sigmoid,
                                   bias=col("rwkv_a0", c)), "a_c")
            act.wait_ge(*at("g_ps", 2))
            for i in range(TT):
                done(ac.copy(g_t[:, i], PS[4 + i][:, :].rearrange("p (h k) -> p h k", h=NH)), "g_t")
            act.wait_ge(*at("kk", 1))
            act.wait_ge(*at("lru_in", 1))
            done(ac.activation(sq, kk, ACT.Square), "kk_sq")
            k_copy(0, 2)
            for c in range(2):
                act.wait_ge(*at("kk_ss", c + 1))
                done(ac.activation(U(1)[:, c * 512:(c + 1) * 512], PS[c][:, :], ACT.Sqrt), "kk_rn")
            act.wait_ge(*at("Z", CT))
            done(ac.activation(Dt, Z, ACT.Exp, scale=-DECAY), "exps")
            done(ac.activation(inv_d, Z, ACT.Exp, scale=DECAY), "exps")
            act.wait_ge(*at("zp", 1))
            done(ac.activation(d_prev, zp, ACT.Exp, scale=-DECAY), "exps")



            k_copy(2, 7)
            for name, dst in (("tok_v_ps", v_t), ("tok_al_ps", RG[:, :, :, 0:64])):
                if name == "tok_al_ps":
                    k_copy(7, 8)
                for i in range(TT):
                    act.wait_ge(*at(name, i + 1))
                    done(ac.copy(dst[:, i], PS[i][:, :].rearrange("p (h k) -> p h k", h=NH)), "tok")
            act.wait_ge(*at("G_ps", 1))
            for j in range(2):
                for np_ in range(2):
                    s = slice(64 * np_, 64 * np_ + 64)
                    done(ac.copy(RG[s, j ^ np_, :, 64:128], PS[4 + j][s, :].rearrange("p (h k) -> p h k", h=NH)), "G")
            v_copy(0, 2)
            for g in range(4):
                act.wait_ge(*at("Et_ps", g + 1))
                done(ac.copy(Et[:, g // 2, 4 * (g % 2):4 * (g % 2) + 4, :],
                             PS[g][:, :].rearrange("p (h k) -> p h k", h=4)), "Et")
            act.wait_ge(*at("Yuv_ps", 1))
            for j in range(2):
                for np_ in range(2):
                    s = slice(64 * np_, 64 * np_ + 64)
                    done(ac.copy(Yuv[s, j ^ np_], PS[2 + j][s, :].rearrange("p (h k) -> p h k", h=NH)), "Yuv")
            for n in (1, 2):
                act.wait_ge(*at("S_ps", n))
                done(ac.copy(St[64:128, n - 1], PS[1][64:128, 0:256].rearrange("p (c k) -> p c k", c=CT)), "St_a")
            v_copy(2, 4)
            act.wait_ge(*at("yT_ps", 2))
            done(ac.copy(YT[:, 6:8, :], PS[1][:, :].rearrange("p (c t) -> p c t", c=2)), "yT_a")

            def square(name, r):
                for u in range(4):
                    act.wait_ge(*at(name, u + 1))
                    done(ac.activation(R[:, 1, 0:512], X[:, u // 2, (u % 2) * 512:(u % 2) * 512 + 512],
                                       ACT.Square, accum_out=halves[:, 4 * r - 4 + u:4 * r - 3 + u]), f"ss_x{r}")

            square("x1", 1)

            def turned(ps_name, gain, made_name):
                for c in TURNED_A:
                    act.wait_ge(*at(ps_name, c // 2 + 1))
                    done(ac.activation(MT[:, c, :], PS[c // 2][:, (c % 2) * 256:(c % 2) * 256 + 256], ACT.Identity,
                                       scale=col(gain, c)), made_name)

            turned("t_x1", "norm_xa_g", "x1T_a")
            for c in range(1, KT, 2):
                act.wait_ge(*at("pe_q", c + 1))
                done(ac.activation(YT[:, c, :], PS[4 + c % 4][:, 0:T], ACT.Identity, scale=float(XD) ** -0.5), "q_a")
            def numerators(lo, hi):
                for u in range(lo, hi):
                    act.wait_ge(*at("nmax", u + 1))
                    done(ac.activation(prob(u), PS[u % 4][:, 0:T], ACT.Exp, bias=ast[:, 1, u:u + 1],
                                       accum_out=ast[:, 2, u:u + 1]), "expd")
                    if u >= 1:
                        normed(u - 1)

            def normed(u):
                act.wait_ge(*at("inv_sum", u + 1))
                done(ac.activation(prob(u), prob(u), ACT.Identity, scale=ast[:, 3, u:u + 1]), "prob")

            def turned_prob(h):
                act.wait_ge(*at("pT_ps", h + 1))
                done(ac.copy(prob_t(h)[:, 1], PS[4 + 2 * (h % 2) + 1][:, 0:T]), "pT_a")

            def head_out(h):
                act.wait_ge(*at("o_ps", 2 * h + 2))
                done(ac.copy(YT[:, 2 * h + 1, :], PS[2 * (h % 2) + 1][:, 0:T]), "oT_a")

            numerators(0, 6)
            turned_prob(0)
            numerators(6, 8)
            normed(7)
            turned_prob(1)
            head_out(0)
            turned_prob(2)
            head_out(1)
            turned_prob(3)
            head_out(2)
            head_out(3)
            square("x2", 2)
            turned("t_x2", "norm_ffn_g", "x2T_a")
            for i in range(TT):
                act.wait_ge(*at("nl", 1))
                done(ac.activation(rt[:, 1, i, :], rt[:, 0, i, :], ACT.Exp, bias=top[:, i, 7:8]), "r_exp")


            act.wait_ge(S("rows_ps"), 1)
            ac.copy(picked_rows, PS[7][:, :]).then_inc(S("rows_sb"), 1)
            act.wait_ge(*at("steps", 1))
            groups = act.value_load(steps_i[0:1, 0:1], min_val=NE // GROUP, max_val=NE * ROUNDS // GROUP)
            with act.Fori(0, groups * GROUP) as i:
                act.wait_ge(S("gate_in"), i + 1)
                ac.activation(m_s, m_g, ACT.Sigmoid, scale=ALPHA).then_inc(S("gate_sig"), 1)
                act.wait_ge(S("turned"), i + 2)
                ac.copy(sel_t, PS[6][:, 0:256].rearrange("p (i t) -> p i t", i=TT)).then_inc(S("sel_t"), 1)
                act.wait_ge(S("used_ring"), (i + 1) * PER_EXPERT)
                ac.copy(y_e, PS[6][:, :]).then_inc(S("y_sb"), 1)
            for u in range(4):
                act.wait_ge(*at("x3", u + 1))
                done(ac.activation(yt_f[:, 1024:1536], X[:, u // 2, (u % 2) * 512:(u % 2) * 512 + 512], ACT.Square,
                                   accum_out=halves[:, 8 + u:9 + u]), "ss_x3")

        @block.vector
        def _(dve):
            v = nc.vector
            made = {}

            def done(ins, name="dve_step"):
                sem = S(name)
                made[sem.name] = made.get(sem.name, 0) + 1
                ins.then_inc(sem, 1)
                dve.wait_ge(sem, made[sem.name])

            done(v.memset(VX[:], 0.0), "xl_pads")
            for i in range(TT):
                dve.wait_ge(*at("rs_x", i + 1))
                done(v.tensor_scalar(xn[:, i, :], X[:, i, :],
                                     st[:, 2 + i:3 + i], ROOT_D, ALU.mult, ALU.mult), "xn")
            dve.wait_ge(*at("par_ps", 1))
            done(v.tensor_copy(par[:, 0:NPAR], PS[7][:, 0:NPAR]), "par")
            dve.wait_ge(*at("t_x", 3))
            for c in TURNED_V:
                done(v.tensor_scalar(HT[:, c, :], PS[c // 2][:, (c % 2) * 256:(c % 2) * 256 + 256],
                                     col("norm_mix_g", c), None, ALU.mult), "hT_v")
            done(v.tensor_scalar(omu[:], par[:, COL["rwkv_mu"]:COL["rwkv_mu"] + 14], -1.0, 1.0, ALU.mult, ALU.add), "omu")
            lm = par[:, COL["lru_lambda"]:COL["lru_lambda"] + CT]
            done(v.tensor_scalar(lam[:, 4, :], lm, -1.0, None, ALU.mult))
            done(v.tensor_tensor(lam[:, 0, :], lam[:, 4, :], lm, ALU.max), "lam_abs")
            dve.wait_ge(*at("lam_e", 1))
            done(v.tensor_scalar(lam[:, 2, :], lam[:, 1, :], 1.0, None, ALU.add), "lam_w")
            done(v.tensor_scalar(lam[:, 5, :], lam[:, 2, :], -1.0, None, ALU.add))

            dve.wait_ge(*at("lam_ln", 1))
            done(v.tensor_scalar(lam[:, 0, :], lam[:, 5, :], 0.0, None, ALU.is_equal))
            done(v.tensor_tensor(lam[:, 5, :], lam[:, 5, :], lam[:, 0, :], ALU.add))
            done(v.reciprocal(lam[:, 5, :], lam[:, 5, :]))
            done(v.tensor_tensor(lam[:, 3, :], lam[:, 3, :], lam[:, 5, :], ALU.mult))
            done(v.tensor_tensor(lam[:, 3, :], lam[:, 3, :], lam[:, 0, :], ALU.add))
            done(v.tensor_tensor(lam[:, 3, :], lam[:, 3, :], lam[:, 1, :], ALU.mult))
            done(v.scalar_tensor_tensor(out=lam[:, 3, :], in0=lam[:, 4, :], scalar=0.0, in1=lam[:, 3, :],
                                        op0=ALU.max, op1=ALU.add))
            done(v.tensor_scalar(lam[:, 6, :], lam[:, 3, :], 8.0, None, ALU.mult), "lam_rate")
            done(v.tensor_scalar(lam[:, 7, :], lam[:, 3, :], -8.0, None, ALU.mult), "lam_rate")
            dve.wait_ge(*at("u_gl", CT))
            for c in range(CT):
                dve.wait_ge(*at("xl", c + 1))
                done(v.tensor_scalar(xc[:, c, :], xl_pad[:, c, 0:T], col("conv_w", c), col("conv_b", c),
                                     ALU.mult, ALU.add), "conv")
                for j in range(1, 4):
                    done(v.scalar_tensor_tensor(out=xc[:, c, :], in0=xl_pad[:, c, j:j + T],
                                                scalar=col("conv_w", 4 * j + c), in1=xc[:, c, :],
                                                op0=ALU.mult, op1=ALU.add), "conv")

            def shift_v(name, dst, mu0):
                n = 2 if name == "lora" else CT
                for c in range(n):
                    dve.wait_ge(*at("sa_" + name, c + 1))
                    done(v.scalar_tensor_tensor(out=dst[:, c, 1:T], in0=PS[4 + c][:, 0:T - 1],
                                                scalar=col("rwkv_mu", mu0 + c), in1=dst[:, c, 1:T],
                                                op0=ALU.mult, op1=ALU.add), "sv_" + name)

            dve.wait_ge(*at("rs_mem", 1))
            for i in range(TT):
                done(v.tensor_scalar(mem[:, i, :], mem[:, i, :], st[:, 6 + i:7 + i], ROOT_D, ALU.mult, ALU.mult), "memn")
            shift_v("r", r_c, 0)
            dve.wait_ge(*at("t_mem", 3))
            for c in TURNED_V:
                done(v.tensor_scalar(MT[:, c, :], PS[c // 2][:, (c % 2) * 256:(c % 2) * 256 + 256],
                                     col("norm_mem_g", c), None, ALU.mult), "mT_v")
            shift_v("k", k_c, 4)
            dve.wait_ge(*at("u_k", CT))
            for c in range(CT):
                done(v.tensor_scalar(kk[:, c, :], k_c[:, c, :], col("rwkv_k_k", c), None, ALU.mult),
                     "kk" if c == CT - 1 else "dve_step")
            shift_v("lora", lora, 12)
            dve.wait_ge(*at("lru_dec", CT))
            done(v.tensor_scalar(ga, th, 1.0, None, ALU.add))
            done(v.reciprocal(ga, ga))
            done(v.scalar_tensor_tensor(out=U(3), in0=U(3), scalar=2.0, in1=U(2), op0=ALU.mult, op1=ALU.mult))
            done(v.tensor_tensor(gx, gx, xc, ALU.mult), "lru_b2")
            shift_v("v", v_c, 8)
            dve.wait_ge(*at("lru_root", 1))
            done(v.tensor_tensor(th, th, gx, ALU.mult), "lru_in")
            for c in range(CT):
                done(v.tensor_tensor_scan(ga[:, c, :], dec[:, c, :], th[:, c, :], 0.0, ALU.mult, ALU.add))
            done(v.tensor_tensor(YT[:, 0:CT, :], YT[:, 0:CT, :], ga, ALU.mult), "y_lru")
            dve.wait_ge(*at("sig", CT))
            for c in range(CT):
                done(v.tensor_tensor_scan(Z[:, c, :], restart[:], sig[:, c, :], 0.0, ALU.mult, ALU.add), "Z")
            done(v.tensor_tensor(zp, Z, sig, ALU.subtract), "zp")
            dve.wait_ge(*at("kk_rn", 2))
            done(v.tensor_scalar(sq, sq, 1e-12, None, ALU.max))
            done(v.reciprocal(sq, sq))
            done(v.tensor_tensor(kk, kk, sq, ALU.mult))
            dve.wait_ge(*at("a_c", CT))
            done(v.tensor_tensor(beta, kk, a_c, ALU.mult))
            dve.wait_ge(*at("exps", 3))
            done(v.scalar_tensor_tensor(out=U(3), in0=U(14), scalar=-1.0, in1=U(13), op0=ALU.mult, op1=ALU.mult), "al_c")
            done(v.tensor_tensor(bt_c, beta, inv_d, ALU.mult), "bt_c")
            for c in range(CT):
                done(v.tensor_scalar(a_c[:, c, :], a_c[:, c, :], 1.0, col("rwkv_k_a", c), ALU.subtract, ALU.mult))
            done(v.scalar_tensor_tensor(out=U(6), in0=U(9), scalar=1.0, in1=U(6), op0=ALU.add, op1=ALU.mult))
            done(v.tensor_tensor(kt_c, k_c, inv_d, ALU.mult), "kt_c")
            last_d = Dt.rearrange("p c (n s) -> p c n s", s=CH)[:, :, :, CH - 1:CH]
            done(v.tensor_copy(dc[:].unsqueeze(3), last_d))
            dcb = dc[:].unsqueeze(3).broadcast_to([P, CT, NCH, CH])
            done(v.tensor_tensor(bh_c.rearrange("p c (n s) -> p c n s", s=CH),
                                 bt_c.rearrange("p c (n s) -> p c n s", s=CH), dcb, ALU.mult), "bh_c")
            done(v.tensor_tensor(kh_c.rearrange("p c (n s) -> p c n s", s=CH),
                                 kt_c.rearrange("p c (n s) -> p c n s", s=CH), dcb, ALU.mult), "kh_c")
            done(v.tensor_tensor(AR[:, 1], r_c, Dt, ALU.mult), "r_til")
            by_half = lambda ap: ap.rearrange("p (c e) k -> p c e k", e=2)
            for i in range(TT):
                dve.wait_ge(*at("n_ps", 2 * i + 2))
                for hp in range(2):
                    done(v.tensor_tensor(by_half(Nm[:, i])[:, :, hp], PS[2 + 2 * i + hp][:, 0:256].rearrange("p (c k) -> p c k", c=CT),
                                         mask_n[:, 0:4, :], ALU.mult))
            done(v.tensor_reduce(N_flat.rearrange("p (x s) -> p x s", x=BL),
                                 U(22).rearrange("p (x b s) -> p x s b", b=CH // BL, s=BL), AX_X, ALU.add), "N_flat")
            dve.wait_ge(*at("bd_cleared", 1))
            for i in range(TT):
                for hp in range(2):
                    for np_ in range(2):
                        s = slice(64 * np_, 64 * np_ + 64)
                        done(v.tensor_tensor(by_half(O_bd[s, i])[:, :, hp, s],
                                             PS[2 + 2 * i + hp][s, 0:256].rearrange("p (c k) -> p c k", c=CT),
                                             mask_o[s, 0:4, :], ALU.mult), "O")
            for c in range(CT):
                done(v.scalar_tensor_tensor(out=rkk[:, c, :], in0=r_c[:, c, :], scalar=col("rwkv_r_k", c),
                                            in1=k_c[:, c, :], op0=ALU.mult, op1=ALU.mult), "rkk")
            for name, dst, b in (("tok_bh_ps", bh_t, 2), ("tok_kh_ps", kh_t, 4)):
                for i in range(TT):
                    dve.wait_ge(*at(name, i + 1))
                    done(v.tensor_copy(dst[:, i], PS[b + i][:, :].rearrange("p (h k) -> p h k", h=NH)), "tok_v")
            for u in range(8):
                kind, i, hp = u // 4, (u // 2) % 2, u % 2
                dst = (STb, STk)[kind]
                dve.wait_ge(*at("st_ps", 2 * (u // 2) + 2))
                done(v.tensor_tensor(dst[:, i].rearrange("p (c e) w k -> p c e w k", e=2)[:, :, hp],
                                     PS[ST_BANKS[u // 2] + u % 2][:, :].rearrange("p (c w k) -> p c w k", c=CT, w=2),
                                     mask_ar, ALU.mult), "st")
            dve.wait_ge(*at("bonus_ps", 1))
            done(v.tensor_copy(gst[:, 7], PS[2][:, 0:TT * NH].rearrange("p (i h) -> p i h", i=TT)), "bonus")
            own_n = N_own.rearrange("p (t s) -> p t s", t=BL)
            own_t, tmp = (ap.rearrange("p (s t) -> p s t", s=BL) for ap in (T_own, T_tmp))
            done(v.tensor_copy(own_t, eye16))
            dve.wait_ge(*at("ld_N", 16 * (P // BL)))
            for k in range(BL - 1):
                size = [P, k + 1, BL - 1 - k]
                new, part = own_t[:, 0:k + 1, k + 1:BL], tmp[:, 0:k + 1, k + 1:BL]
                n_col = own_n[:, k + 1:BL, k:k + 1].rearrange("p t s -> p s t").broadcast_to(size)
                done(v.tensor_tensor(part, own_t[:, 0:k + 1, k:k + 1].broadcast_to(size), n_col, ALU.mult))
                done(v.tensor_tensor(new, new, part, ALU.add), "T_flat" if k == BL - 2 else "dve_step")
            for n in (1, 2):
                done(v.tensor_tensor(DI[:, n - 1], eye8[:, 0:CT, :],
                                     dc[:, :, n:n + 1].broadcast_to([P, CT, CH]), ALU.mult), "DI")
            bc = lambda x: x.unsqueeze(3).broadcast_to([P, TT, NH, HEAD])
            lx = lambda w: lnx[:, w, :].rearrange("p (h k) -> p h k", h=NH)
            dve.wait_ge(*at("ld_late", 64))
            dve.wait_ge(*at("tok", 2))
            dve.wait_ge(*at("g_t", 2))
            done(v.tensor_tensor(y_add, v_t, bc(gst[:, 7]), ALU.mult))
            for i in range(TT):
                done(v.tensor_tensor(y_add[:, i], y_add[:, i], lx(1), ALU.add))
            done(v.tensor_tensor(y_add, y_add, g_t, ALU.mult))
            for i in range(TT):
                done(v.tensor_tensor(g_t[:, i], g_t[:, i], lx(0), ALU.mult))
            dve.wait_ge(*at("ld_T", 16 * (P // BL)))
            for np_ in range(2):
                s = slice(64 * np_, 64 * np_ + 64)
                size = [64, TT * NH, CH // BL, BL]
                done(v.tensor_tensor(T16[s, :, :, s].rearrange("p i h (b t) -> p (i h) b t", b=CH // BL),
                                     T_flat[s].rearrange("p (x t) -> p x t", x=BL).unsqueeze(2).broadcast_to(size),
                                     own_block[s].unsqueeze(1).unsqueeze(3).broadcast_to(size), ALU.mult), "T16")
            for m in range(4):
                for g in range(4):
                    dve.wait_ge(*at(f"X{m}_ps", g + 1))
                    quarter = lambda x: x[:, g // 2, 4 * (g % 2):4 * (g % 2) + 4, :]
                    src = PS[X_BANKS[m] + g][:, :].rearrange("p (h k) -> p h k", h=4)
                    if m == 0:
                        done(v.tensor_copy(quarter(Xs[0]), src), "X0")
                    else:
                        done(v.tensor_tensor(quarter(Xs[m]), src, quarter(Xs[0]), ALU.add), f"X{m}")
            dve.wait_ge(*at("NS_ps", 1))
            done(v.tensor_copy(NS[:, 0:3:2], PS[4][:, :].rearrange("p (i c k) -> p i c k", i=2, c=CT)), "NS")
            done(v.tensor_copy(NS[:, 1], PS[5][:, 0:256].rearrange("p (c k) -> p c k", c=CT)), "NS")
            dve.wait_ge(*at("M_ps", 1))
            done(v.tensor_tensor(Mt[:, 0], PS[1][:, 0:256].rearrange("p (c k) -> p c k", c=CT), DI[:, 0], ALU.add), "Mt")
            done(v.tensor_tensor(Mt[:, 1], PS[0][:, 0:256].rearrange("p (c k) -> p c k", c=CT), DI[:, 1], ALU.add), "Mt")
            dve.wait_ge(*at("Q_ps", 1))
            r_v = AR[:, 1].rearrange("p c (n s) -> p c n s", s=CH)
            for n in (1, 2, 3):
                src = PS[4 + n % 2][:, (n // 2) * 256:(n // 2) * 256 + 256].rearrange("p (c k) -> p c k", c=CT)
                done(v.tensor_tensor(Q[:, n], src, r_v[:, :, n, :], ALU.add), "Q")
            for n in (1, 2):
                dve.wait_ge(*at("S_ps", n))
                done(v.tensor_copy(St[0:64, n - 1], PS[0][0:64, 0:256].rearrange("p (c k) -> p c k", c=CT)), "St_v")
            for i in range(TT):
                dve.wait_ge(*at("Ys_ps", i + 1))
                dve.wait_ge(*at("Yuv", 4))
                s = slice(64, P) if i == 0 else slice(0, P)
                if i == 0:
                    done(v.tensor_copy(Y[0:64, 0], Yuv[0:64, 0]))
                for hp in range(2):
                    e = lambda t: t[s, i].rearrange("p (c e) k -> p c e k", e=2)[:, :, hp]
                    done(v.tensor_tensor(e(Y), PS[4 - 2 * i + hp][s, 0:256].rearrange("p (c k) -> p c k", c=CT),
                                         e(Yuv), ALU.add), "Y")
            done(v.tensor_reduce(gst[:, 0], Y, AX_X, ALU.add))
            done(v.tensor_scalar(gst[:, 1], gst[:, 0], 1.0 / HEAD, None, ALU.mult))
            done(v.tensor_tensor(Y, Y, bc(gst[:, 1]), ALU.subtract))
            done(v.tensor_tensor(Ysq, Y, Y, ALU.mult))
            done(v.tensor_reduce(gst[:, 2], Ysq, AX_X, ALU.add), "gn_ss")
            dve.wait_ge(*at("gn_rs", 1))
            done(v.tensor_scalar(gst[:, 3], gst[:, 4], ROOT_HEAD, None, ALU.mult))
            done(v.tensor_tensor(Y, Y, bc(gst[:, 3]), ALU.mult))
            done(v.tensor_tensor(Y, Y, g_t, ALU.mult))
            done(v.tensor_tensor(Y, Y, y_add, ALU.add), "y_rwkv")
            dve.wait_ge(*at("yT_ps", 1))
            done(v.tensor_copy(YT[:, 4:6, :], PS[0][:, :].rearrange("p (c t) -> p c t", c=2)), "yT_v")

            def add_to_x(ps_name, made_name):
                for u in range(4):
                    dve.wait_ge(*at(ps_name, u + 1))
                    i, h = u // 2, u % 2
                    xs = X[:, i, h * 512:(h + 1) * 512]
                    done(v.tensor_tensor(xs, PS[4 + u][:, :], xs, ALU.add), made_name)

            def norm_rows(r, made_name, dst):
                for i in range(TT):
                    dve.wait_ge(S(f"rs_x{r}"), i + 1)
                    at_ = 6 + 4 * r + i
                    done(v.tensor_scalar(dst[:, i, :], X[:, i, :], st[:, at_:at_ + 1], ROOT_D, ALU.mult, ALU.mult), made_name)

            def turned(ps_name, gain, made_name):
                for c in TURNED_V:
                    dve.wait_ge(*at(ps_name, c // 2 + 1))
                    done(v.tensor_scalar(MT[:, c, :], PS[c // 2][:, (c % 2) * 256:(c % 2) * 256 + 256],
                                         col(gain, c), None, ALU.mult), made_name)

            add_to_x("pe_wout", "x1")
            norm_rows(1, "x1n", xm)
            turned("t_x1", "norm_xa_g", "x1T_v")
            for c in range(0, KT, 2):
                dve.wait_ge(*at("pe_q", c + 1))
                done(v.tensor_scalar(YT[:, c, :], PS[4 + c % 4][:, 0:T], float(XD) ** -0.5, None, ALU.mult), "q_v")

            def row_max(u):
                dve.wait_ge(*at("sc_ps", u + 1))
                done(v.tensor_reduce(ast[:, 1, u:u + 1], PS[u % 4][:, 0:T], AX_X, ALU.max, negate=True), "nmax")

            def invert_sum(u):
                dve.wait_ge(*at("expd", u + 1))
                done(v.reciprocal(ast[:, 3, u:u + 1], ast[:, 2, u:u + 1]), "inv_sum")

            def turned_prob(h):
                dve.wait_ge(*at("pT_ps", h + 1))
                done(v.tensor_copy(prob_t(h)[:, 0], PS[4 + 2 * (h % 2)][:, 0:T]), "pT_v")

            def head_out(h):
                dve.wait_ge(*at("o_ps", 2 * h + 1))
                done(v.tensor_copy(YT[:, 2 * h, :], PS[2 * (h % 2)][:, 0:T]), "oT_v")

            for u in range(2 * XH + 1):
                if u < 2 * XH:
                    row_max(u)
                if u >= 1:
                    invert_sum(u - 1)
                if u == 6:
                    turned_prob(0)
            turned_prob(1)
            head_out(0)
            turned_prob(2)
            head_out(1)
            turned_prob(3)
            head_out(2)
            head_out(3)
            add_to_x("pe_wo", "x2")
            norm_rows(2, "x2n", x3n)
            turned("t_x2", "norm_ffn_g", "x2T_v")
            each = [P, TT, NE]
            dve.wait_ge(*at("rl_ps", 2))
            done(v.tensor_tensor(rt[:, 0], PS[4][:, 0:TT * NE].rearrange("p (i e) -> p i e", i=TT),
                                 b_rt[:].unsqueeze(1).broadcast_to(each), ALU.add))
            for i in range(TT):
                done(v.max(top[:, i, :], rt[:, 0, i, :]))
            done(v.tensor_scalar(top[:, :, 7:8], top[:, :, 0:1], -1.0, None, ALU.mult), "nl")
            thr = top[:, :, 3:4].broadcast_to(each)
            done(v.tensor_tensor(rt[:, 2], rt[:, 0], thr, ALU.is_gt))
            done(v.tensor_tensor(rt[:, 3], rt[:, 0], thr, ALU.is_equal))
            done(v.tensor_reduce(cnt[:, 0:2], rt[:, 2], AX_X, ALU.add))
            done(v.tensor_scalar(cnt[:, 0:2], cnt[:, 0:2], -1.0, 4.0, ALU.mult, ALU.add))
            for i in range(TT):
                done(v.tensor_tensor_scan(rt[:, 4, i, :], ones[:, 0:NE], rt[:, 3, i, :], 0.0, ALU.mult, ALU.add))
            done(v.tensor_tensor(rt[:, 4], rt[:, 4], cnt[:, 0:2].unsqueeze(2).broadcast_to(each), ALU.is_le))
            done(v.tensor_tensor(rt[:, 3], rt[:, 3], rt[:, 4], ALU.mult))
            done(v.tensor_tensor(rt[:, 5], rt[:, 2], rt[:, 3], ALU.add), "picked")
            dve.wait_ge(*at("r_exp", 2))
            done(v.tensor_tensor(rt[:, 1], rt[:, 1], rt[:, 5], ALU.mult))
            done(v.tensor_reduce(cnt[:, 2:4], rt[:, 1], AX_X, ALU.add))
            done(v.reciprocal(cnt[:, 2:4], cnt[:, 2:4]))
            done(v.tensor_tensor(gate[:], rt[:, 1], cnt[:, 2:4].unsqueeze(2).broadcast_to(each), ALU.mult), "gate")
            dve.wait_ge(*at("rank_ps", 3))
            done(v.scalar_tensor_tensor(out=key[:], in0=PS[6][:, 0:TT * NE].rearrange("p (i e) -> p i e", i=TT), scalar=1.0,
                                        in1=rt[:, 5], op0=ALU.add, op1=ALU.mult))
            done(v.tensor_scalar(key[:], key[:], -1.0, None, ALU.add), "key")

            def select(e):
                for t in range(TT):
                    v.tensor_scalar(self_[:, t, :], slot_no[:, 0, :], key[:, t, bass.ds(e, 1)], None,
                                    ALU.is_equal).then_inc(S("self_sb"), 1)

            select(0)
            done(v.memset(yt_f[:, 512:768], 0.0))
            dve.wait_ge(*at("gt_ps", 4))
            for g in range(2):
                s = slice(64 * g, 64 * g + NE)
                done(v.tensor_copy(yt_f[s, 512:768], PS[4 + g][s, 0:T]))
            dve.sem_inc(S("sel_t"), 1)
            dve.sem_inc(S("y_sb"), 1)
            done(v.tensor_reduce(cnt[:, 4:5], PS[6][:, 2 * NE:3 * NE], AX_X, ALU.max))
            done(v.tensor_scalar(cnt[:, 5:6], cnt[:, 4:5], float(SLOTS), None, ALU.is_gt))
            for r in range(2, ROUNDS):
                done(v.scalar_tensor_tensor(out=cnt[:, 5:6], in0=cnt[:, 4:5], scalar=float(r * SLOTS),
                                            in1=cnt[:, 5:6], op0=ALU.is_gt, op1=ALU.add))
            done(v.tensor_scalar(cnt[:, 5:6], cnt[:, 5:6], float(NE // GROUP), float(NE // GROUP), ALU.mult, ALU.add))
            done(v.tensor_copy(steps_i[:], cnt[:, 5:6]), "steps_v")
            dve.sem_inc(S("steps"), 1)
            for u in range(4):
                done(v.memset(PS[u][:, :], 0.0), "banks_cleared")
            groups = dve.value_load(steps_i[0:1, 0:1], min_val=NE // GROUP, max_val=NE * ROUNDS // GROUP)
            dve.sem_inc(S("act_sb"), 1)
            gcol = par[:, COL["norm_ffn_g"]:COL["norm_ffn_g"] + KT].rearrange("p (h b) -> p h b", h=2) \
                .unsqueeze(3).broadcast_to([P, 2, 4, SLOTS])

            def rows_out(n):
                dve.wait_ge(S("rows_ps"), n + 1)
                v.tensor_copy(picked_rows, PS[7][:, :]).then_inc(S("rows_sb"), 1)

            def spread():
                v.tensor_tensor(xg.rearrange("p (h b) s -> p h b s", h=2),
                                PS[7][:, :].rearrange("p (b h s) -> p h b s", b=4, h=2), gcol, ALU.mult).then_inc(S("xg"), 1)

            dve.wait_ge(*at("ld_fing", 16))
            done(v.tensor_scalar(fin_g, fin_g, ROOT_D, None, ALU.mult))
            dve.wait_ge(S("gathered"), 1)
            spread()
            with dve.Fori(0, groups * GROUP) as i:
                dve.wait_ge(S("turned"), i + 1)
                e = i % NE
                for t in range(TT):
                    v.tensor_scalar(sel[:, t], slot_no[:], key[:, t, bass.ds(e, 1)], gate[:, t, bass.ds(e, 1)],
                                    ALU.is_equal, ALU.mult).then_inc(S("sel_sb"), 1)
                dve.wait_ge(S("sel_sb"), TT * (i + 1))
                for t in range(TT):
                    k_e = key[:, t, bass.ds(e, 1)]
                    v.tensor_scalar(k_e, k_e, float(SLOTS), None, ALU.subtract).then_inc(S("key_moved"), 1)
                dve.wait_ge(S("key_moved"), TT * (i + 1))
                select((i + 1) % NE)
                rows_out(i + 1)
                dve.wait_ge(S("used_ring"), i * PER_EXPERT + GU_CHUNKS)
                v.tensor_scalar(m_g, PS[4][:, :], LIMIT, None, ALU.min).then_inc(S("gate_in"), 1)
                v.tensor_scalar(m_u, PS[5][:, :], LIMIT, -LIMIT, ALU.min, ALU.max).then_inc(S("up_in"), 1)
                dve.wait_ge(S("up_in"), i + 1)
                v.scalar_tensor_tensor(out=m_a, in0=m_u, scalar=1.0, in1=m_g, op0=ALU.add, op1=ALU.mult).then_inc(S("up_gate"), 1)
                dve.wait_ge(S("up_gate"), i + 1)
                dve.wait_ge(S("gate_sig"), i + 1)
                v.tensor_tensor(m_a, m_a, m_s, ALU.mult).then_inc(S("act_sb"), 1)
                dve.wait_ge(S("gathered"), i + 2)
                spread()
                dve.wait_ge(S("act_ps"), i + 1)
                v.tensor_copy(act_t, PS[6][:, :].rearrange("p (f m) -> p f m", f=4)).then_inc(S("act_t"), 1)
            for u in range(4):
                i, h = u // 2, u % 2
                dve.wait_ge(S("scattered"), groups * (GROUP * TT) + i + 1)
                xs = X[:, i, h * 512:(h + 1) * 512]
                done(v.tensor_tensor(xs, PS[u][:, :], xs, ALU.add), "x3")
            for i in range(TT):
                dve.wait_ge(S("rs_x3"), i + 1)
                done(v.scalar_tensor_tensor(out=fin[:, i, :], in0=X[:, i, :], scalar=st[:, 18 + i:19 + i], in1=fin_g,
                                            op0=ALU.mult, op1=ALU.mult), "y_out")

        @block.tensor
        def _(pe):
            mm, tr = nc.tensor.matmul, nc.tensor.transpose

            def turn(src, ready, name):
                for i in range(TT):
                    pe.wait_ge(*at(ready, i + 1))
                    for c in range(KT):
                        x = tr(PS[c // 2][:, (c % 2) * 256 + i * P:(c % 2) * 256 + i * P + P],
                               src[:, i, c * P:(c + 1) * P], ident[:])
                        if i == TT - 1 and c % 2 == 1:
                            x.then_inc(S(name), 1)

            def await_turned(name, c):
                by_v = c in TURNED_V
                n = (TURNED_V if by_v else TURNED_A).index(c) + 1
                pe.wait_ge(*at(name + ("_v" if by_v else "_a"), n))

            pe.wait_ge(*at("ident", 1))
            turn(xn, "xn", "t_x")
            pe.wait_ge(*at("ld_par", 16 * len(PARAM_ROWS)))
            tr(PS[7][:, 0:NPAR], par_rows[0:NPAR, :], ident[0:NPAR, 0:NPAR]).then_inc(S("par_ps"), 1)

            def u_tiles(name, lo, hi, free):
                w, _ = WV[name]
                pe.wait_ge(*at("ld_" + name, 16))
                for c in range(lo, hi):
                    if free:
                        pe.wait_ge(*at(free, c + 1))
                    for k in range(KT):
                        if name == "xl" and c == 0:
                            await_turned("hT", k)
                        x = mm(PS[4 + c][:, 0:T], w[:, k, c * P:(c + 1) * P], HT[:, k, :], start=(k == 0), stop=(k == KT - 1))
                    x.then_inc(S("u_" + name), 1)

            pe.wait_ge(*at("par", 1))
            u_tiles("xl", 0, CT, None)
            u_tiles("gl", 0, CT, "xl")
            u_tiles("r", 0, CT, "gelu")
            turn(mem, "memn", "t_mem")
            u_tiles("k", 0, CT, "sv_r")
            pe.wait_ge(*at("ld_lruw", 64))
            pe.wait_ge(*at("mT_a", 4))
            pe.wait_ge(*at("mT_v", 4))
            for c in range(CT):
                pe.wait_ge(*at("conv", 4 * c + 4))
                mm(PS[c][:, 0:T], wx_bd[:, c, :], xc[:, c, :], start=True, stop=True)
                mm(PS[c][:, T:2 * T], wa_bd[:, c, :], xc[:, c, :], start=True, stop=True).then_inc(S("lru_gates"), 1)
            u_tiles("lora", 0, 2, "sv_k")
            pe.wait_ge(*at("sv_k", 4))
            pe.wait_ge(*at("sv_lora", 2))
            u_tiles("v", 0, CT, None)
            pe.wait_ge(*at("ld_lora_up", 48))
            pe.wait_ge(*at("lora_f", 2))
            pe.wait_ge(*at("ga", CT))
            for c in range(CT):
                for h in range(2):
                    x = mm(PS[2 * h + c // 2][:, (c % 2) * T:(c % 2) * T + T], wa_up[64 * h:64 * h + 64, c * P:(c + 1) * P],
                           lora[64 * h:64 * h + 64, 0, :], start=True, stop=True)
            x.then_inc(S("z_a"), 1)
            pe.wait_ge(*at("sv_v", CT))
            for i in range(TT):
                mm(PS[4 + i][:, :], lora[:, 1, i * P:(i + 1) * P], g_up[:], start=True, stop=True).then_inc(S("g_ps"), 1)

            def k_tile(c):
                if c == 0:
                    pe.wait_ge(*at("ld_wk", 16))
                    pe.wait_ge(*at("sv_v", CT))
                if c >= 2:
                    pe.wait_ge(*at("K", c - 1))
                for k in range(KT):
                    x = mm(PS[6 + c % 2][:, 0:T], WB[:, k, c * P:(c + 1) * P], MT[:, k, :], start=(k == 0), stop=(k == KT - 1))
                x.then_inc(S("pe_k"), 1)

            def v_part(q):
                m, h = q // 2, q % 2
                if q == 0:
                    pe.wait_ge(*at("ld_wv", 16))
                    pe.wait_ge(*at("K", KT))
                if q >= 2:
                    pe.wait_ge(*at("V", q - 1))
                for k in range(KT):
                    x = mm(PS[6 + q % 2][:, :], MT[:, k, m * P:(m + 1) * P], WB[:, k, h * 512:(h + 1) * 512],
                           start=(k == 0), stop=(k == KT - 1))
                x.then_inc(S("pe_v"), 1)

            k_tile(0)
            k_tile(1)
            pe.wait_ge(*at("kk_sq", 1))
            pe.wait_ge(*at("sig", CT))
            pe.wait_ge(*at("consts_all", 1))
            for c in range(2):
                mm(PS[c][:, :], head_ones[:], U(1)[:, c * 512:(c + 1) * 512], start=True, stop=True).then_inc(S("kk_ss"), 1)
            for c in range(2, 6):
                k_tile(c)

            def to_tokens(src, banks, name):
                for i in range(TT):
                    for c in range(CT):
                        x = tr(PS[banks + i][:, c * P:(c + 1) * P], src[:, c, i * P:(i + 1) * P], ident[:])
                    x.then_inc(S(name), 1)

            pe.wait_ge(*at("a_c", CT))
            pe.wait_ge(*at("al_c", 1))
            pe.wait_ge(*at("bt_c", 1))
            pe.wait_ge(*at("g_t", 2))
            for i in range(TT):
                for np_ in range(2):
                    t0 = (2 * i + np_) * CH
                    for c in range(CT):
                        for hp in range(2):
                            h = slice(64 * hp, 64 * hp + 64)
                            x = mm(PS[2 + 2 * i + hp][64 * np_:64 * np_ + 64, c * 64:(c + 1) * 64],
                                   AR[h, 0, c, t0:t0 + CH], bt_c[h, c, t0:t0 + CH], start=True, stop=True)
                            if np_ == 1 and c == CT - 1:
                                x.then_inc(S("n_ps"), 1)
            k_tile(6)
            pe.wait_ge(*at("kk_rn", 2))
            to_tokens(v_c, 0, "tok_v_ps")
            k_tile(7)
            pe.wait_ge(*at("tok", 2))
            to_tokens(AR[:, 0], 0, "tok_al_ps")
            pe.wait_ge(*at("bh_c", 1))
            pe.wait_ge(*at("O", 4))
            to_tokens(bh_c, 2, "tok_bh_ps")
            pe.wait_ge(*at("kh_c", 1))
            pe.wait_ge(*at("O", 8))
            to_tokens(kh_c, 4, "tok_kh_ps")
            for q in range(4):
                kind, i = q // 2, q % 2
                src = (bt_c, kt_c)[kind]
                if q == 0:
                    pe.wait_ge(*at("r_til", 1))
                    pe.wait_ge(*at("tok", 4))
                if q in (1, 2):
                    pe.wait_ge(*at("tok_v", 2 * q))
                if q == 3:
                    pe.wait_ge(*at("st", 2))
                for np_ in range(2):
                    t0 = (2 * i + np_) * CH
                    for c in range(CT):
                        for hp in range(2):
                            h = slice(64 * hp, 64 * hp + 64)
                            x = mm(PS[ST_BANKS[q] + hp][64 * np_:64 * np_ + 64, c * 128:(c + 1) * 128].rearrange("p (w k) -> p w k", w=2),
                                   src[h, c, t0:t0 + CH], AR[h, :, c, t0:t0 + CH], start=True, stop=True)
                            if np_ == 1 and c == CT - 1:
                                x.then_inc(S("st_ps"), 1)
            pe.wait_ge(*at("rkk", CT))
            pe.wait_ge(*at("st", 4))
            for i in range(TT):
                for c in range(CT):
                    x = mm(PS[2][:, i * NH + 2 * c:i * NH + 2 * c + 2], rkk[:, c, i * P:(i + 1) * P],
                           head_ones[:, 0:P:64], start=True, stop=True)
            x.then_inc(S("bonus_ps"), 1)

            def product(bank, name, *terms):
                for flip in range(2):
                    for h in range(NH):
                        for np_ in range(2):
                            j = np_ ^ flip
                            rows = slice(64 * np_, 64 * np_ + 64)
                            for n, (l, r) in enumerate(terms):
                                x = mm(PS[bank + j][rows, h * 64:(h + 1) * 64], l(rows, np_, j)[:, h], r(rows, np_, j)[:, h],
                                       start=(n == 0), stop=(n == len(terms) - 1))
                x.then_inc(S(name), 1)


            by_i = lambda t: (lambda rows, np_, j: t[rows, j ^ np_])
            part = lambda t, w: (lambda rows, np_, j: t[rows, j ^ np_, :, w])

            pe.wait_ge(*at("st", 8))
            product(4, "G_ps", (part(STk, 0), by_i(v_t)))
            v_part(0)
            v_part(1)

            def pair_product(l, r, bank, name, before=None):
                for g in range(4):
                    if before:
                        before(g)
                    for h in range(4):
                        i, hh = g // 2, 4 * (g % 2) + h
                        x = mm(PS[bank + g][:, h * P:(h + 1) * P], l[:, i, hh, :], r[:, i, hh, :], start=True, stop=True)
                    x.then_inc(S(name), 1)

            pe.wait_ge(*at("T16", 2))
            pe.wait_ge(*at("bonus", 1))
            pair_product(O_bd, T16, 0, "Et_ps")
            pe.wait_ge(*at("G", 4))
            pe.wait_ge(*at("V", 2))
            pair_product(T16, RG, X_BANKS[0], "X0_ps")

            def step_in(m):
                def before(g):
                    if m == 1:
                        pe.wait_ge(*at("Et", g + 1))
                    pe.wait_ge(*at(f"X{m - 1}", g + 1))
                return before

            for m in range(1, 4):
                pair_product(Et, Xs[m - 1], X_BANKS[m], f"X{m}_ps", step_in(m))
            pe.wait_ge(*at("X3", 4))

            def by_chunk(chunks, bank, name, width, *terms):
                for c in range(CT):
                    for hp in range(2):
                        for k in range(2):
                            for n in chunks:
                                if n // 2 != k:
                                    continue
                                np_, i = n % 2, n // 2
                                j = i ^ np_
                                rows = slice(64 * np_, 64 * np_ + 64)
                                o = PS[bank + np_][64 * hp:64 * hp + 64, (i * width + c) * 64:(i * width + c + 1) * 64]
                                for m, (l, r) in enumerate(terms):
                                    x = mm(o, l(rows, np_, j)[:, 2 * c + hp], r(rows, np_, j)[:, 2 * c + hp],
                                           start=(m == 0), stop=(m == len(terms) - 1))
                x.then_inc(S(name), 1)

            by_chunk((0, 1, 2), 4, "NS_ps", CT, (by_i(bh_t), by_i(XU)), (by_i(kh_t), by_i(v_t)))
            by_chunk((1, 2), 0, "M_ps", 0, (by_i(XW), by_i(bh_t)))
            product(2, "Yuv_ps", (part(STb, 1), by_i(XU)), (part(STk, 1), by_i(v_t)))
            pe.wait_ge(*at("NS", 2))
            by_chunk((1, 2, 3), 4, "Q_ps", CT, (by_i(XW), part(STb, 1)))
            pe.wait_ge(*at("Mt", 2))
            for n in (1, 2):
                if n == 2:
                    pe.wait_ge(*at("St_a", 1))
                    pe.wait_ge(*at("St_v", 1))
                prev = NS[:, 0] if n == 1 else St[:, 0]
                for c in range(CT):
                    for hp in range(2):
                        h = slice(64 * hp, 64 * hp + 64)
                        o = PS[hp][h, c * 64:(c + 1) * 64]
                        mm(o, ident[h, h], NS[h, n, c, :], start=True, stop=False)
                        x = mm(o, Mt[h, n - 1, c, :], prev[h, c, :], start=False, stop=True)
                x.then_inc(S("S_ps"), 1)
            pe.wait_ge(*at("Q", 3))
            pe.wait_ge(*at("St_a", 2))
            pe.wait_ge(*at("St_v", 2))
            for i in range(TT):
                if i == 1:
                    pe.wait_ge(*at("Yuv", 4))
                for c in range(CT):
                    for np_ in range(2):
                        n = 2 * i + np_
                        if n == 0:
                            continue
                        state = NS[:, 0] if n == 1 else St[:, n - 2]
                        for hp in range(2):
                            h = slice(64 * hp, 64 * hp + 64)
                            x = mm(PS[4 - 2 * i + hp][64 * np_:64 * np_ + 64, c * 64:(c + 1) * 64],
                                   Q[h, n, c, :], state[h, c, :], start=True, stop=True)
                x.then_inc(S("Ys_ps"), 1)
            v_part(2)
            v_part(3)
            pe.wait_ge(*at("y_rwkv", 1))
            y_tok = R[:, 0, :].rearrange("p (i d) -> p i d", i=TT)
            for q in range(2):
                for c in (2 * q, 2 * q + 1):
                    for i in range(TT):
                        x = tr(PS[q][:, (c % 2) * 256 + i * P:(c % 2) * 256 + i * P + P], y_tok[:, i, c * P:(c + 1) * P], ident[:])
                x.then_inc(S("yT_ps"), 1)

            def project(src, w, name):
                for u in range(4):
                    i, h = u // 2, u % 2
                    for k in range(KT):
                        x = mm(PS[4 + u][:, :], src[:, k, i * P:(i + 1) * P], w[:, k, h * 512:(h + 1) * 512],
                               start=(k == 0), stop=(k == KT - 1))
                    x.then_inc(S(name), 1)

            pe.wait_ge(*at("ld_wo1", 16))
            pe.wait_ge(*at("y_lru", 1))
            pe.wait_ge(*at("yT_a", 1))
            pe.wait_ge(*at("yT_v", 1))
            pe.wait_ge(*at("V", 4))
            project(YT, W2, "pe_wout")
            turn(xm, "x1n", "t_x1")
            pe.wait_ge(*at("ld_wq", 16))
            for c in range(KT):
                if c >= 4:
                    pe.wait_ge(*at("q_a" if c % 2 else "q_v", (c - 4) // 2 + 1))
                for k in range(KT):
                    if c == 0:
                        await_turned("x1T", k)
                    x = mm(PS[4 + c % 4][:, 0:T], W1[:, k, c * P:(c + 1) * P], MT[:, k, :], start=(k == 0), stop=(k == KT - 1))
                x.then_inc(S("pe_q"), 1)
            pe.wait_ge(*at("q_a", 4))
            pe.wait_ge(*at("q_v", 4))
            def scores(lo, hi):
                for u in range(lo, hi):
                    h, i = u // 2, u % 2
                    if u >= 4:
                        pe.wait_ge(*at("expd", u - 3))
                    for k in range(2):
                        x = mm(PS[u % 4][:, 0:T], YT[:, 2 * h + k, i * P:(i + 1) * P], HT[:, 2 * h + k, :], start=(k == 0), stop=(k == 1))
                    x.then_inc(S("sc_ps"), 1)

            def turn_prob(h):
                pe.wait_ge(*at("prob", 2 * h + 2))
                if h >= 2:
                    pe.wait_ge(*at("pT_a", h - 1))
                    pe.wait_ge(*at("pT_v", h - 1))
                for m in range(2):
                    for i in range(TT):
                        x = tr(PS[4 + 2 * (h % 2) + m][:, i * P:(i + 1) * P], prob(2 * h + i)[:, m * P:(m + 1) * P], ident[:])
                x.then_inc(S("pT_ps"), 1)

            def head_out(h):
                pe.wait_ge(*at("pT_a", h + 1))
                pe.wait_ge(*at("pT_v", h + 1))
                if h == 0:
                    pe.wait_ge(*at("expd", 2 * XH))
                if h >= 2:
                    pe.wait_ge(*at("oT_a", h - 1))
                    pe.wait_ge(*at("oT_v", h - 1))
                for d in range(2):
                    for m in range(2):
                        x = mm(PS[2 * (h % 2) + d][:, 0:T], V[:, m, (2 * h + d) * P:(2 * h + d + 1) * P], prob_t(h)[:, m],
                               start=(m == 0), stop=(m == 1))
                    x.then_inc(S("o_ps"), 1)

            scores(0, 6)
            turn_prob(0)
            scores(6, 8)
            turn_prob(1)
            head_out(0)
            turn_prob(2)
            head_out(1)
            turn_prob(3)
            head_out(2)
            head_out(3)
            pe.wait_ge(*at("oT_a", 4))
            pe.wait_ge(*at("oT_v", 4))
            pe.wait_ge(*at("ld_wo2", 16))
            project(YT, WB, "pe_wo")
            turn(x3n, "x2n", "t_x2")
            pe.wait_ge(*at("ld_late", 64))
            for i in range(TT):
                for k in range(KT):
                    if i == 0:
                        await_turned("x2T", k)
                    x = mm(PS[4][:, i * NE:(i + 1) * NE], MT[:, k, i * P:(i + 1) * P], w_rt[:, k, :], start=(k == 0), stop=(k == KT - 1))
                x.then_inc(S("rl_ps"), 1)
            pe.wait_ge(*at("picked", 1))
            m0, m1 = rt[:, 5, 0, :], rt[:, 5, 1, :]
            mm(PS[6][:, 0:NE], before[:], m0, start=True, stop=True).then_inc(S("rank_ps"), 1)
            mm(PS[6][:, NE:2 * NE], ones[:], m0, start=True, stop=False)
            mm(PS[6][:, NE:2 * NE], before[:], m1, start=False, stop=True).then_inc(S("rank_ps"), 1)
            mm(PS[6][:, 2 * NE:3 * NE], ones[:], m0, start=True, stop=False)
            mm(PS[6][:, 2 * NE:3 * NE], ones[:], m1, start=False, stop=True).then_inc(S("rank_ps"), 1)
            pe.wait_ge(*at("gate", 1))
            for g in range(2):
                for i in range(TT):
                    mm(PS[4 + g][64 * g:64 * g + NE, i * P:(i + 1) * P], gate[:, i, :], ident[:],
                       start=True, stop=True).then_inc(S("gt_ps"), 1)
            pe.sem_inc(S("turned"), 1)

            def pick(n):
                pe.wait_ge(S("self_sb"), TT * (n + 1))
                for t in range(TT):
                    for h in range(2):
                        x = mm(PS[7][64 * h:64 * h + 64, :], self_[:, t, :], x3n[:, t, h * 512:(h + 1) * 512],
                               start=(t == 0), stop=(t == TT - 1))
                x.then_inc(S("rows_ps"), 1)

            def gather(n):
                pe.wait_ge(S("rows_sb"), n + 1)
                for b in range(4):
                    x = tr(PS[7][:, b * P:(b + 1) * P], picked_rows[:, b * P:(b + 1) * P], ident[:])
                x.then_inc(S("gathered"), 1)

            def scatter(n):
                pe.wait_ge(S("y_sb"), n + 1)
                pe.wait_ge(S("sel_t"), n + 1)
                for t in range(TT):
                    for g in range(2):
                        h = slice(64 * g, 64 * g + 64)
                        x = mm(PS[2 * t + g][:, :], sel_t[h, t, :], y_e[h, :], start=False, stop=True,
                               skip_group_check=True)
                    x.then_inc(S("scattered"), 1)

            pick(0)
            gather(0)
            pe.wait_ge(*at("banks_cleared", 4))
            pe.wait_ge(*at("ld_bdn", 32))
            pe.wait_ge(*at("steps", 1))
            groups = pe.value_load(steps_i[0:1, 0:1], min_val=NE // GROUP, max_val=NE * ROUNDS // GROUP)

            def expert_pass(group, u):
                i = group * GROUP + u

                def chunk(q):
                    m = PER_EXPERT * u + q
                    pe.wait_ge(S(f"ld_ring{m % RING}"), (group * TURNS + m // RING + 1) * 16)
                    return ring[m % RING]

                pe.wait_ge(S(f"ld_bgu{u % 2}"), (group * (GROUP // 2) + u // 2 + 1) * 16)
                pe.wait_ge(S("act_sb"), i + 1)
                for w in range(2):
                    x = mm(PS[4 + w][:, :], half_rows[:, :], bgu[:, u % 2, w, :], start=True, stop=False)
                x.then_inc(S("used_b"), 1)
                pe.wait_ge(S("xg"), i + 1)
                for k in range(KT):
                    gu = as_gu(chunk(k))
                    for w in range(2):
                        for g in range(2):
                            x = mm(PS[4 + w][64 * g:64 * g + 64, :], xg[:, k, :], gu[:, w, g, :],
                                   start=False, stop=(k == KT - 1))
                    x.then_inc(S("used_ring"), 1)
                    if k == 3:
                        pick(i + 1)
                scatter(i)
                pe.wait_ge(S("sel_sb"), TT * (i + 1))
                for t in range(TT):
                    x = tr(PS[6][:, t * P:(t + 1) * P], sel[:, t].rearrange("p w s -> p (w s)"), ident[:])
                x.then_inc(S("turned"), 1)
                gather(i + 1)
                pe.wait_ge(S("act_sb"), i + 2)
                pe.wait_ge(S("sel_t"), i + 2)
                for f in range(4):
                    x = tr(PS[6][:, f * P:(f + 1) * P], m_a[:, f * P:(f + 1) * P], ident[:])
                x.then_inc(S("act_ps"), 1)
                pe.wait_ge(S("act_t"), i + 1)
                for q in range(DN_CHUNKS):
                    dn = as_dn(chunk(GU_CHUNKS + q))
                    for c in range(2):
                        k = 2 * q + c
                        for g in range(2):
                            x = mm(PS[6][64 * g:64 * g + 64, :], act_t[:, k % 4, 64 * (k // 4):64 * (k // 4) + 64],
                                   dn[:, c, g, :], start=(k == 0), stop=(k == KT - 1))
                    x.then_inc(S("used_ring"), 1)

            with pe.Fori(0, groups) as group:
                for u in range(GROUP):
                    expert_pass(group, u)
            scatter(groups * GROUP)


_NAMES = ['x', 'mem', 'norm_mix_g', 'w_in', 'conv_w', 'conv_b', 'lru_wx', 'lru_bx', 'lru_wa', 'lru_ba',
          'lru_lambda', 'rwkv_mu', 'rwkv_w0', 'rwkv_w_up', 'rwkv_a0', 'rwkv_a_up', 'rwkv_g_up', 'rwkv_k_k',
          'rwkv_k_a', 'rwkv_r_k', 'rwkv_lnx_g', 'rwkv_lnx_b', 'w_out', 'norm_xa_g', 'norm_mem_g', 'xa_wq',
          'xa_wk', 'xa_wv', 'xa_wo', 'norm_ffn_g', 'w_router', 'b_router', 'w_gu', 'b_gu', 'w_dn', 'b_dn',
          'final_norm_g']


def kernel(**inputs):
    import numpy as _np
    import concourse.bacc as _bacc
    from concourse import mybir as _mybir
    from concourse.bass_utils import run_bass_kernel_spmd as _run

    nc = _bacc.Bacc("TRN2", target_bir_lowering=False, num_devices=1)
    arrays, aps = {}, {}
    for name in _NAMES:
        arr = _np.ascontiguousarray(inputs[name])
        arrays[f"in_{name}"] = arr
        aps[name] = nc.dram_tensor(f"in_{name}", arr.shape, _mybir.dt.from_np(arr.dtype), kind="ExternalInput").ap()
    out = nc.dram_tensor("out", (1, T, D), _mybir.dt.float32, kind="ExternalOutput").ap()
    build(nc, aps, out)
    r = _run(nc, [arrays], core_ids=[0])
    return r.results[0]["out"]
```
